# Optimizing a Trainium2 kernel written in Bass

```python
import math
import jax
import jax.numpy as jnp
from jax import lax
import numpy as np
import jax, jax.numpy as jnp

D_MODEL = 1024
BATCH = 1
SEQ = 1024
DEPTH = 1

CHUNK = 64
Q_BLOCK = 128
GMLP_BLOCK = 128

A_GROUPS = 4
A_GDIM = 64
A_WIDTH = A_GROUPS * A_GDIM
B_HEADS = 4
B_QK_DIM = 64
B_V_DIM = 2 * B_QK_DIM
B_WIDTH = B_HEADS * B_V_DIM
C_HEADS = 4
C_HEAD_DIM = 64
C_WIDTH = C_HEADS * C_HEAD_DIM
IDX_HEADS = 8
IDX_DIM = 32
TOPK_MAX = 256
MIX_WIDTH = A_WIDTH + B_WIDTH + C_WIDTH

FFN_HIDDEN = -(-8 * D_MODEL // (3 * 256)) * 256

OFF_A_U = 0
OFF_A_V = OFF_A_U + A_WIDTH
OFF_B_Q = OFF_A_V + A_WIDTH
OFF_B_K = OFF_B_Q + B_HEADS * 2 * B_QK_DIM
OFF_B_V = OFF_B_K + B_HEADS * 2 * B_QK_DIM
OFF_C_Q = OFF_B_V + B_WIDTH
OFF_C_K = OFF_C_Q + C_WIDTH
OFF_C_V = OFF_C_K + C_WIDTH
OFF_I_Q = OFF_C_V + C_WIDTH
OFF_I_K = OFF_I_Q + IDX_HEADS * IDX_DIM
OFF_I_W = OFF_I_K + IDX_DIM
IN_WIDTH = OFF_I_W + IDX_HEADS

DEEPNORM_ALPHA = (2 * DEPTH) ** 0.25
DEEPNORM_BETA = (8 * DEPTH) ** -0.25
LN_EPS = 1e-5


def layer_norm(x, g, b):
    xf = x.astype(jnp.float32)
    mu = jnp.mean(xf, axis=-1, keepdims=True)
    xc = xf - mu
    var = jnp.mean(xc * xc, axis=-1, keepdims=True)
    return (xc * lax.rsqrt(var + LN_EPS) * g.astype(jnp.float32) + b.astype(jnp.float32)).astype(x.dtype)

def rms_norm(x, g):
    xf = x.astype(jnp.float32)
    ms = jnp.mean(xf * xf, axis=-1, keepdims=True)
    return (xf * lax.rsqrt(ms + LN_EPS) * g.astype(jnp.float32)).astype(x.dtype)

def alibi_slopes(n):
    return jnp.asarray([2.0 ** (-8.0 * (h + 1) / n) for h in range(n)], dtype=jnp.float32)

def to_blocks(a, size):
    bn, s = a.shape[:2]
    return jnp.moveaxis(a.reshape((bn, s // size, size) + a.shape[2:]), 1, 0)

def from_blocks(a):
    n, bn, t = a.shape[:3]
    return jnp.moveaxis(a, 0, 1).reshape((bn, n * t) + a.shape[3:])

def gmlp_mixer(u, v, w_s, b_s, ln_g, ln_b):
    bn, s, _ = u.shape
    nblk = s // GMLP_BLOCK
    u = jax.nn.gelu(u)
    v = jax.nn.gelu(v).reshape(bn, nblk, GMLP_BLOCK, A_GROUPS, A_GDIM)
    v = layer_norm(v, ln_g, ln_b)
    pos_chunk = jnp.arange(GMLP_BLOCK) // CHUNK
    mask = pos_chunk[None, :] <= pos_chunk[:, None]
    w = jnp.where(mask[None], w_s, jnp.zeros_like(w_s))
    sg = jnp.einsum('gts,bnsgc->bntgc', w, v) + b_s.T[None, None, :, :, None]
    return u * sg.reshape(bn, s, A_WIDTH)

def diff_attention(q, k, v, lam, lam_init, subln_g):
    bn, s = q.shape[:2]
    nblk = s // Q_BLOCK
    scale = B_QK_DIM ** -0.5
    slopes = alibi_slopes(B_HEADS)
    kpos = jnp.arange(s)
    kchunk = kpos // CHUNK

    def block(args):
        qblk, i = args
        qpos = i * Q_BLOCK + jnp.arange(Q_BLOCK)
        allowed = kchunk[None, :] <= (qpos // CHUNK)[:, None]
        dist = jnp.abs(qpos[:, None] - kpos[None, :]).astype(jnp.float32)
        bias = -slopes[:, None, None] * dist[None]
        logits = jnp.einsum('bthmd,bshmd->bhmts', qblk, k).astype(jnp.float32) * scale
        logits = logits + bias[None, :, None]
        logits = jnp.where(allowed[None, None, None], logits, -jnp.inf)
        p = jax.nn.softmax(logits, axis=-1)
        attn = p[:, :, 0] - lam * p[:, :, 1]
        return jnp.einsum('bhts,bshe->bthe', attn.astype(v.dtype), v)

    o = from_blocks(lax.map(block, (to_blocks(q, Q_BLOCK), jnp.arange(nblk))))
    o = rms_norm(o, subln_g) * (1.0 - lam_init)
    return o.reshape(bn, s, B_WIDTH)

def dsa_attention(q, k, v, qi, ki, wi):
    bn, s = q.shape[:2]
    nblk = s // Q_BLOCK
    topk = min(TOPK_MAX, s // 4)
    scale = C_HEAD_DIM ** -0.5
    idx_scale = (IDX_HEADS ** -0.5) * (IDX_DIM ** -0.5)
    slopes = alibi_slopes(C_HEADS)
    kchunk = jnp.arange(s) // CHUNK

    def block(args):
        qblk, qiblk, wiblk, i = args
        qpos = i * Q_BLOCK + jnp.arange(Q_BLOCK)
        qchunk = qpos // CHUNK
        allowed = kchunk[None, :] <= qchunk[:, None]
        idx_logits = jnp.einsum('bthd,bsd->bths', qiblk, ki).astype(jnp.float32)
        score = jnp.einsum('bth,bths->bts', wiblk.astype(jnp.float32) * idx_scale, jax.nn.relu(idx_logits))
        score = jnp.where(allowed[None], score, -jnp.inf)
        _, sel = lax.top_k(score, topk)
        sel_ok = (sel // CHUNK) <= qchunk[None, :, None]
        k_sel = jax.vmap(lambda kb, ib: kb[ib])(k, sel)
        v_sel = jax.vmap(lambda vb, ib: vb[ib])(v, sel)
        logits = jnp.einsum('bthd,btkhd->bhtk', qblk, k_sel).astype(jnp.float32) * scale
        dist = jnp.abs(qpos[None, :, None] - sel).astype(jnp.float32)
        logits = logits - slopes[None, :, None, None] * dist[:, None]
        logits = jnp.where(sel_ok[:, None], logits, -jnp.inf)
        p = jax.nn.softmax(logits, axis=-1)
        return jnp.einsum('bhtk,btkhd->bthd', p.astype(v_sel.dtype), v_sel)

    xs = (to_blocks(q, Q_BLOCK), to_blocks(qi, Q_BLOCK), to_blocks(wi, Q_BLOCK), jnp.arange(nblk))
    o = from_blocks(lax.map(block, xs))
    return o.reshape(bn, s, C_WIDTH)

def hybrid_layer(x, layer_idx, w_in, w_s, b_s, a_ln_g, a_ln_b, lam_q1, lam_k1, lam_q2, lam_k2,
                 subln_g, w_out, ln1_g, ln1_b, w_gu, w_down, ln2_g, ln2_b):
    bn, s, _ = x.shape
    h = jnp.einsum('bsd,de->bse', x, w_in)
    a_u = h[..., OFF_A_U:OFF_A_V]
    a_v = h[..., OFF_A_V:OFF_B_Q]
    b_q = h[..., OFF_B_Q:OFF_B_K].reshape(bn, s, B_HEADS, 2, B_QK_DIM)
    b_k = h[..., OFF_B_K:OFF_B_V].reshape(bn, s, B_HEADS, 2, B_QK_DIM)
    b_v = h[..., OFF_B_V:OFF_C_Q].reshape(bn, s, B_HEADS, B_V_DIM)
    c_q = h[..., OFF_C_Q:OFF_C_K].reshape(bn, s, C_HEADS, C_HEAD_DIM)
    c_k = h[..., OFF_C_K:OFF_C_V].reshape(bn, s, C_HEADS, C_HEAD_DIM)
    c_v = h[..., OFF_C_V:OFF_I_Q].reshape(bn, s, C_HEADS, C_HEAD_DIM)
    i_q = h[..., OFF_I_Q:OFF_I_K].reshape(bn, s, IDX_HEADS, IDX_DIM)
    i_k = h[..., OFF_I_K:OFF_I_W]
    i_w = h[..., OFF_I_W:IN_WIDTH]

    out_a = gmlp_mixer(a_u, a_v, w_s, b_s, a_ln_g, a_ln_b)

    lam_init = 0.8 - 0.6 * math.exp(-0.3 * layer_idx)
    lam = (jnp.exp(jnp.sum(lam_q1.astype(jnp.float32) * lam_k1.astype(jnp.float32)))
           - jnp.exp(jnp.sum(lam_q2.astype(jnp.float32) * lam_k2.astype(jnp.float32))) + lam_init)
    out_b = diff_attention(b_q, b_k, b_v, lam, lam_init, subln_g)

    out_c = dsa_attention(c_q, c_k, c_v, i_q, i_k, i_w)

    mix = jnp.concatenate([out_a, out_b, out_c], axis=-1)
    x = layer_norm(DEEPNORM_ALPHA * x + jnp.einsum('bse,ed->bsd', mix, w_out), ln1_g, ln1_b)

    gu = jnp.einsum('bsd,df->bsf', x, w_gu)
    gate, up = gu[..., :FFN_HIDDEN], gu[..., FFN_HIDDEN:]
    ffn = jnp.einsum('bsf,fd->bsd', jax.nn.silu(gate) * up, w_down)
    return layer_norm(DEEPNORM_ALPHA * x + ffn, ln2_g, ln2_b)

def first_inputs(seed: int = 0) -> dict:
    key = jax.random.key(seed)
    ks = jax.random.split(key, 20)
    f32 = jnp.float32
    nrm = lambda k, shape: jax.random.normal(k, shape, dtype=f32)
    return {
        'x': nrm(ks[0], (BATCH, SEQ, D_MODEL)),
        'w_in': nrm(ks[1], (DEPTH, D_MODEL, IN_WIDTH)) * D_MODEL ** -0.5,
        'gmlp_w_s': nrm(ks[2], (DEPTH, A_GROUPS, GMLP_BLOCK, GMLP_BLOCK)) * GMLP_BLOCK ** -0.5,
        'gmlp_b_s': 1.0 + 0.1 * nrm(ks[3], (DEPTH, A_GROUPS, GMLP_BLOCK)),
        'gmlp_ln_g': 1.0 + 0.05 * nrm(ks[4], (DEPTH, A_GROUPS, A_GDIM)),
        'gmlp_ln_b': 0.02 * nrm(ks[5], (DEPTH, A_GROUPS, A_GDIM)),
        'lam_q1': 0.1 * nrm(ks[6], (DEPTH, B_QK_DIM)),
        'lam_k1': 0.1 * nrm(ks[7], (DEPTH, B_QK_DIM)),
        'lam_q2': 0.1 * nrm(ks[8], (DEPTH, B_QK_DIM)),
        'lam_k2': 0.1 * nrm(ks[9], (DEPTH, B_QK_DIM)),
        'diff_subln_g': 1.0 + 0.05 * nrm(ks[10], (DEPTH, B_V_DIM)),
        'w_out': nrm(ks[11], (DEPTH, MIX_WIDTH, D_MODEL)) * MIX_WIDTH ** -0.5 * DEEPNORM_BETA,
        'ln1_g': 1.0 + 0.05 * nrm(ks[12], (DEPTH, D_MODEL)),
        'ln1_b': 0.02 * nrm(ks[13], (DEPTH, D_MODEL)),
        'w_gu': nrm(ks[14], (DEPTH, D_MODEL, 2 * FFN_HIDDEN)) * D_MODEL ** -0.5,
        'w_down': nrm(ks[15], (DEPTH, FFN_HIDDEN, D_MODEL)) * FFN_HIDDEN ** -0.5 * DEEPNORM_BETA,
        'ln2_g': 1.0 + 0.05 * nrm(ks[16], (DEPTH, D_MODEL)),
        'ln2_b': 0.02 * nrm(ks[17], (DEPTH, D_MODEL)),
    }

def first_block(x, w_in, gmlp_w_s, gmlp_b_s, gmlp_ln_g, gmlp_ln_b, lam_q1, lam_k1, lam_q2, lam_k2,
              diff_subln_g, w_out, ln1_g, ln1_b, w_gu, w_down, ln2_g, ln2_b):
    for l in range(DEPTH):
        x = hybrid_layer(x, l, w_in[l], gmlp_w_s[l], gmlp_b_s[l], gmlp_ln_g[l], gmlp_ln_b[l],
                         lam_q1[l], lam_k1[l], lam_q2[l], lam_k2[l], diff_subln_g[l], w_out[l],
                         ln1_g[l], ln1_b[l], w_gu[l], w_down[l], ln2_g[l], ln2_b[l])
    return x


MIX_WIDTH_2 = D_MODEL
SB_WIDTH = D_MODEL // 2
SB_HEADS = 8
SB_HEAD_DIM = SB_WIDTH // SB_HEADS
POOL_WIDTH = MIX_WIDTH_2 - SB_WIDTH
POOL_WINDOWS = (2, 4, 8, 16)
POOL_GROUPS = len(POOL_WINDOWS)
POOL_GROUP_DIM = POOL_WIDTH // POOL_GROUPS
IN_WIDTH_2 = 3 * SB_WIDTH + POOL_WIDTH
D_FF = -(-8 * D_MODEL // (3 * 256)) * 256
N_MOD = 6
EPS = 1e-6


def rmsnorm(x, g):
    xf = x.astype(jnp.float32)
    y = xf * lax.rsqrt(jnp.mean(xf * xf, axis=-1, keepdims=True) + EPS)
    return (y * g.astype(jnp.float32)).astype(x.dtype)

def stick_breaking_attention(q, k, v):
    S = q.shape[2]
    inv_sqrt = 1.0 / math.sqrt(q.shape[-1])
    outs = []
    for i in range(S // Q_BLOCK):
        L = (i + 1) * Q_BLOCK
        qb = q[:, :, i * Q_BLOCK:L].astype(jnp.float32)
        kb = k[:, :, :L].astype(jnp.float32)
        vb = v[:, :, :L].astype(jnp.float32)
        z = jnp.einsum('bhqd,bhkd->bhqk', qb, kb) * inv_sqrt
        t_idx = i * Q_BLOCK + jnp.arange(Q_BLOCK)[:, None]
        s_idx = jnp.arange(L)[None, :]
        mask = s_idx < t_idx
        log1m = jnp.where(mask, -jax.nn.softplus(z), 0.0)
        after = lax.cumsum(log1m, axis=3, reverse=True) - log1m
        logw = jax.nn.log_sigmoid(z) + after
        w = jnp.where(mask, jnp.exp(jnp.where(mask, logw, 0.0)), 0.0)
        outs.append(jnp.einsum('bhqk,bhkd->bhqd', w, vb))
    return jnp.concatenate(outs, axis=2).astype(v.dtype)

def pooling_mixer(u, w_pool, pool_scale):
    B, S, P = u.shape
    uf = u.astype(jnp.float32)
    cs = jnp.concatenate([jnp.zeros((B, 1, P), jnp.float32), jnp.cumsum(uf, axis=1)], axis=1)
    t = jnp.arange(S)
    parts = []
    for g, win in enumerate(POOL_WINDOWS):
        sl = slice(g * POOL_GROUP_DIM, (g + 1) * POOL_GROUP_DIM)
        lo = jnp.maximum(t + 1 - win, 0)
        cnt = (t + 1 - lo).astype(jnp.float32)
        csg = cs[..., sl]
        mean = (csg[:, 1:] - csg[:, lo]) / cnt[None, :, None]
        parts.append(mean - uf[..., sl])
    pooled = jnp.stack(parts, axis=2)
    y = jnp.einsum('bsgc,gcd->bsgd', pooled, w_pool.astype(jnp.float32)).reshape(B, S, P)
    return (y * pool_scale.astype(jnp.float32)).astype(u.dtype)

def second_inputs(seed: int = 0) -> dict:
    key = jax.random.key(seed)
    ks = jax.random.split(key, 16)
    f32 = jnp.float32

    def nrm(k, shape, fan_in):
        return jax.random.normal(k, shape, f32) * fan_in ** -0.5

    def gain(k):
        return 1.0 + 0.05 * jax.random.normal(k, (DEPTH, D_MODEL), f32)

    return {
        "x": jax.random.normal(ks[0], (BATCH, SEQ, D_MODEL), f32),
        "c": jax.random.normal(ks[1], (BATCH, D_MODEL), f32),
        "w_cond": nrm(ks[2], (DEPTH, D_MODEL, N_MOD * D_MODEL), D_MODEL),
        "b_cond": 0.01 * jax.random.normal(ks[3], (DEPTH, N_MOD * D_MODEL), f32),
        "g_mix_pre": gain(ks[4]),
        "g_mix_post": gain(ks[5]),
        "w_in": nrm(ks[6], (DEPTH, D_MODEL, IN_WIDTH_2), D_MODEL),
        "w_pool": nrm(ks[7], (DEPTH, POOL_GROUPS, POOL_GROUP_DIM, POOL_GROUP_DIM), POOL_GROUP_DIM),
        "pool_scale": 1.0 + 0.1 * jax.random.normal(ks[8], (DEPTH, POOL_WIDTH), f32),
        "w_out": nrm(ks[9], (DEPTH, MIX_WIDTH_2, D_MODEL), MIX_WIDTH_2),
        "g_ffn_pre": gain(ks[10]),
        "g_ffn_post": gain(ks[11]),
        "w_gate": nrm(ks[12], (DEPTH, D_MODEL, D_FF), D_MODEL),
        "w_up": nrm(ks[13], (DEPTH, D_MODEL, D_FF), D_MODEL),
        "w_down": nrm(ks[14], (DEPTH, D_FF, D_MODEL), D_FF),
    }

def second_block(x, c, w_cond, b_cond, g_mix_pre, g_mix_post, w_in, w_pool, pool_scale,
              w_out, g_ffn_pre, g_ffn_post, w_gate, w_up, w_down):
    B, S, D = x.shape
    for l in range(DEPTH):
        mod = jax.nn.silu(c) @ w_cond[l] + b_cond[l]
        shift_m, scale_m, gate_m, shift_f, scale_f, gate_f = [
            m[:, None, :] for m in jnp.split(mod, N_MOD, axis=-1)]

        h = rmsnorm(x, g_mix_pre[l]) * (1.0 + scale_m) + shift_m
        proj = h @ w_in[l]
        q, k, v, u = jnp.split(proj, [SB_WIDTH, 2 * SB_WIDTH, 3 * SB_WIDTH], axis=-1)
        to_heads = lambda a: a.reshape(B, S, SB_HEADS, SB_HEAD_DIM).transpose(0, 2, 1, 3)
        attn = stick_breaking_attention(to_heads(q), to_heads(k), to_heads(v))
        attn = attn.transpose(0, 2, 1, 3).reshape(B, S, SB_WIDTH)
        pool = pooling_mixer(u, w_pool[l], pool_scale[l])
        mix = jnp.concatenate([attn, pool], axis=-1) @ w_out[l]
        x = x + gate_m * rmsnorm(mix, g_mix_post[l])

        h = rmsnorm(x, g_ffn_pre[l]) * (1.0 + scale_f) + shift_f
        f = (jax.nn.silu(h @ w_gate[l]) * (h @ w_up[l])) @ w_down[l]
        x = x + gate_f * rmsnorm(f, g_ffn_post[l])
    return x


def setup_inputs(seed=0):
    out = dict(first_inputs(seed))
    for name, value in second_inputs(seed + 1).items():
        if name != "x":
            out[name + "_2"] = value
    return out


def reference(
    x, w_in, gmlp_w_s, gmlp_b_s, gmlp_ln_g, gmlp_ln_b, lam_q1, lam_k1, lam_q2, lam_k2,
    diff_subln_g, w_out, ln1_g, ln1_b, w_gu, w_down, ln2_g, ln2_b, c_2, w_cond_2, b_cond_2,
    g_mix_pre_2, g_mix_post_2, w_in_2, w_pool_2, pool_scale_2, w_out_2, g_ffn_pre_2,
    g_ffn_post_2, w_gate_2, w_up_2, w_down_2,
):
    x = first_block(
        x, w_in, gmlp_w_s, gmlp_b_s, gmlp_ln_g, gmlp_ln_b, lam_q1, lam_k1, lam_q2, lam_k2,
        diff_subln_g, w_out, ln1_g, ln1_b, w_gu, w_down, ln2_g, ln2_b,
    )
    return second_block(
        x, c_2, w_cond_2, b_cond_2, g_mix_pre_2, g_mix_post_2, w_in_2, w_pool_2, pool_scale_2,
        w_out_2, g_ffn_pre_2, g_ffn_post_2, w_gate_2, w_up_2, w_down_2,
    )


_drawn_inputs = setup_inputs


def setup_inputs(seed=0):
    import zlib

    import numpy as np

    out = dict(_drawn_inputs(seed))
    spreads = {}
    factors = {'gmlp_b_s': 3.491,
     'gmlp_ln_g': 7.781,
     'gmlp_ln_b': 33.21,
     'lam_q1': 161.04,
     'lam_k2': 161.362,
     'diff_subln_g': 3.305,
     'ln2_b': 2.735,
     'b_cond_2': 3.582,
     'lam_k1': 3.887}
    for name, (base, spread) in spreads.items():
        noise = np.random.default_rng([zlib.crc32(name.encode()), seed]).standard_normal(out[name].shape)
        drawn = base * np.exp(spread * noise) if base else spread * noise
        out[name] = jnp.asarray(drawn.astype(out[name].dtype))
    for name, factor in factors.items():
        out[name] = (out[name] * factor).astype(out[name].dtype)
    return out
```

```python
from contextlib import ExitStack

import numpy as np

import concourse.bass as bass
from concourse import mybir

F32 = mybir.dt.float32
FR = mybir.dt.float32r
U32 = mybir.dt.uint32
I32 = mybir.dt.int32
BF = mybir.dt.bfloat16
ALU = mybir.AluOpType
ACT = mybir.ActivationFunctionType
AX = mybir.AxisListType

D = 1024
S = 1024
NB = 8
FF = 2816
BIG = 1.0e30
OFF_BQ, OFF_BK, OFF_BV = 512, 1024, 1536
OFF_CQ, OFF_CK, OFF_CV = 2048, 2304, 2560
OFF_IQ, OFF_IK, OFF_IW = 2816, 3072, 3104
ALPHA = 2.0 ** 0.25
LAM_INIT = 0.2
LN_EPS = 1e-5
EPS = 1e-6
GELU_C = 0.7978845608028654
NRAW = 3
NU = 5
CHUNKS = [(0, 6), (6, 6), (12, 6), (18, 4)]
WINDOWS = (2, 4, 8, 16)
C_ID, C_NU, C_N1, C_Q, C_END = 0, 128, 256, 384, 386


def shape_constants():
    p = np.arange(128)[:, None]
    r = np.arange(1024)[None, :] - 896
    neg = -np.abs(p - r).astype(np.float32)
    neg = np.where((r >= 64) & (p < 64), np.float32(-BIG), neg).astype(np.float32)
    q = np.arange(128)[None, :]
    c = np.zeros((128, C_END), np.float32)
    c[:, C_ID:C_ID + 128] = np.eye(128)
    c[:, C_NU:C_NU + 128] = -(p >= q).astype(np.float32)
    c[:, C_N1:C_N1 + 128] = -1.0
    for j in range(2):
        for h in range(2):
            c[64 * h:64 * h + 64, C_Q + j] = 2.0 ** (2 * (2 * j + h + 1) - 3)
    m = np.zeros((128, 4, 3, 128), np.float32)
    s_ = np.arange(128)[:, None]
    t_ = np.arange(128)[None, :]
    for g, w in enumerate(WINDOWS):
        eye = (s_ == t_).astype(np.float32)
        m[:, g, 0, :] = ((s_ <= t_) & (s_ > t_ - w)) / w - eye
        m[:, g, 1, :] = ((s_ - 128) > t_ - w) / w
        m[:, g, 2, :] = ((s_ <= t_) & (s_ > t_ - w)) / np.minimum(t_ + 1, w) - eye
    return c, neg, m.reshape(128, 1536)


class Queue:

    def __init__(self, sem):
        self.sem = sem
        self.n = 0
        self.items = []
        self.held = []

    def put(self, fn, waits, inc=True):
        self.items.append(([*self.held, waits], fn, self.sem if inc else None, 1))
        self.held = []
        if inc:
            self.n += 1
        return (self.sem, self.n)

    def now(self):
        return (self.sem, self.n)

    def emit(self, eng):
        seen = {}
        for waits, fn, sem, k in self.items:
            need = {}
            flat(waits, need)
            for s, v in need.values():
                if seen.get(s.name, 0) < v:
                    eng.wait_ge(s, v)
                    seen[s.name] = v
            if fn is None:
                continue
            ins = fn(eng)
            if sem is not None:
                ins.then_inc(sem, k)


def flat(waits, need):
    if not waits:
        return
    if isinstance(waits, tuple) and len(waits) == 2 and isinstance(waits[1], int):
        s, v = waits
        if v > need.get(s.name, (s, 0))[1]:
            need[s.name] = (s, v)
        return
    for w in waits:
        flat(w, need)


def merge(*gens):
    left = [[g, n, 0] for g, n in gens]
    while left:
        left.sort(key=lambda x: x[2] / x[1])
        try:
            next(left[0][0])
            left[0][2] += 1
        except StopIteration:
            left.pop(0)


def run(gen):
    for _ in gen:
        pass


def build(nc, T, out, debug=None):
    top = ExitStack()
    with top:
        def sem(name):
            return top.enter_context(nc.semaphore(name))

        def sb(ctx, name, n, dt=F32, p=128):
            return ctx.enter_context(nc.sbuf_tensor(name, [p, n], dt))

        PE, DV, AC, PO, SP = [Queue(sem("s_" + n)) for n in ("pe", "dve", "act", "pool", "sp")]
        NDS = 32
        dsem = [sem(f"d{i}") for i in range(NDS)]
        dcount = [0] * NDS
        dnext = [0]
        drams = []

        def dma(q, o, i, *waits, store=False):
            k = dnext[0] % NDS
            dnext[0] += 1
            prev = (dsem[k], 16 * dcount[k]) if dcount[k] else None
            dcount[k] += 1
            q.items.append(([*q.held, waits, prev], lambda e: e.dma_start(o, i), dsem[k], 16))
            q.held = []
            tok = (dsem[k], 16 * dcount[k])
            if store:
                drams.append(tok)
            return tok

        def barrier():
            toks = [q.now() for q in (PE, DV, AC, PO)] + [(dsem[k], 16 * dcount[k]) for k in range(NDS) if dcount[k]]
            for q in (PE, DV, AC, PO):
                q.held = [toks]
            return toks

        def act(o, i, func, *w, bias=0.0, scale=1.0, acc=None):
            if acc is None:
                return AC.put(lambda e: e.activation(o, i, func, bias=bias, scale=scale), w)
            return AC.put(lambda e: e.activation(o, i, func, bias=bias, scale=scale, accum_out=acc), w)

        def copy_a(o, i, *w, scale=1.0):
            return act(o, i, ACT.Copy, *w, scale=scale)

        def copy_v(o, i, *w):
            return DV.put(lambda e: e.tensor_copy(o, i), w)

        def ts(o, i, s1, s2, op0, op1, *w, acc=None, q=None):
            q = q or DV
            if acc is not None:
                return q.put(lambda e: e.tensor_scalar(o, i, s1, s2, op0, op1, accum_out=acc), w)
            if op1 is None:
                return q.put(lambda e: e.tensor_scalar(o, i, s1, None, op0), w)
            return q.put(lambda e: e.tensor_scalar(o, i, s1, s2, op0, op1), w)

        def tt(o, a, b, op, *w, q=None):
            return (q or DV).put(lambda e: e.tensor_tensor(o, a, b, op), w)

        def stt(o, a, s, b, op0, op1, *w):
            return DV.put(lambda e: e.scalar_tensor_tensor(out=o, in0=a, scalar=s, in1=b, op0=op0, op1=op1), w)

        def ttr(o, a, b, scale, init, op0, op1, acc, *w):
            return DV.put(lambda e: e.tensor_tensor_reduce(out=o, in0=a, in1=b, scale=scale, scalar=init,
                                                           op0=op0, op1=op1, accum_out=acc), w)

        def mm(o, l, r, start, stop, *w, inc=False, skip=False):
            return PE.put(lambda e: e.matmul(o, l, r, start=start, stop=stop, skip_group_check=skip), w, inc)

        def tr(o, i, idn, *w, inc=False):
            return PE.put(lambda e: e.transpose(o, i, idn), w, inc)

        class Ring:

            def __init__(self, bufs):
                self.bufs = bufs
                self.free = [(j, None) for j in range(len(bufs))]

            def take(self):
                j, toks = self.free.pop(0)
                return j, self.bufs[j], toks

            def give(self, j, *toks):
                self.free.append((j, toks))

        banks = [top.enter_context(nc.psum_tensor(f"bank{i}", [128, 512], F32)) for i in range(8)]
        G = Ring(banks[0:3])
        L = Ring(banks[3:6])
        X = Ring(banks[6:8])

        con = sb(top, "con", C_END)
        t_con = dma(SP, con[:, :], T["consts"])
        idn = con[:, C_ID:C_ID + 128]
        negu = con[:, C_NU:C_NU + 128]
        neg1 = con[:, C_N1:C_N1 + 128]
        st = sb(top, "st", 512)
        modv = None

        raw = [sb(top, f"raw{i}", 1024) for i in range(NRAW)]
        wh = [sb(top, f"wh{i}", 1024, FR) for i in range(NU)]
        wl = [sb(top, f"wl{i}", 1024, FR) for i in range(NU)]
        rsem = [sem(f"r{i}") for i in range(NRAW)]

        def plan():
            for c in (OFF_IQ, OFF_IQ + 128, OFF_IK):
                yield ("F", "w_in", c)
            for j in range(4):
                yield ("T", "w_in", j, 0)
            for h in range(4):
                for o in (OFF_BQ, OFF_BK, OFF_BV):
                    yield ("F", "w_in", o + 128 * h)
            for h in range(2):
                for o in (OFF_CQ, OFF_CK, OFF_CV):
                    yield ("F", "w_in", o + 128 * h)
            for n in range(2):
                for j in range(4):
                    yield ("T", "w_out", j, 512 * n)
            for a, k in CHUNKS:
                for f in range(a, a + k):
                    yield ("F", "w_gu", 128 * f)
                    yield ("F", "w_gu", FF + 128 * f)
                for n in range(2):
                    for j in range(a // 2, (a + k) // 2):
                        yield ("T", "w_down", j, 512 * n)
            for n in range(4):
                for j in range(4):
                    yield ("R", "w_cond_2", j, 512 * n)
            for n in range(2):
                for j in range(4):
                    yield ("T", "w_in_2", j, 1024 + 512 * n)
            for h in range(4):
                yield ("F", "w_in_2", 128 * h)
                yield ("F", "w_in_2", 512 + 128 * h)
            for n in range(2):
                for j in range(4):
                    yield ("T", "w_out_2", j, 512 * n)
            for n in range(4, 12):
                for j in range(4):
                    yield ("R", "w_cond_2", j, 512 * n)
            for a, k in CHUNKS:
                for f in range(a, a + k):
                    yield ("F", "w_gate_2", 128 * f)
                    yield ("F", "w_up_2", 128 * f)
                for n in range(2):
                    for j in range(a // 2, (a + k) // 2):
                        yield ("T", "w_down_2", j, 512 * n)

        keys = list(plan())
        raw_free = [None] * NRAW
        raw_tok = {}
        split_tok = {}
        raw_rel = set()
        rel = {}
        slot_of = {}
        at = {"dma": 0, "split": 0, "get": 0, "slots": 0}
        slot_prev = [None] * NU

        def pump():
            while True:
                moved = False
                m = at["dma"]
                if m < len(keys) and (m < NRAW or (m - NRAW) in raw_rel):
                    key = keys[m]
                    w = T[key[1]]
                    r = raw[m % NRAW]
                    if key[0] == "F":
                        dst = r[:, :].rearrange("p (k c) -> p k c", k=8)
                        wv = w.rearrange("(k p) c -> p k c", p=128)
                        if key[2] == OFF_IK and key[1] == "w_in":
                            pairs = [(dst[:, :, 32 * j:32 * j + 32], wv[:, :, key[2]:key[2] + 32]) for j in range(4)]
                        else:
                            pairs = [(dst, wv[:, :, key[2]:key[2] + 128])]
                    else:
                        dst = r[:, :].rearrange("p (k c) -> p k c", k=2)
                        wv = w[256 * key[2]:256 * key[2] + 256, key[3]:key[3] + 512]
                        pairs = [(dst, wv.rearrange("(k p) c -> p k c", p=128))]
                    toks = []
                    for j, (o, i) in enumerate(pairs):
                        if len(pairs) == 1:
                            cnt = at.get(m % NRAW, 0) + 16
                            at[m % NRAW] = cnt
                            SP.items.append(([raw_free[m % NRAW]], lambda e, o=o, i=i: e.dma_start(o, i),
                                             rsem[m % NRAW], 16))
                            toks.append((rsem[m % NRAW], cnt))
                        else:
                            toks.append(dma(SP, o, i, raw_free[m % NRAW]))
                    raw_tok[m] = toks
                    at["dma"] += 1
                    moved = True
                m = at["split"]
                if m < len(keys) and m < at["dma"] and m <= at["get"] + NU:
                    if keys[m][0] == "R":
                        at["split"] += 1
                        moved = True
                    else:
                        s = at["slots"] % NU
                        if slot_prev[s] is None or slot_prev[s] in rel:
                            prev = rel.get(slot_prev[s])
                            r = raw[m % NRAW]
                            th = copy_a(wh[s][:, :], r[:, :], raw_tok[m], prev)
                            tl = tt(wl[s][:, :], r[:, :], wh[s][:, :].bitcast(F32), ALU.subtract, th, raw_tok[m], prev, q=PO)
                            raw_free[m % NRAW] = (th, tl)
                            raw_rel.add(m)
                            split_tok[m] = (th, tl)
                            slot_of[m] = s
                            slot_prev[s] = m
                            at["slots"] += 1
                            at["split"] += 1
                            moved = True
                if not moved:
                    return

        def get(*key):
            m = at["get"]
            assert keys[m] == key, (keys[m], key)
            at["get"] += 1
            pump()
            if key[0] == "R":
                return m, raw[m % NRAW], None, raw_tok[m]
            assert m in split_tok, key
            s = slot_of[m]
            return m, wh[s], wl[s], split_tok[m]

        def done(m, *toks):
            if keys[m][0] == "R":
                raw_free[m % NRAW] = toks
                raw_rel.add(m)
            else:
                rel[m] = toks
            pump()

        def gemm_f(u, xh, xl, t0, n, w):
            m, h, l, tok = u
            j, bank, fr = G.take()
            for k in range(8):
                a, b = h[:, 128 * k:128 * k + 128], l[:, 128 * k:128 * k + 128]
                xa, xb = xh[:, 1024 * k + t0:1024 * k + t0 + n], xl[:, 1024 * k + t0:1024 * k + t0 + n]
                mm(bank[:, 0:n], a, xa, k == 0, False, tok, w, fr)
                mm(bank[:, 0:n], a, xb, False, False)
                r = mm(bank[:, 0:n], b, xa, False, k == 7, inc=k == 7)
            return j, bank, r

        def gemm_t(us, xh, xl, tb, w, ks=None, stride=1024):
            j, bank, fr = G.take()
            nk = 2 * len(us)
            for k in range(nk):
                m, h, l, tok = us[k // 2]
                c = 512 * (k % 2)
                o = stride * k + 128 * tb
                xa, xb = xh[:, o:o + 128], xl[:, o:o + 128]
                mm(bank[:, :], xa, h[:, c:c + 512], k == 0, False, tok, w, fr)
                mm(bank[:, :], xa, l[:, c:c + 512], False, False)
                r = mm(bank[:, :], xb, h[:, c:c + 512], False, k == nk - 1, inc=k == nk - 1)
            return j, bank, r

        def gemm_tf(u, xh, xl, tb, w):
            m, h, l, tok = u
            j, bank, fr = G.take()
            for k in range(8):
                o = 1024 * k + 128 * tb
                xa, xb = xh[:, o:o + 128], xl[:, o:o + 128]
                a, b = h[:, 128 * k:128 * k + 128], l[:, 128 * k:128 * k + 128]
                mm(bank[:, 0:128], xa, a, k == 0, False, tok, w, fr)
                mm(bank[:, 0:128], xa, b, False, False)
                r = mm(bank[:, 0:128], xb, a, False, k == 7, inc=k == 7)
            return j, bank, r

        def turn(src, tb, xh, xl, *w):
            last = None
            for half in range(2):
                j, bank, fr = X.take()
                for k in range(4):
                    c = 128 * (4 * half + k)
                    t = tr(bank[:, 128 * k:128 * k + 128], src[:, c:c + 128], idn, w, fr, t_con, inc=k == 3)
                v = bank[:, :].rearrange("p (k c) -> p k c", k=4)
                oh = xh[:, :].rearrange("p (k c) -> p k c", k=8)[:, 4 * half:4 * half + 4, 128 * tb:128 * tb + 128]
                ol = xl[:, :].rearrange("p (k c) -> p k c", k=8)[:, 4 * half:4 * half + 4, 128 * tb:128 * tb + 128]
                a = copy_a(oh, v, t)
                b = tt(ol, v, oh.bitcast(F32), ALU.subtract, a)
                X.give(j, b)
                last = b
            return last

        stn = [0]
        st_tok = {}

        def small(n):
            if stn[0] + n > 512:
                stn[0] = 0
            o = stn[0]
            stn[0] += n
            return st[:, o:o + n]

        bns = sb(top, "bns", 24)

        def mean_rstd(src, eps, *w):
            mv, r = small(2), small(2)
            a = DV.put(lambda e: e.bn_stats(bns[:, 0:6], src[:, 0:512]), w)
            b = DV.put(lambda e: e.bn_stats(bns[:, 6:12], src[:, 512:1024]), w)
            c = DV.put(lambda e: e.bn_aggr(mv, bns[:, 0:12]), (a, b))
            d = ts(r[:, 0:1], mv[:, 1:2], eps, None, ALU.add, None, c)
            f = act(r[:, 1:2], r[:, 0:1], ACT.Sqrt, d)
            g = DV.put(lambda e: e.reciprocal(r[:, 0:1], r[:, 1:2]), (f,))
            return mv[:, 0:1], r[:, 0:1], g

        def rms(src, eps, junk, *w):
            ss, r = small(1), small(2)
            a = act(junk, src, ACT.Square, w, acc=ss)
            b = ts(r[:, 0:1], ss, 1.0 / 1024, eps, ALU.mult, ALU.add, a)
            f = act(r[:, 1:2], r[:, 0:1], ACT.Sqrt, b)
            g = DV.put(lambda e: e.reciprocal(r[:, 0:1], r[:, 1:2]), (f,))
            return r[:, 0:1], g, a

        mix_d, x2_d = T["mix_d"], T["x2_d"]
        xd = T["x"]

        ph = ExitStack()
        xh, xl = sb(ph, "xh", 8192, FR), sb(ph, "xl", 8192, FR)
        score = sb(ph, "score", 4224)
        cols = {}
        o = 0
        for i in range(2, 8):
            cols[i] = (o, 128 * (i + 1))
            o += 128 * (i + 1)
        vals = [sb(ph, f"vals{i}", 1024) for i in range(4)]
        V = Ring(vals)
        pt = [sb(ph, f"pt{i}", 1024) for i in range(2)]
        PT = Ring(pt)
        cand = sb(ph, "cand", 64)
        nd = sb(ph, "nd", 1024)
        t_nd = dma(SP, nd[:, :], T["dist"])
        mixw = {}

        t_x = [None] * 8
        for tb in range(8):
            j, buf, fr = V.take()
            d = dma(SP, buf[:, :], xd[128 * tb:128 * tb + 128, :], fr)
            t_x[tb] = turn(buf, tb, xh, xl, d)
            V.give(j, t_x[tb], PE.now())

        pump()
        sub = ExitStack()
        iq, ik, iw = sb(sub, "iq", 2048), sb(sub, "ik", 1024), sb(sub, "iw", 64)
        wih, wil, wir = sb(sub, "wih", 64, FR), sb(sub, "wil", 64, FR), sb(sub, "wir", 64)
        t_w = dma(SP, wir[:, :].rearrange("p (k c) -> p k c", k=8),
                  T["w_in"].rearrange("(k p) c -> p k c", p=128)[:, :, OFF_IW:OFF_IW + 8])
        th = copy_a(wih[:, :], wir[:, :], t_w)
        tl = tt(wil[:, :], wir[:, :], wih[:, :].bitcast(F32), ALU.subtract, th)
        t_iq = []
        for n, c in enumerate((OFF_IQ, OFF_IQ + 128, OFF_IK)):
            u = get("F", "w_in", c)
            for half in range(2):
                j, bank, r = gemm_f(u, xh, xl, 512 * half, 512, t_x)
                dst = iq[:, 1024 * n + 512 * half:1024 * n + 512 * half + 512] if n < 2 else ik[:, 512 * half:512 * half + 512]
                e = copy_v(dst, bank[:, :], r) if half else copy_a(dst, bank[:, :], r)
                G.give(j, e)
                t_iq.append(e)
            done(u[0], r)
        t_iw = []
        for tb in range(8):
            j, bank, fr = G.take()
            for k in range(8):
                o = 1024 * k + 128 * tb
                mm(bank[:, 0:8], xh[:, o:o + 128], wih[:, 8 * k:8 * k + 8], k == 0, False, th, tl, fr)
                mm(bank[:, 0:8], xh[:, o:o + 128], wil[:, 8 * k:8 * k + 8], False, False)
                r = mm(bank[:, 0:8], xl[:, o:o + 128], wih[:, 8 * k:8 * k + 8], False, k == 7, inc=k == 7)
            e = ts(iw[:, 8 * tb:8 * tb + 8], bank[:, 0:8], 1.0 / 16, None, ALU.mult, None, r)
            G.give(j, e)
            t_iw.append(e)

        t_score = {}

        def scores():
            for i in range(2, 8):
                o, ln = cols[i]
                for c0 in range(0, ln, 512):
                    n = min(512, ln - c0)
                    prev = None
                    for h in range(8):
                        j, bank, fr = L.take()
                        pr = slice(32 * (h % 4), 32 * (h % 4) + 32)
                        q = iq[pr, 1024 * (h // 4) + 128 * i:1024 * (h // 4) + 128 * i + 128]
                        r = mm(bank[:, 0:n], q, ik[pr, c0:c0 + n], True, True, fr, t_iq, inc=True)
                        jv, vb, vf = V.take()
                        a = act(vb[:, 0:n], bank[:, 0:n], ACT.Relu, r, vf)
                        L.give(j, a)
                        dst = score[:, o + c0:o + c0 + n]
                        w8 = iw[:, 8 * i + h:8 * i + h + 1]
                        if h == 0:
                            prev = ts(dst, vb[:, 0:n], w8, None, ALU.mult, None, a, t_iw)
                        else:
                            prev = stt(dst, vb[:, 0:n], w8, dst, ALU.mult, ALU.add, a, prev)
                        V.give(jv, prev)
                        yield
                t_score[i] = DV.put(lambda e, o=o, ln=ln: e.memset(score[0:64, o + ln - 64:o + ln], -BIG), (prev,))

        run(scores())
        bt = barrier()
        sub.close()

        sub = ExitStack()
        au, av = sb(sub, "au", 2048), sb(sub, "av", 2048)
        wst = sb(sub, "wst", 512)
        lng = sb(sub, "lng", 512)
        bsc = sb(sub, "bsc", 8)
        gst = sb(sub, "gst", 256)
        tmp = sb(sub, "gtmp", 512)
        t_g = [dma(SP, lng[:, 0:256], T["gmlp_ln_g"].rearrange("a b -> (a b)").partition_broadcast(128), bt),
               dma(SP, lng[:, 256:512], T["gmlp_ln_b"].rearrange("a b -> (a b)").partition_broadcast(128), bt)]
        t_ws = dma(SP, tmp[:, :].rearrange("p (g s) -> p g s", g=4), T["gmlp_w_s"].rearrange("g t s -> t g s"), bt)
        t_b4 = dma(SP, gst[0:4, 0:128], T["gmlp_b_s"], bt)
        j, bank, fr = X.take()
        for g in range(4):
            t = tr(bank[:, 128 * g:128 * g + 128], tmp[:, 128 * g:128 * g + 128], idn, t_ws, fr, inc=g == 3)
        e1 = copy_v(wst[:, :], bank[:, :], t)
        X.give(j, e1)
        wv = wst[64:128, :].rearrange("p (g s) -> p g s", g=4)[:, :, 0:64]
        e1 = DV.put(lambda e: e.memset(wv, 0.0), (e1,))
        j, bank, fr = X.take()
        t = tr(bank[:, 0:4], gst[0:4, 0:128], idn[0:4, 0:4], t_b4, fr, inc=True)
        e2 = copy_v(bsc[:, 0:4], bank[:, 0:4], t)
        X.give(j, e2)
        us = [get("T", "w_in", j, 0) for j in range(4)]
        t_uv = []
        for tb in range(8):
            j, bank, r = gemm_t(us, xh, xl, tb, t_x)
            a = copy_a(au[:, 256 * tb:256 * tb + 256], bank[:, 0:256], r)
            b = copy_v(av[:, 256 * tb:256 * tb + 256], bank[:, 256:512], r, a)
            G.give(j, a, b)
            t_uv.append((a, b))
        for u in us:
            done(u[0], r)
        t_ge = {}
        for nm, a in (("u", au), ("v", av)):
            for q in range(4):
                s_ = a[:, 512 * q:512 * q + 512]
                t_ge[nm, q] = act(s_, s_, ACT.Gelu_apprx_tanh, t_uv)
        last = []
        for q in range(4):
            vq = av[:, 512 * q:512 * q + 512].rearrange("p (n c) -> p n c", c=64)
            s8 = gst[:, 8 * q:8 * q + 8]
            a = DV.put(lambda e, vq=vq, s8=s8: e.tensor_reduce(s8, vq, AX.X, ALU.add), (t_ge["v", q], t))
            b = ts(s8, s8, 1.0 / 64, None, ALU.mult, None, a)
            c = tt(vq, vq, s8.unsqueeze(2).broadcast_to([128, 8, 64]),
                   ALU.subtract, b)
            sq = tmp[:, 0:512]
            d = tt(sq, av[:, 512 * q:512 * q + 512], av[:, 512 * q:512 * q + 512], ALU.mult, c, e1, last)
            v8 = gst[:, 32 + 8 * q:40 + 8 * q]
            f = DV.put(lambda e, sq=sq, v8=v8: e.tensor_reduce(v8, sq.rearrange("p (n c) -> p n c", c=64), AX.X, ALU.add), (d,))
            g = ts(v8, v8, 1.0 / 64, LN_EPS, ALU.mult, ALU.add, f)
            h = act(gst[:, 64 + 8 * q:72 + 8 * q], v8, ACT.Sqrt, g)
            r8 = gst[:, 96 + 8 * q:104 + 8 * q]
            k = DV.put(lambda e, q=q, r8=r8: e.reciprocal(r8, gst[:, 64 + 8 * q:72 + 8 * q]), (h,))
            m = tt(vq, vq, r8.unsqueeze(2).broadcast_to([128, 8, 64]), ALU.mult, k)
            v2 = av[:, 512 * q:512 * q + 512].rearrange("p (n c) -> p n c", c=256)
            m = tt(v2, v2, lng[:, 0:256].unsqueeze(1).broadcast_to([128, 2, 256]), ALU.mult, m, t_g)
            m = tt(v2, v2, lng[:, 256:512].unsqueeze(1).broadcast_to([128, 2, 256]), ALU.add, m, t_g)
            last = m
        t_oa = []
        for g in range(4):
            j, bank, fr = L.take()
            mv = av[:, :].rearrange("p (n g c) -> p n g c", g=4, c=64)[:, :, g, :]
            r = mm(bank[:, :].rearrange("p (n c) -> p n c", n=8), wst[:, 128 * g:128 * g + 128], mv, True, True,
                   fr, last, e1, inc=True)
            uv = au[:, :].rearrange("p (n g c) -> p n g c", g=4, c=64)[:, :, g, :]
            e = stt(uv, bank[:, :].rearrange("p (n c) -> p n c", n=8), bsc[:, g:g + 1], uv, ALU.add, ALU.mult,
                    r, e2, [t_ge["u", q] for q in range(4)])
            L.give(j, e)
            t_oa.append(e)
        for tb in range(8):
            mixw[tb, "a"] = dma(SP, mix_d[128 * tb:128 * tb + 128, 0:256], au[:, 256 * tb:256 * tb + 256], t_oa, store=True)
        bt = barrier()
        sub.close()

        sub = ExitStack()
        hq = [[sb(sub, f"h{x}{i}", 1024) for x in "qkv"] for i in range(2)]
        hfree = [None, None]
        osb = sb(sub, "osb", 1024)
        sg = sb(sub, "sg", 128)
        lamt = sb(sub, "lamt", 264)
        t_sg = dma(SP, sg[:, :], T["diff_subln_g"].partition_broadcast(128), bt)
        t_l = [dma(SP, lamt[:, 64 * n:64 * n + 64], T[nm].partition_broadcast(128), bt)
               for n, nm in enumerate(("lam_q1", "lam_k1", "lam_q2", "lam_k2"))]
        a = ttr(lamt[:, 0:64], lamt[:, 0:64], lamt[:, 64:128], 1.0, 0.0, ALU.mult, ALU.add, lamt[:, 256:257], t_l)
        b = ttr(lamt[:, 128:192], lamt[:, 128:192], lamt[:, 192:256], 1.0, 0.0, ALU.mult, ALU.add, lamt[:, 257:258], t_l)
        c = act(lamt[:, 258:260], lamt[:, 256:258], ACT.Exp, a, b)
        d = tt(lamt[:, 260:261], lamt[:, 259:260], lamt[:, 258:259], ALU.subtract, c)
        t_lam = ts(lamt[:, 261:262], lamt[:, 260:261], -LAM_INIT, None, ALU.add, None, d)
        nlam = lamt[:, 261:262]

        def project(n, off, h, scale, xw):
            q, k, v = hq[n % 2]
            toks = []
            for dst, o in ((q, off[0]), (k, off[1])):
                u = get("F", "w_in", o + 128 * h)
                for half in range(2):
                    j, bank, r = gemm_f(u, xh, xl, 512 * half, 512, xw)
                    d = dst[:, 512 * half:512 * half + 512]
                    if dst is q:
                        e = ts(d, bank[:, :], scale, None, ALU.mult, None, r, hfree[n % 2]) if not isinstance(scale, float) \
                            else copy_a(d, bank[:, :], r, hfree[n % 2], scale=scale)
                    else:
                        e = copy_a(d, bank[:, :], r, hfree[n % 2])
                    G.give(j, e)
                    toks.append(e)
                    yield
                done(u[0], r)
            u = get("F", "w_in", off[2] + 128 * h)
            for tb in range(8):
                j, bank, r = gemm_tf(u, xh, xl, tb, xw)
                e = copy_a(v[:, 128 * tb:128 * tb + 128], bank[:, 0:128], r, hfree[n % 2])
                G.give(j, e)
                toks.append(e)
                yield
            done(u[0], r)
            ready[n] = toks

        ready = {}

        def softmax(i, q, k, bias, slope, w, wb):
            ln = 128 * (i + 1)
            jv, vb, vf = V.take()
            mx = small(4)
            prev = None
            for c0 in range(0, ln, 512):
                n = min(512, ln - c0)
                j, bank, fr = L.take()
                r = mm(bank[:, 0:n], q[:, 128 * i:128 * i + 128], k[:, c0:c0 + n], True, True, fr, w, inc=True)
                z = c0 // 512
                prev = ttr(vb[:, c0:c0 + n], bank[:, 0:n], bias[:, c0:c0 + n], 1.0, -3.0e38 if z == 0 else mx[:, 0:1],
                           ALU.add, ALU.max, mx[:, z:z + 1], r, vf, prev, wb)
                L.give(j, prev)
            m = mx[:, z:z + 1]
            nb = ts(mx[:, 2:3], m, -slope, None, ALU.mult, None, prev)
            e = act(vb[:, 0:ln], vb[:, 0:ln], ACT.Exp, nb, prev, bias=mx[:, 2:3], scale=slope, acc=mx[:, 3:4])
            rc = small(1)
            t = DV.put(lambda en: en.reciprocal(rc, mx[:, 3:4]), (e,))
            return jv, vb, e, rc, t

        def weigh(i, vb, v, vw, w, cols_v, obuf, scale, wo):
            jp, pb, pf = PT.take()
            toks = []
            for c0 in range(0, i + 1, 4):
                m = min(4, i + 1 - c0)
                j, bank, fr = X.take()
                for b in range(m):
                    t = tr(bank[:, 128 * b:128 * b + 128], vb[:, 128 * (c0 + b):128 * (c0 + b) + 128], idn, w, fr, inc=b == m - 1)
                e = copy_a(pb[:, 128 * c0:128 * (c0 + m)], bank[:, 0:128 * m], t, pf)
                X.give(j, e)
                toks.append(e)
            tlast = t
            j, bank, fr = X.take()
            nv = cols_v[1] - cols_v[0]
            for b in range(i + 1):
                r = mm(bank[:, 0:nv], pb[:, 128 * b:128 * b + 128], v[:, 128 * b + cols_v[0]:128 * b + cols_v[1]],
                       b == 0, b == i, toks, vw, fr, inc=b == i)
            PT.give(jp, r)
            if scale is None:
                e = copy_v(obuf, bank[:, 0:nv], r, wo)
            else:
                e = ts(obuf, bank[:, 0:nv], scale, None, ALU.mult, None, r, wo)
            X.give(j, e)
            return tlast, e, r

        ofree = [None]

        def attend_b(n, h):
            q, k, v = hq[n % 2]
            w = ready[n]
            slope = 2.0 ** (-2 * (h + 1))
            oe = []
            for i in range(8):
                bias = nd[:, 896 - 128 * i:1024]
                ln = 128 * (i + 1)
                a = softmax(i, q[0:64, :], k[0:64, :], bias, slope, w, t_nd)
                yield
                b = softmax(i, q[64:128, :], k[64:128, :], bias, slope, w, t_nd)
                c2 = small(1)
                t2 = tt(c2, b[3], nlam, ALU.mult, b[4], t_lam)
                t3 = ts(a[1][:, 0:ln], a[1][:, 0:ln], a[3], None, ALU.mult, None, a[2], a[4])
                t4 = stt(a[1][:, 0:ln], b[1][:, 0:ln], c2, a[1][:, 0:ln], ALU.mult, ALU.add, t3, t2, b[2])
                V.give(b[0], t4)
                yield
                tlast, e, r = weigh(i, a[1], v, w, t4, (0, 128), osb[:, 128 * i:128 * i + 128], None, ofree[0])
                V.give(a[0], tlast)
                oe.append(e)
                yield
            hfree[n % 2] = (r,)
            ss = small(24)
            jv, vb, vf = V.take()
            d = tt(vb[:, :], osb[:, :], osb[:, :], ALU.mult, oe, vf)
            d = DV.put(lambda en: en.tensor_reduce(ss[:, 0:8], vb[:, :].rearrange("p (n c) -> p n c", n=8), AX.X, ALU.add), (d,))
            V.give(jv, d)
            d = ts(ss[:, 0:8], ss[:, 0:8], 1.0 / 128, LN_EPS, ALU.mult, ALU.add, d)
            d = act(ss[:, 8:16], ss[:, 0:8], ACT.Sqrt, d)
            d = DV.put(lambda en: en.reciprocal(ss[:, 16:24], ss[:, 8:16]), (d,))
            d = ts(ss[:, 16:24], ss[:, 16:24], 1.0 - LAM_INIT, None, ALU.mult, None, d)
            yield
            for i in range(8):
                ob = osb[:, 128 * i:128 * i + 128]
                e = stt(ob, ob, ss[:, 16 + i:17 + i], sg[:, :], ALU.mult, ALU.mult, d, t_sg)
                mixw[i, h] = dma(SP, mix_d[128 * i:128 * i + 128, 256 + 128 * h:384 + 128 * h], ob, e, store=True)
            ofree[0] = [mixw[i, h] for i in range(8)]
            yield

        t_sel = {}

        def topk():
            cu, ci = cand[:, 0:6].bitcast(U32), cand[:, 0:6].bitcast(I32)
            cnt = cand[:, 8:14]
            rj = cand[:, 16:22]
            tmp6 = cand[:, 24:30]
            jj, junk, jf = V.take()
            V_hold = jf

            def count(thr, waits, op=ALU.is_ge):
                ts_ = []
                for n, i in enumerate(range(2, 8)):
                    o, ln = cols[i]
                    t1 = thr if isinstance(thr, float) else thr[:, n:n + 1]
                    ts_.append(ts(junk[:, 0:ln], score[:, o:o + ln], t1, 0.0, op, ALU.add, waits, t_score[i], V_hold,
                                  ts_[-1] if ts_ else None, acc=cnt[:, n:n + 1]))
                return ts_

            c = count(0.0, None)
            yield
            p = ts(ci, cnt, 256.0, -1.0, ALU.is_lt, ALU.mult, c)
            p = ts(cu, cu, 1 << 30, None, ALU.bitwise_xor, None, p)
            for b in range(30, -1, -1):
                c = count(cand[:, 0:6], (p,))
                yield
                r = ts(rj.bitcast(U32), cnt, 256.0, float(2 ** b), ALU.is_lt, ALU.mult, c)
                if b:
                    p = tt(cu, cu, rj.bitcast(U32), ALU.bitwise_xor, r)
                    p = ts(cu, cu, 1 << (b - 1), None, ALU.bitwise_xor, None, p)
                else:
                    p = tt(cu, cu, rj.bitcast(U32), ALU.bitwise_xor, r)
                yield
            c = count(cand[:, 0:6], (p,), ALU.is_gt)
            need = ts(tmp6, cnt, -1.0, 256.0, ALU.mult, ALU.add, c)
            jk, cum, cf = V.take()
            prev = None
            for n, i in enumerate(range(2, 8)):
                o, ln = cols[i]
                sc = score[:, o:o + ln]
                thr = cand[:, n:n + 1]
                a = ts(junk[:, 0:ln], sc, thr, None, ALU.is_equal, None, p, need, prev)
                b = DV.put(lambda e, ln=ln: e.tensor_tensor_scan(cum[:, 0:ln], junk[:, 0:ln], junk[:, 0:ln], 0.0,
                                                                 ALU.add, ALU.bypass), (a, cf, prev))
                d = stt(junk[:, 0:ln], cum[:, 0:ln], tmp6[:, n:n + 1], junk[:, 0:ln], ALU.is_le, ALU.mult, b)
                f = stt(sc, sc, thr, junk[:, 0:ln], ALU.is_gt, ALU.add, d)
                g = ts(sc, sc, -1.0, BIG, ALU.add, ALU.mult, f)
                prev = tt(sc, sc, nd[:, 896 - 128 * i:1024], ALU.add, g, t_nd)
                t_sel[i] = prev
                yield
            V.give(jj, prev)
            V.give(jk, prev)

        def attend_c(n, pair):
            q, k, v = hq[n % 2]
            w = ready[n]
            oe = []
            for i in range(8):
                bias = nd[:, 896 - 128 * i:1024] if i < 2 else score[:, cols[i][0]:cols[i][0] + cols[i][1]]
                for hh in range(2):
                    slope = 2.0 ** (-2 * (2 * pair + hh + 1))
                    pr = slice(64 * hh, 64 * hh + 64)
                    a = softmax(i, q[pr, :], k[pr, :], bias, slope, w, t_sel.get(i, t_nd))
                    yield
                    tlast, e, r = weigh(i, a[1], v, w, a[2], (64 * hh, 64 * hh + 64),
                                        osb[:, 128 * i + 64 * hh:128 * i + 64 * hh + 64], a[3], (ofree[0], a[4]))
                    V.give(a[0], tlast)
                    oe.append(e)
                    yield
                mixw[i, "c", pair] = dma(SP, mix_d[128 * i:128 * i + 128, 768 + 128 * pair:896 + 128 * pair],
                                         osb[:, 128 * i:128 * i + 128], oe, store=True)
            ofree[0] = [mixw[i, "c", pair] for i in range(8)]
            hfree[n % 2] = (r,)

        def heads_b():
            run(project(0, (OFF_BQ, OFF_BK, OFF_BV), 0, 2.0 ** (2 - 3), t_x))
            for h in range(4):
                nxt = None
                if h < 3:
                    nxt = project(h + 1, (OFF_BQ, OFF_BK, OFF_BV), h + 1, 2.0 ** (2 * (h + 2) - 3), t_x)
                else:
                    nxt = project(4, (OFF_CQ, OFF_CK, OFF_CV), 0, con[:, C_Q:C_Q + 1], t_x)
                for k, _ in enumerate(attend_b(h, h)):
                    if k % 2 == 0:
                        next(nxt, None)
                    yield
                run(nxt)

        if debug != "a":
            if debug == "notop":
                for i in range(2, 8):
                    t_sel[i] = t_con
                run(topk())
            merge((heads_b(), 104), (topk(), 70))
            run_c = [attend_c(4, 0), attend_c(5, 1)]
            nxt = project(5, (OFF_CQ, OFF_CK, OFF_CV), 1, con[:, C_Q + 1:C_Q + 2], t_x)
            for k, _ in enumerate(run_c[0]):
                if k % 2 == 0:
                    next(nxt, None)
            run(nxt)
            run(run_c[1])
        bt = barrier()
        sub.close()
        ph.close()

        def bc(ctx, name, src, *w):
            t = sb(ctx, name, 1024)
            return t, dma(SP, t[:, :], src.partition_broadcast(128), *w)

        def mix_gemm(wname, ah, al, tw, finish):
            for n in range(2):
                us = [get("T", wname, j, 512 * n) for j in range(4)]
                for tb in range(8):
                    j, bank, r = gemm_t(us, ah, al, tb, tw)
                    G.give(j, finish(tb, n, bank, r))
                for u in us:
                    done(u[0], r)

        def load_turn(ctx, src, ah, al, bt, toks):
            stage = [sb(ctx, f"stage{i}", 1024) for i in range(2)]
            fr = [bt, bt]
            r = []
            for tb in range(8):
                d = dma(SP, stage[tb % 2][:, :], src[128 * tb:128 * tb + 128, :], fr[tb % 2], toks(tb))
                r.append(turn(stage[tb % 2], tb, ah, al, d))
                fr[tb % 2] = PE.now()
            return r

        def ffn(ctx, yh, yl, tw, wg, wu, up_off, wd, acc, acc_tok, fresh=False):
            hh, hl = sb(ctx, "hh" + wg, 6144, FR), sb(ctx, "hl" + wg, 6144, FR)
            sil = [sb(ctx, f"sil{i}" + wg, 512) for i in range(2)]
            SR = Ring(sil)
            hfr = [None] * 6
            for a, kk in CHUNKS:
                ht = []
                for f in range(a, a + kk):
                    ug = get("F", wg, 128 * f)
                    uu = get("F", wu, up_off + 128 * f)
                    for half in range(2):
                        jg, bg, rg = gemm_f(ug, yh, yl, 512 * half, 512, tw)
                        ju, bu, ru = gemm_f(uu, yh, yl, 512 * half, 512, tw)
                        s, sbuf, sf = SR.take()
                        e = act(sbuf[:, :], bg[:, :], ACT.Silu, rg, sf)
                        G.give(jg, e)
                        m = tt(sbuf[:, :], sbuf[:, :], bu[:, :], ALU.mult, e, ru)
                        G.give(ju, m)
                        o = 1024 * (f - a) + 512 * half
                        c = copy_a(hh[:, o:o + 512], sbuf[:, :], m, hfr[f - a])
                        d = tt(hl[:, o:o + 512], sbuf[:, :], hh[:, o:o + 512].bitcast(F32), ALU.subtract, c, hfr[f - a])
                        SR.give(s, d)
                        ht.append((c, d))
                    done(ug[0], rg)
                    done(uu[0], ru)
                for n in range(2):
                    us = [get("T", wd, j, 512 * n) for j in range(a // 2, (a + kk) // 2)]
                    for tb in range(8):
                        j, bank, r = gemm_t(us, hh, hl, tb, ht)
                        dst = acc[:, 1024 * tb + 512 * n:1024 * tb + 512 * n + 512]
                        if fresh and a == 0:
                            e = copy_v(dst, bank[:, :], r, acc_tok[tb])
                        else:
                            e = tt(dst, bank[:, :], dst, ALU.add, r, acc_tok[tb])
                        acc_tok[tb] = (acc_tok[tb], e)
                        G.give(j, e)
                    for u in us:
                        done(u[0], r)
                hfr = [r] * 6

        def dump(buf, toks):
            for tb in range(8):
                dma(SP, out[128 * tb:128 * tb + 128, :], buf[:, 1024 * tb:1024 * tb + 1024], toks, store=True)

        G = Ring(banks[0:5])
        X = Ring(banks[5:8])
        ph = ExitStack()
        res = sb(ph, "res", 8192)
        yh, yl = sb(ph, "yh", 8192, FR), sb(ph, "yl", 8192, FR)
        sub = ExitStack()
        if debug in ("a", "mix", "notop"):
            wd_ = 256 if debug == "a" else 1024
            mz = DV.put(lambda e: e.memset(res[:, :], 0.0), ())
            for tb in range(8):
                d = dma(SP, res[:, 1024 * tb:1024 * tb + wd_], mix_d[128 * tb:128 * tb + 128, 0:wd_], bt, mz)
            dump(res, [(dsem[k], 16 * dcount[k]) for k in range(NDS) if dcount[k]])
        else:
            g1, tg1 = bc(sub, "g1", T["ln1_g"], bt)
            b1, tb1 = bc(sub, "b1", T["ln1_b"], bt)
            t_r = [dma(SP, res[:, 1024 * tb:1024 * tb + 1024], xd[128 * tb:128 * tb + 128, :], bt) for tb in range(8)]
            tm = load_turn(sub, mix_d, yh, yl, bt, lambda tb: [v for k, v in mixw.items() if k[0] == tb])
            t_r = list(t_r)

            def fin1(tb, n, bank, r):
                dst = res[:, 1024 * tb + 512 * n:1024 * tb + 512 * n + 512]
                e = stt(dst, dst, ALPHA, bank[:, :], ALU.mult, ALU.add, r, t_r[tb])
                t_r[tb] = (t_r[tb], e)
                return e

            mix_gemm("w_out", yh, yl, tm, fin1)
            pe_done = PE.now()
            ty = []
            for tb in range(8):
                src = res[:, 1024 * tb:1024 * tb + 1024]
                mu, rs, t = mean_rstd(src, LN_EPS, t_r[tb])
                t = ts(src, src, mu, rs, ALU.subtract, ALU.mult, t)
                t = tt(src, src, g1[:, :], ALU.mult, t, tg1)
                t = tt(src, src, b1[:, :], ALU.add, t, tb1)
                ty.append(turn(src, tb, yh, yl, t, pe_done))
                t_r[tb] = ts(src, src, ALPHA, None, ALU.mult, None, PE.now(), t)
            bt = barrier()
            sub.close()
            sub = ExitStack()
            ffn(sub, yh, yl, ty, "w_gu", "w_gu", FF, "w_down", res, t_r)
            bt = barrier()
            sub.close()

            sub = ExitStack()
            g2, tg2 = bc(sub, "g2", T["ln2_g"], bt)
            b2, tb2 = bc(sub, "b2", T["ln2_b"], bt)
            gp, tgp = bc(sub, "gp", T["g_mix_pre_2"], bt)
            cb = sb(sub, "cb", 1024)
            sm = sb(sub, "smod", 2048)
            bcnd = sb(sub, "bcnd", 2048)
            junk = sb(sub, "junk", 1024)
            cc = sb(sub, "cc", 8)
            c8 = sb(sub, "c8", 128, p=8)
            d = dma(SP, c8[:, :], T["c_2"].rearrange("(k p) -> k p", p=128), bt)
            j, bank, fr = X.take()
            t = tr(bank[:, 0:8], c8[:, :], idn[0:8, 0:8], d, fr, inc=True)
            e = act(cc[:, :], bank[:, 0:8], ACT.Silu, t)
            X.give(j, e)
            t_cc = e

            def make_cb(cb, cc, w):
                toks = []
                for k in range(8):
                    toks.append(ts(cb[:, 128 * k:128 * k + 128], neg1, cc[:, k:k + 1], -1.0, ALU.mult, ALU.mult, w, t_con))
                return toks

            t_cb = make_cb(cb, cc, t_cc)
            d = dma(SP, bcnd[:, :], T["b_cond_2"][0:2048].partition_broadcast(128), bt)

            def modulate(n0, n1, cb, t_cb, bias, tbias, dst):
                toks = []
                for n in range(n0, n1):
                    j, bank, fr = G.take()
                    for q in range(4):
                        u = get("R", "w_cond_2", q, 512 * n)
                        for k in range(2):
                            r = mm(bank[:, :], cb[:, 256 * q + 128 * k:256 * q + 128 * k + 128],
                                   u[1][:, 512 * k:512 * k + 512], q == 0 and k == 0, q == 3 and k == 1,
                                   u[3], t_cb, fr, inc=k == 1)
                        done(u[0], r)
                    o = 512 * (n - n0)
                    e = tt(dst[:, o:o + 512], bank[:, :], bias[:, o:o + 512], ALU.add, r, tbias)
                    G.give(j, e)
                    toks.append(e)
                return toks

            t_mod = modulate(0, 4, cb, t_cb, bcnd, d, sm)
            shift = sm[:, 0:1024]
            t_gs = stt(gp[:, :], sm[:, 1024:2048], 1.0, gp[:, :], ALU.add, ALU.mult, t_mod, tgp)

            t_h = []
            t_x2 = []
            yb = [sb(sub, f"yb{i}", 1024) for i in range(2)]
            ybf = [bt, bt]
            jfree = None
            for tb in range(8):
                src = res[:, 1024 * tb:1024 * tb + 1024]
                mu, rs, t = mean_rstd(src, LN_EPS, t_r[tb])
                t = ts(src, src, mu, rs, ALU.subtract, ALU.mult, t)
                t = tt(src, src, g2[:, :], ALU.mult, t, tg2)
                t = tt(src, src, b2[:, :], ALU.add, t, tb2)
                t_x2.append(dma(SP, x2_d[128 * tb:128 * tb + 128, :], src, t, store=True))
                rr, t2, jfree = rms(src, EPS, junk[:, :], t, jfree)
                y = yb[tb % 2]
                t = stt(y[:, :], src, rr, gp[:, :], ALU.mult, ALU.mult, t2, t_gs, ybf[tb % 2])
                t = tt(y[:, :], y[:, :], shift, ALU.add, t)
                t_h.append(turn(y, tb, yh, yl, t))
                ybf[tb % 2] = PE.now()
            bt = barrier()
            sub.close()
            if debug == "x2":
                dump(res, bt)
            else:
                sub = ExitStack()
                vt = sb(sub, "vt", 4096)
                sq = ExitStack()
                ut = sb(sq, "ut", 4096)
                bd = sb(sq, "bd", 1536)
                wp = sb(sq, "wp", 512)
                pl = [sb(sq, f"pl{i}", 1024) for i in range(2)]
                ps = sb(sq, "ps", 8)
                ps4 = sb(sq, "ps4", 128, p=4)
                t_bd = dma(SP, bd[:, :], T["bands"], bt)
                t_wp = dma(SP, wp[:, :].rearrange("p (g d) -> p g d", g=4), T["w_pool_2"].rearrange("g c d -> c g d"), bt)
                d = dma(SP, ps4[:, :], T["pool_scale_2"].rearrange("(g p) -> g p", p=128), bt)
                j, bank, fr = X.take()
                t = tr(bank[:, 0:4], ps4[:, :], idn[0:4, 0:4], d, fr, inc=True)
                t_ps = copy_v(ps[:, 0:4], bank[:, 0:4], t)
                X.give(j, t_ps)
                tv, tu = [], []
                for n, (dst, toks) in enumerate(((vt, tv), (ut, tu))):
                    us = [get("T", "w_in_2", j, 1024 + 512 * n) for j in range(4)]
                    for tb in range(8):
                        j, bank, r = gemm_t(us, yh, yl, tb, t_h)
                        e = copy_a(dst[:, 512 * tb:512 * tb + 512], bank[:, :], r)
                        G.give(j, e)
                        toks.append(e)
                    for u in us:
                        done(u[0], r)
                plf = [None, None]
                for g in range(4):
                    p_ = pl[g % 2]
                    te = []
                    for c in range(2):
                        j, bank, fr = X.take()
                        for b in range(4 * c, 4 * c + 4):
                            o = bank[:, 128 * (b % 4):128 * (b % 4) + 128]
                            ub = ut[:, 512 * b + 128 * g:512 * b + 128 * g + 128]
                            band = bd[:, 384 * g:384 * g + 384]
                            if b == 0:
                                r = mm(o, ub, band[:, 256:384], True, True, tu, t_bd, fr, inc=True)
                            else:
                                up = ut[:, 512 * (b - 1) + 128 * g:512 * (b - 1) + 128 * g + 128]
                                mm(o, ub, band[:, 0:128], True, False, tu, t_bd, fr)
                                r = mm(o, up, band[:, 128:256], False, True, inc=True)
                        e = copy_v(p_[:, 512 * c:512 * c + 512], bank[:, :], r, plf[g % 2])
                        X.give(j, e)
                        te.append(e)
                    for c in range(2):
                        j, bank, fr = X.take()
                        r = mm(bank[:, :], wp[:, 128 * g:128 * g + 128], p_[:, 512 * c:512 * c + 512], True, True,
                               te, t_wp, fr, inc=True)
                        e = ts(res[:, 1024 * (4 + g) + 512 * c:1024 * (4 + g) + 512 * c + 512], bank[:, :], ps[:, g:g + 1],
                               None, ALU.mult, None, r, t_ps, t_x2)
                        X.give(j, e)
                    plf[g % 2] = r
                bt = barrier()
                sq.close()

                sq = ExitStack()
                qk = [[sb(sq, f"s{x}{i}", 1024) for x in "qk"] for i in range(2)]
                lt = [sb(sq, f"lt{i}", 512) for i in range(3)]
                spb = [sb(sq, f"sp{i}", 512) for i in range(4)]
                wt = [sb(sq, f"wt{i}", 512) for i in range(2)]
                run_s = [sb(sq, f"rs{i}", 512) for i in range(2)]
                zb = sb(sq, "zb", 512, BF)
                t_zb = DV.put(lambda e: e.memset(zb[:, :], 0.0), ())
                LT, SPR, WT = Ring(lt), Ring(spb), Ring(wt)
                G, Z, O = Ring(banks[0:2]), Ring(banks[2:6]), Ring(banks[6:8])
                sfree = [bt, bt]
                sready = {}

                def project2(h):
                    toks = []
                    for n, dst in enumerate(qk[h % 2]):
                        u = get("F", "w_in_2", 512 * n + 128 * h)
                        for half in range(2):
                            j, bank, r = gemm_f(u, yh, yl, 512 * half, 512, t_h)
                            e = copy_a(dst[:, 512 * half:512 * half + 512], bank[:, :], r, sfree[h % 2],
                                       scale=0.125 if n == 0 else 1.0)
                            G.give(j, e)
                            toks.append(e)
                            yield
                        done(u[0], r)
                    sready[h] = toks

                def stick(h, hh, toks_out):
                    q, k = qk[h % 2]
                    pr = slice(64 * hh, 64 * hh + 64)
                    w = sready[h]
                    rs = run_s[hh]
                    for c in range(2):
                        jo, ob, fo = O.take()
                        mm(ob[0:64, :], zb[:, 0:64], zb[:, :], True, False, t_zb, fo, skip=True)
                        z0 = DV.put(lambda e: e.memset(rs[:, :], 0.0), (rfree[hh],))
                        state = {"sum": z0}

                        def first(b):
                            t0 = max(128 * b, 512 * c)
                            n = 512 * (c + 1) - t0
                            jz, z, fz = Z.take()
                            r = mm(z[:, 0:n], k[pr, 128 * b:128 * b + 128], q[pr, t0:t0 + n], True, False, fz, w, inc=True, skip=True)
                            jl, l, fl = LT.take()
                            a = act(l[:, 0:n], z[:, 0:n], ACT.Abs, r, fl)
                            a = act(l[:, 0:n], l[:, 0:n], ACT.Exp, a, scale=-1.0)
                            a = act(l[:, 0:n], l[:, 0:n], ACT.Ln, a, bias=1.0)
                            js, s_, fs = SPR.take()
                            d = stt(s_[:, 0:n], z[:, 0:n], 0.0, l[:, 0:n], ALU.max, ALU.add, a, fs)
                            LT.give(jl, d)
                            m = d
                            if 128 * b >= 512 * c:
                                m = PO.put(lambda e: e.affine_select(out=s_[:, 0:128], in_=s_[:, 0:128], compare_op=ALU.is_gt,
                                                                     fill=0.0, base=0, pattern=[[1, 128]],
                                                                     channel_multiplier=-1), (d,))
                            return b, t0, n, jz, z, js, s_, m, d

                        def second(x):
                            b, t0, n, jz, z, js, s_, m, d = x
                            o0 = t0 - 512 * c
                            top_b = 4 * c + 3
                            r = mm(z[:, 0:n], negu, s_[:, 0:n], False, b == top_b, m, d, inc=True, skip=True)
                            if b != top_b:
                                r = mm(z[:, 0:n], neg1, rs[:, o0:512], False, True, state["sum"], inc=True, skip=True)
                            if b:
                                state["sum"] = tt(rs[:, o0:512], rs[:, o0:512], s_[:, 0:n], ALU.add, r, m, state["sum"], q=PO)
                                SPR.give(js, state["sum"])
                            else:
                                SPR.give(js, r)
                                rfree[hh] = r
                            jw, wb, fw = WT.take()
                            e = act(wb[:, 0:n], z[:, 0:n], ACT.Exp, r, fw)
                            Z.give(jz, e)
                            if 128 * b >= 512 * c:
                                e = PO.put(lambda en: en.affine_select(out=wb[:, 0:128], in_=wb[:, 0:128], compare_op=ALU.is_gt,
                                                                       fill=0.0, base=0, pattern=[[1, 128]],
                                                                       channel_multiplier=-1), (e,))
                            r = mm(ob[0:64, o0:512], vt[:, 512 * b + 128 * h + 64 * hh:512 * b + 128 * h + 64 * hh + 64],
                                   wb[:, 0:n], False, b == 0, e, tv, inc=True, skip=True)
                            WT.give(jw, r)
                            return r

                        x = first(4 * c + 3)
                        yield
                        for b in range(4 * c + 2, -1, -1):
                            y = first(b)
                            r = second(x)
                            x = y
                            yield
                        r = second(x)
                        e = copy_v(res[pr, 1024 * h + 512 * c:1024 * h + 512 * c + 512], ob[0:64, :], r, t_x2)
                        O.give(jo, e)
                        toks_out.append(e)
                        yield
                    last_r[0] = r

                rfree = [bt, bt]
                last_r = [None]
                t_mix = []
                run(project2(0))
                for h in range(4):
                    gens = [(stick(h, 0, t_mix), 14), (stick(h, 1, t_mix), 14)]
                    if h < 3:
                        gens.append((project2(h + 1), 5))
                    merge(*gens)
                    sfree[h % 2] = (last_r[0], PE.now())
                bt = barrier()
                sq.close()
                sub.close()
                if debug == "mix2":
                    dump(res, bt)
                else:
                    sub = ExitStack()
                    G = Ring(banks[0:5])
                    X = Ring(banks[5:8])
                    gm, t1 = bc(sub, "gm", T["b_cond_2"][2048:3072], bt)
                    sf, t2 = bc(sub, "sf", T["b_cond_2"][3072:4096], bt)
                    gs, t3 = bc(sub, "gs", T["b_cond_2"][4096:5120], bt)
                    gf, t4 = bc(sub, "gf", T["b_cond_2"][5120:6144], bt)
                    gt, t5 = bc(sub, "gt", T["g_mix_post_2"], bt)
                    cb = sb(sub, "cb2", 1024)
                    cc = sb(sub, "cc2", 8)
                    c8 = sb(sub, "c82", 128, p=8)
                    junk = sb(sub, "junk2", 1024)
                    d = dma(SP, c8[:, :], T["c_2"].rearrange("(k p) -> k p", p=128), bt)
                    j, bank, fr = X.take()
                    t = tr(bank[:, 0:8], c8[:, :], idn[0:8, 0:8], d, fr, inc=True)
                    e = act(cc[:, :], bank[:, 0:8], ACT.Silu, t)
                    X.give(j, e)
                    t_cb = make_cb(cb, cc, e)
                    t_s = []
                    for k in range(8):
                        src = res[:, 1024 * k:1024 * k + 1024]
                        a = copy_a(yh[:, 1024 * k:1024 * k + 1024], src)
                        b = tt(yl[:, 1024 * k:1024 * k + 1024], src, yh[:, 1024 * k:1024 * k + 1024].bitcast(F32), ALU.subtract, a)
                        t_s += [a, b]
                    t_m = [None] * 8

                    def fin2(tb, n, bank, r):
                        e = copy_a(res[:, 1024 * tb + 512 * n:1024 * tb + 512 * n + 512], bank[:, :], r, t_s)
                        t_m[tb] = (t_m[tb], e)
                        return e

                    mix_gemm("w_out_2", yh, yl, t_s, fin2)
                    pe_done = PE.now()
                    m1 = modulate(4, 6, cb, t_cb, gm, t1, gm)
                    m2 = modulate(6, 8, cb, t_cb, sf, t2, sf)
                    m3 = modulate(8, 10, cb, t_cb, gs, t3, gs)
                    m4 = modulate(10, 12, cb, t_cb, gf, t4, gf)
                    m1 = tt(gm[:, :], gm[:, :], gt[:, :], ALU.mult, m1, t5)
                    d = dma(SP, gt[:, :], T["g_ffn_pre_2"].partition_broadcast(128), m1)
                    m3 = stt(gs[:, :], gs[:, :], 1.0, gt[:, :], ALU.add, ALU.mult, m3, d)
                    d = dma(SP, gt[:, :], T["g_ffn_post_2"].partition_broadcast(128), m3)
                    m4 = tt(gf[:, :], gf[:, :], gt[:, :], ALU.mult, m4, d)
                    t_gf = dma(SP, T["vec_d"], gf[0:1, :], m4, store=True)
                    xb = [sb(sub, f"xb{i}", 1024) for i in range(2)]
                    xbf = [bt, bt]
                    jfree = None
                    ty = []
                    t_x3 = []
                    for tb in range(8):
                        src = res[:, 1024 * tb:1024 * tb + 1024]
                        x_ = xb[tb % 2]
                        d = dma(SP, x_[:, :], x2_d[128 * tb:128 * tb + 128, :], xbf[tb % 2], t_x2)
                        rr, t, jfree = rms(src, EPS, junk[:, :], t_m[tb], jfree)
                        t = stt(src, src, rr, gm[:, :], ALU.mult, ALU.mult, t, m1)
                        t = tt(src, src, x_[:, :], ALU.add, t, d)
                        t_x3.append(dma(SP, mix_d[128 * tb:128 * tb + 128, :], src, t, store=True))
                        rr, t2, jfree = rms(src, EPS, junk[:, :], t, jfree)
                        t = stt(x_[:, :], src, rr, gs[:, :], ALU.mult, ALU.mult, t2, m3, t)
                        t = tt(x_[:, :], x_[:, :], sf[:, :], ALU.add, t, m2)
                        ty.append(turn(x_, tb, yh, yl, t, pe_done))
                        xbf[tb % 2] = PE.now()
                    bt = barrier()
                    sub.close()
                    sub = ExitStack()
                    t_acc = list(t_x3)
                    ffn(sub, yh, yl, ty, "w_gate_2", "w_up_2", 0, "w_down_2", res, t_acc, fresh=True)
                    bt = barrier()
                    sub.close()
                    sub = ExitStack()
                    gf = sb(sub, "gf3", 1024)
                    tgf = dma(SP, gf[:, :], T["vec_d"][0].partition_broadcast(128), bt, t_gf)
                    xb = [sb(sub, f"xc{i}", 1024) for i in range(4)]
                    junk = sb(sub, "junk3", 1024)
                    jfree = None
                    xbf = [bt] * 4
                    for tb in range(8):
                        src = res[:, 1024 * tb:1024 * tb + 1024]
                        x_ = xb[tb % 4]
                        d = dma(SP, x_[:, :], mix_d[128 * tb:128 * tb + 128, :], xbf[tb % 4], t_x3)
                        rr, t, jfree = rms(src, EPS, junk[:, :], t_acc[tb], jfree)
                        t = stt(src, src, rr, gf[:, :], ALU.mult, ALU.mult, t, tgf)
                        t = tt(src, src, x_[:, :], ALU.add, t, d)
                        xbf[tb % 4] = t
                        dma(SP, out[128 * tb:128 * tb + 128, :], src, t, store=True)
        sub.close()
        ph.close()
        SPw = [*drams]
        SP.items.append(([SPw], None, None, 0))
        block = top.enter_context(nc.Block())

        @block.sync
        def _(e):
            SP.emit(e)

        @block.scalar
        def _(e):
            AC.emit(e)

        @block.vector
        def _(e):
            DV.emit(e)

        @block.gpsimd
        def _(e):
            PO.emit(e)

        @block.tensor
        def _(e):
            PE.emit(e)


DEBUG = "full"
_NAMES = ['x', 'w_in', 'gmlp_w_s', 'gmlp_b_s', 'gmlp_ln_g', 'gmlp_ln_b', 'lam_q1', 'lam_k1', 'lam_q2', 'lam_k2',
          'diff_subln_g', 'w_out', 'ln1_g', 'ln1_b', 'w_gu', 'w_down', 'ln2_g', 'ln2_b', 'c_2', 'w_cond_2',
          'b_cond_2', 'g_mix_pre_2', 'g_mix_post_2', 'w_in_2', 'w_pool_2', 'pool_scale_2', 'w_out_2',
          'g_ffn_pre_2', 'g_ffn_post_2', 'w_gate_2', 'w_up_2', 'w_down_2']


def kernel(**inputs):
    import concourse.bacc as _bacc
    from concourse.bass_utils import run_bass_kernel_spmd as _run

    nc = _bacc.Bacc("TRN2", target_bir_lowering=False, num_devices=1)
    arrays, T = {}, {}
    for name in _NAMES:
        a = np.ascontiguousarray(inputs[name])
        arrays["in_" + name] = a
        T[name] = nc.dram_tensor("in_" + name, a.shape, mybir.dt.from_np(a.dtype), kind="ExternalInput").ap()[0]
    con, dist, bands = shape_constants()
    for name, a in (("consts", con), ("dist", dist), ("bands", bands)):
        arrays["in_" + name] = a
        T[name] = nc.dram_tensor("in_" + name, a.shape, F32, kind="ExternalInput").ap()
    T["mix_d"] = nc.dram_tensor("mix_d", (1024, 1024), F32, kind="Internal").ap()
    T["vec_d"] = nc.dram_tensor("vec_d", (1, 1024), F32, kind="Internal").ap()
    T["x2_d"] = nc.dram_tensor("x2_d", (1024, 1024), F32, kind="Internal").ap()
    out = nc.dram_tensor("out_0", (1, 1024, 1024), F32, kind="ExternalOutput").ap()
    build(nc, T, out[0], DEBUG)
    r = _run(nc, [arrays], core_ids=[0])
    return r.results[0]["out_0"]
```

```python
from contextlib import ExitStack

import numpy as np

import concourse.bass as bass
from concourse import mybir

F32 = mybir.dt.float32
FR = mybir.dt.float32r
U32 = mybir.dt.uint32
I32 = mybir.dt.int32
BF = mybir.dt.bfloat16
ALU = mybir.AluOpType
ACT = mybir.ActivationFunctionType
AX = mybir.AxisListType

D = 1024
S = 1024
NB = 8
FF = 2816
BIG = 1.0e30
OFF_BQ, OFF_BK, OFF_BV = 512, 1024, 1536
OFF_CQ, OFF_CK, OFF_CV = 2048, 2304, 2560
OFF_IQ, OFF_IK, OFF_IW = 2816, 3072, 3104
ALPHA = 2.0 ** 0.25
LAM_INIT = 0.2
LN_EPS = 1e-5
EPS = 1e-6
GELU_C = 0.7978845608028654
NRAW = 3
NU = 5
CHUNKS = [(0, 6), (6, 6), (12, 6), (18, 4)]
WINDOWS = (2, 4, 8, 16)
C_ID, C_NU, C_N1, C_Q, C_END = 0, 128, 256, 384, 386


def shape_constants():
    p = np.arange(128)[:, None]
    r = np.arange(1024)[None, :] - 896
    neg = -np.abs(p - r).astype(np.float32)
    neg = np.where((r >= 64) & (p < 64), np.float32(-BIG), neg).astype(np.float32)
    q = np.arange(128)[None, :]
    c = np.zeros((128, C_END), np.float32)
    c[:, C_ID:C_ID + 128] = np.eye(128)
    c[:, C_NU:C_NU + 128] = -(p >= q).astype(np.float32)
    c[:, C_N1:C_N1 + 128] = -1.0
    for j in range(2):
        for h in range(2):
            c[64 * h:64 * h + 64, C_Q + j] = 2.0 ** (2 * (2 * j + h + 1) - 3)
    m = np.zeros((128, 4, 3, 128), np.float32)
    s_ = np.arange(128)[:, None]
    t_ = np.arange(128)[None, :]
    for g, w in enumerate(WINDOWS):
        eye = (s_ == t_).astype(np.float32)
        m[:, g, 0, :] = ((s_ <= t_) & (s_ > t_ - w)) / w - eye
        m[:, g, 1, :] = ((s_ - 128) > t_ - w) / w
        m[:, g, 2, :] = ((s_ <= t_) & (s_ > t_ - w)) / np.minimum(t_ + 1, w) - eye
    return c, neg, m.reshape(128, 1536)


class Queue:

    def __init__(self, sem):
        self.sem = sem
        self.n = 0
        self.items = []

    def put(self, fn, waits, inc=True):
        self.items.append((flat(waits, {}), fn, self.sem if inc else None, 1))
        if inc:
            self.n += 1
        return (self.sem, self.n)

    def now(self):
        return (self.sem, self.n)

    def emit(self, eng):
        seen = {}
        for need, fn, sem, k in self.items:
            for s, v in need.values():
                if seen.get(s.name, 0) < v:
                    eng.wait_ge(s, v)
                    seen[s.name] = v
            if fn is None:
                continue
            ins = fn(eng)
            if sem is not None:
                ins.then_inc(sem, k)


def flat(waits, need):
    if not waits:
        return need
    if isinstance(waits, tuple) and len(waits) == 2 and isinstance(waits[1], int):
        s, v = waits
        if v > need.get(s.name, (s, 0))[1]:
            need[s.name] = (s, v)
        return need
    for w in waits:
        flat(w, need)
    return need


def merge(*gens):
    left = [[g, n, 0] for g, n in gens]
    while left:
        left.sort(key=lambda x: x[2] / x[1])
        try:
            next(left[0][0])
            left[0][2] += 1
        except StopIteration:
            left.pop(0)


def run(gen):
    for _ in gen:
        pass


def build(nc, T, out):
    top = ExitStack()
    with top:
        def sem(name):
            return top.enter_context(nc.semaphore(name))

        def sb(ctx, name, n, dt=F32, p=128):
            return ctx.enter_context(nc.sbuf_tensor(name, [p, n], dt))

        PE, DV, AC, PO, SP = [Queue(sem("s_" + n)) for n in ("pe", "dve", "act", "pool", "sp")]
        NDS = 32
        dsem = [sem(f"d{i}") for i in range(NDS)]
        dcount = [0] * NDS
        dnext = [0]
        drams = []

        def dma(q, o, i, *waits, store=False):
            k = dnext[0] % NDS
            dnext[0] += 1
            prev = (dsem[k], 16 * dcount[k]) if dcount[k] else None
            dcount[k] += 1
            q.items.append((flat([waits, prev], {}), lambda e: e.dma_start(o, i), dsem[k], 16))
            tok = (dsem[k], 16 * dcount[k])
            if store:
                drams.append(tok)
            return tok

        def so_far():
            return [q.now() for q in (PE, DV, AC, PO)] + [(dsem[k], 16 * dcount[k]) for k in range(NDS) if dcount[k]]

        def act(o, i, func, *w, bias=0.0, scale=1.0, acc=None):
            if acc is None:
                return AC.put(lambda e: e.activation(o, i, func, bias=bias, scale=scale), w)
            return AC.put(lambda e: e.activation(o, i, func, bias=bias, scale=scale, accum_out=acc), w)

        def copy_a(o, i, *w, scale=1.0):
            return act(o, i, ACT.Copy, *w, scale=scale)

        def copy_v(o, i, *w):
            return DV.put(lambda e: e.tensor_copy(o, i), w)

        def ts(o, i, s1, s2, op0, op1, *w, acc=None, q=None):
            q = q or DV
            if acc is not None:
                return q.put(lambda e: e.tensor_scalar(o, i, s1, s2, op0, op1, accum_out=acc), w)
            if op1 is None:
                return q.put(lambda e: e.tensor_scalar(o, i, s1, None, op0), w)
            return q.put(lambda e: e.tensor_scalar(o, i, s1, s2, op0, op1), w)

        def tt(o, a, b, op, *w, q=None):
            return (q or DV).put(lambda e: e.tensor_tensor(o, a, b, op), w)

        def stt(o, a, s, b, op0, op1, *w):
            return DV.put(lambda e: e.scalar_tensor_tensor(out=o, in0=a, scalar=s, in1=b, op0=op0, op1=op1), w)

        def ttr(o, a, b, scale, init, op0, op1, acc, *w):
            return DV.put(lambda e: e.tensor_tensor_reduce(out=o, in0=a, in1=b, scale=scale, scalar=init,
                                                           op0=op0, op1=op1, accum_out=acc), w)

        def mm(o, l, r, start, stop, *w, inc=False, skip=False):
            return PE.put(lambda e: e.matmul(o, l, r, start=start, stop=stop, skip_group_check=skip), w, inc)

        def tr(o, i, idn, *w, inc=False):
            return PE.put(lambda e: e.transpose(o, i, idn), w, inc)

        class Ring:

            def __init__(self, bufs, toks=None):
                self.bufs = bufs
                self.free = [(j, toks) for j in range(len(bufs))]

            def take(self):
                j, toks = self.free.pop(0)
                return j, self.bufs[j], toks

            def give(self, j, *toks):
                self.free.append((j, toks))

        banks = [top.enter_context(nc.psum_tensor(f"bank{i}", [128, 512], F32)) for i in range(8)]
        G = Ring(banks[0:3])
        L = Ring(banks[3:6])
        X = Ring(banks[6:8])

        con = sb(top, "con", C_END)
        t_con = dma(SP, con[:, :], T["consts"])
        idn = con[:, C_ID:C_ID + 128]
        negu = con[:, C_NU:C_NU + 128]
        neg1 = con[:, C_N1:C_N1 + 128]
        st = sb(top, "st", 512)
        xh, xl = sb(top, "xh", 8192, FR), sb(top, "xl", 8192, FR)

        raw = [sb(top, f"raw{i}", 1024) for i in range(NRAW)]
        wh = [sb(top, f"wh{i}", 1024, FR) for i in range(NU)]
        wl = [sb(top, f"wl{i}", 1024, FR) for i in range(NU)]
        rsem = [sem(f"r{i}") for i in range(NRAW)]

        def plan():
            for j in range(4):
                yield ("T", "w_in", j, 0)
            for c in (OFF_IQ, OFF_IQ + 128, OFF_IK):
                yield ("F", "w_in", c)
            for h in range(4):
                for m, o in enumerate((OFF_BQ, OFF_BK, OFF_BV)):
                    yield ("F", "w_in", o + 128 * h)
                    for j in range(4):
                        yield ("R", "w_cond_2", j, 512 * (3 * h + m))
            for h in range(2):
                for o in (OFF_CQ, OFF_CK, OFF_CV):
                    yield ("F", "w_in", o + 128 * h)
            for n in range(2):
                for j in range(4):
                    yield ("T", "w_out", j, 512 * n)
            for a, k in CHUNKS:
                for f in range(a, a + k):
                    yield ("F", "w_gu", 128 * f)
                    yield ("F", "w_gu", FF + 128 * f)
                for n in range(2):
                    for j in range(a // 2, (a + k) // 2):
                        yield ("T", "w_down", j, 512 * n)
            for n in range(2):
                for j in range(4):
                    yield ("T", "w_in_2", j, 1024 + 512 * n)
            for h in range(4):
                yield ("F", "w_in_2", 128 * h)
                yield ("F", "w_in_2", 512 + 128 * h)
            for n in range(2):
                for j in range(4):
                    yield ("T", "w_out_2", j, 512 * n)
            for a, k in CHUNKS:
                for f in range(a, a + k):
                    yield ("F", "w_gate_2", 128 * f)
                    yield ("F", "w_up_2", 128 * f)
                for n in range(2):
                    for j in range(a // 2, (a + k) // 2):
                        yield ("T", "w_down_2", j, 512 * n)

        keys = list(plan())
        raw_free = [None] * NRAW
        raw_tok = {}
        split_tok = {}
        raw_rel = set()
        rel = {}
        slot_of = {}
        at = {"dma": 0, "split": 0, "get": 0, "slots": 0}
        slot_prev = [None] * NU

        def pump():
            while True:
                moved = False
                m = at["dma"]
                if m < len(keys) and (m < NRAW or (m - NRAW) in raw_rel):
                    key = keys[m]
                    w = T[key[1]]
                    r = raw[m % NRAW]
                    if key[0] == "F":
                        dst = r[:, :].rearrange("p (k c) -> p k c", k=8)
                        wv = w.rearrange("(k p) c -> p k c", p=128)
                        if key[2] == OFF_IK and key[1] == "w_in":
                            pairs = [(dst[:, :, 32 * j:32 * j + 32], wv[:, :, key[2]:key[2] + 32]) for j in range(4)]
                        else:
                            pairs = [(dst, wv[:, :, key[2]:key[2] + 128])]
                    else:
                        dst = r[:, :].rearrange("p (k c) -> p k c", k=2)
                        wv = w[256 * key[2]:256 * key[2] + 256, key[3]:key[3] + 512]
                        pairs = [(dst, wv.rearrange("(k p) c -> p k c", p=128))]
                    toks = []
                    for j, (o, i) in enumerate(pairs):
                        if len(pairs) == 1:
                            cnt = at.get(m % NRAW, 0) + 16
                            at[m % NRAW] = cnt
                            SP.items.append((flat([raw_free[m % NRAW]], {}), lambda e, o=o, i=i: e.dma_start(o, i),
                                             rsem[m % NRAW], 16))
                            toks.append((rsem[m % NRAW], cnt))
                        else:
                            toks.append(dma(SP, o, i, raw_free[m % NRAW]))
                    raw_tok[m] = toks
                    at["dma"] += 1
                    moved = True
                m = at["split"]
                if m < len(keys) and m < at["dma"] and m <= at["get"] + NU:
                    if keys[m][0] == "R":
                        at["split"] += 1
                        moved = True
                    else:
                        s = at["slots"] % NU
                        if slot_prev[s] is None or slot_prev[s] in rel:
                            prev = rel.get(slot_prev[s])
                            r = raw[m % NRAW]
                            th = copy_a(wh[s][:, :], r[:, :], raw_tok[m], prev)
                            tl = tt(wl[s][:, :], r[:, :], wh[s][:, :].bitcast(F32), ALU.subtract, th, raw_tok[m], prev, q=PO)
                            raw_free[m % NRAW] = (th, tl)
                            raw_rel.add(m)
                            split_tok[m] = (th, tl)
                            slot_of[m] = s
                            slot_prev[s] = m
                            at["slots"] += 1
                            at["split"] += 1
                            moved = True
                if not moved:
                    return

        def get(*key):
            m = at["get"]
            assert keys[m] == key, (keys[m], key)
            at["get"] += 1
            pump()
            if key[0] == "R":
                return m, raw[m % NRAW], None, raw_tok[m]
            assert m in split_tok, key
            s = slot_of[m]
            return m, wh[s], wl[s], split_tok[m]

        def done(m, *toks):
            if keys[m][0] == "R":
                raw_free[m % NRAW] = toks
                raw_rel.add(m)
            else:
                rel[m] = toks
            pump()

        def gemm_f(u, xh, xl, t0, n, w):
            m, h, l, tok = u
            j, bank, fr = G.take()
            for k in range(8):
                a, b = h[:, 128 * k:128 * k + 128], l[:, 128 * k:128 * k + 128]
                xa, xb = xh[:, 1024 * k + t0:1024 * k + t0 + n], xl[:, 1024 * k + t0:1024 * k + t0 + n]
                mm(bank[:, 0:n], a, xa, k == 0, False, tok, w, fr)
                mm(bank[:, 0:n], a, xb, False, False)
                r = mm(bank[:, 0:n], b, xa, False, k == 7, inc=k == 7)
            return j, bank, r

        def gemm_t(us, xh, xl, tb, w, last=False):
            j, bank, fr = G.take()
            nk = 2 * len(us)
            for k in range(nk):
                m, h, l, tok = us[k // 2]
                c = 512 * (k % 2)
                o = 1024 * (k % 4 if isinstance(xh, list) else k) + 128 * tb
                ah, al = (xh[k // 4], xl[k // 4]) if isinstance(xh, list) else (xh, xl)
                xa, xb = ah[:, o:o + 128], al[:, o:o + 128]
                mm(bank[:, :], xa, h[:, c:c + 512], k == 0, False, tok, w, fr)
                mm(bank[:, :], xa, l[:, c:c + 512], False, False)
                free = k == nk - 1 or (last and k % 2 == 1)
                r = mm(bank[:, :], xb, h[:, c:c + 512], False, k == nk - 1, inc=free)
                if last and k % 2 == 1:
                    done(m, r)
            return j, bank, r

        def gemm_tf(u, xh, xl, tb, w):
            m, h, l, tok = u
            j, bank, fr = G.take()
            for k in range(8):
                o = 1024 * k + 128 * tb
                xa, xb = xh[:, o:o + 128], xl[:, o:o + 128]
                a, b = h[:, 128 * k:128 * k + 128], l[:, 128 * k:128 * k + 128]
                mm(bank[:, 0:128], xa, a, k == 0, False, tok, w, fr)
                mm(bank[:, 0:128], xa, b, False, False)
                r = mm(bank[:, 0:128], xb, a, False, k == 7, inc=k == 7)
            return j, bank, r

        def turn(src, tb, xh, xl, *w):
            last = None
            for half in range(2):
                j, bank, fr = X.take()
                for k in range(4):
                    c = 128 * (4 * half + k)
                    t = tr(bank[:, 128 * k:128 * k + 128], src[:, c:c + 128], idn, w, fr, t_con, inc=k == 3)
                v = bank[:, :].rearrange("p (k c) -> p k c", k=4)
                oh = xh[:, :].rearrange("p (k c) -> p k c", k=8)[:, 4 * half:4 * half + 4, 128 * tb:128 * tb + 128]
                ol = xl[:, :].rearrange("p (k c) -> p k c", k=8)[:, 4 * half:4 * half + 4, 128 * tb:128 * tb + 128]
                a = copy_a(oh, v, t)
                b = tt(ol, v, oh.bitcast(F32), ALU.subtract, a)
                X.give(j, b)
                last = b
            return last

        stn = [0]
        st_tok = {}

        def small(n):
            if stn[0] + n > 512:
                stn[0] = 0
            o = stn[0]
            stn[0] += n
            return st[:, o:o + n]

        bns = sb(top, "bns", 24)

        def mean_rstd(src, eps, *w):
            mv, r = small(2), small(2)
            a = DV.put(lambda e: e.bn_stats(bns[:, 0:6], src[:, 0:512]), w)
            b = DV.put(lambda e: e.bn_stats(bns[:, 6:12], src[:, 512:1024]), w)
            c = DV.put(lambda e: e.bn_aggr(mv, bns[:, 0:12]), (a, b))
            d = ts(r[:, 0:1], mv[:, 1:2], eps, None, ALU.add, None, c)
            f = act(r[:, 1:2], r[:, 0:1], ACT.Sqrt, d)
            g = DV.put(lambda e: e.reciprocal(r[:, 0:1], r[:, 1:2]), (f,))
            return mv[:, 0:1], r[:, 0:1], g

        def rms(src, eps, junk, *w):
            ss, r = small(1), small(2)
            a = act(junk, src, ACT.Square, w, acc=ss)
            b = ts(r[:, 0:1], ss, 1.0 / 1024, eps, ALU.mult, ALU.add, a)
            f = act(r[:, 1:2], r[:, 0:1], ACT.Sqrt, b)
            g = DV.put(lambda e: e.reciprocal(r[:, 0:1], r[:, 1:2]), (f,))
            return r[:, 0:1], g, a

        mix_d, x2_d = T["mix_d"], T["x2_d"]
        xd = T["x"]

        ph = ExitStack()
        score = sb(ph, "score", 4224)
        cols = {}
        o = 0
        for i in range(2, 8):
            cols[i] = (o, 128 * (i + 1))
            o += 128 * (i + 1)
        V = Ring([sb(ph, f"vals{i}", 1024) for i in range(4)])
        cand = sb(ph, "cand", 64)
        nd = sb(ph, "nd", 1024)
        hbuf = sb(ph, "hbuf", 6144)
        cc = sb(ph, "cc", 8)
        mrow = [sb(ph, f"mrow{i}", 512, p=1) for i in range(2)]
        mixw = {}

        t_x = [None] * 8
        for tb in range(8):
            j, buf, fr = V.take()
            d = dma(SP, buf[:, :], xd[128 * tb:128 * tb + 128, :], fr)
            t_x[tb] = turn(buf, tb, xh, xl, d)
            V.give(j, t_x[tb], PE.now())
            if tb == 3:
                pump()
        t_nd = dma(SP, nd[:, :], T["dist"])

        d2 = dma(SP, score[0:8, 0:128], T["c_2"].rearrange("(k p) -> k p", p=128))
        j, bank, fr = X.take()
        t = tr(bank[:, 0:8], score[0:8, 0:128], idn[0:8, 0:8], d2, fr, t_con, inc=True)
        t_cc = act(cc[:, :], bank[:, 0:8], ACT.Silu, t)
        X.give(j, t_cc)
        mod_free = [None, None]
        mod_w = []

        def modulate(n):
            row = mrow[n % 2]
            d = dma(SP, row[:, :], T["b_cond_2"][512 * n:512 * n + 512].unsqueeze(0), mod_free[n % 2])
            j, bank, fr = G.take()
            for q in range(4):
                u = get("R", "w_cond_2", q, 512 * n)
                for k in range(2):
                    r = mm(bank[0:1, :], cc[:, 2 * q + k:2 * q + k + 1], u[1][:, 512 * k:512 * k + 512],
                           q == 0 and k == 0, q == 3 and k == 1, u[3], t_cc, fr, inc=k == 1)
                done(u[0], r)
                if q < 3:
                    yield
            e = tt(row[:, :], bank[0:1, :], row[:, :], ALU.add, r, d)
            G.give(j, e)
            mod_free[n % 2] = dma(SP, T["vec_d"][0:1, 512 * n:512 * n + 512], row[:, :], e, store=True)
            mod_w.append(mod_free[n % 2])
            yield

        au, av = hbuf[:, 0:2048], hbuf[:, 2048:4096]
        wst, lng, tmp = hbuf[:, 4096:4608], hbuf[:, 4608:5120], hbuf[:, 5120:5632]
        bsc, gst = hbuf[:, 5632:5640], hbuf[:, 5640:5768]
        b4 = hbuf[0:4, 5768:5896]
        t_g = [dma(SP, lng[:, 0:256], T["gmlp_ln_g"].rearrange("a b -> (a b)").partition_broadcast(128)),
               dma(SP, lng[:, 256:512], T["gmlp_ln_b"].rearrange("a b -> (a b)").partition_broadcast(128))]
        t_ws = dma(SP, tmp.rearrange("p (g s) -> p g s", g=4), T["gmlp_w_s"].rearrange("g t s -> t g s"))
        t_b4 = dma(SP, b4, T["gmlp_b_s"])
        j, bank, fr = X.take()
        for g in range(4):
            t = tr(bank[:, 128 * g:128 * g + 128], tmp[:, 128 * g:128 * g + 128], idn, t_ws, fr, inc=g == 3)
        e1 = copy_v(wst, bank[:, :], t)
        X.give(j, e1)
        wv = wst[64:128, :].rearrange("p (g s) -> p g s", g=4)[:, :, 0:64]
        e1 = DV.put(lambda e: e.memset(wv, 0.0), (e1,))
        j, bank, fr = X.take()
        t = tr(bank[:, 0:4], b4, idn[0:4, 0:4], t_b4, fr, inc=True)
        e2 = copy_v(bsc[:, 0:4], bank[:, 0:4], t)
        X.give(j, e2)
        us = [get("T", "w_in", j, 0) for j in range(4)]
        t_ge = {}
        for tb in range(8):
            j, bank, r = gemm_t(us, xh, xl, tb, t_x[tb], last=tb == 7)
            a = act(au[:, 256 * tb:256 * tb + 256], bank[:, 0:256], ACT.Gelu_apprx_tanh, r)
            b = act(av[:, 256 * tb:256 * tb + 256], bank[:, 256:512], ACT.Gelu_apprx_tanh, r)
            G.give(j, a, b)
            t_ge["u", tb], t_ge["v", tb] = a, b
        last = []

        def gmlp_norm():
            prev = None
            for q in range(4):
                flat_v = av[:, 512 * q:512 * q + 512]
                vq = flat_v.rearrange("p (n c) -> p n c", c=64)
                s8 = gst[:, 8 * q:8 * q + 8]
                a = DV.put(lambda e, vq=vq, s8=s8: e.tensor_reduce(s8, vq, AX.X, ALU.add), (t_ge["v", 2 * q], t_ge["v", 2 * q + 1]))
                b = ts(s8, s8, 1.0 / 64, None, ALU.mult, None, a)
                c = tt(vq, vq, s8.unsqueeze(2).broadcast_to([128, 8, 64]), ALU.subtract, b)
                d = tt(tmp, flat_v, flat_v, ALU.mult, c, e1, prev)
                yield
                v8 = gst[:, 32 + 8 * q:40 + 8 * q]
                f = DV.put(lambda e, v8=v8: e.tensor_reduce(v8, tmp.rearrange("p (n c) -> p n c", c=64), AX.X, ALU.add), (d,))
                g = ts(v8, v8, 1.0 / 64, LN_EPS, ALU.mult, ALU.add, f)
                h = act(gst[:, 64 + 8 * q:72 + 8 * q], v8, ACT.Sqrt, g)
                r8 = gst[:, 96 + 8 * q:104 + 8 * q]
                k = DV.put(lambda e, q=q, r8=r8: e.reciprocal(r8, gst[:, 64 + 8 * q:72 + 8 * q]), (h,))
                m = tt(vq, vq, r8.unsqueeze(2).broadcast_to([128, 8, 64]), ALU.mult, k)
                v2 = flat_v.rearrange("p (n c) -> p n c", c=256)
                m = tt(v2, v2, lng[:, 0:256].unsqueeze(1).broadcast_to([128, 2, 256]), ALU.mult, m, t_g)
                m = tt(v2, v2, lng[:, 256:512].unsqueeze(1).broadcast_to([128, 2, 256]), ALU.add, m, t_g)
                prev = m
                last.append(m)
                yield

        sub = ExitStack()
        iq, ik, iw = sb(sub, "iq", 2048), sb(sub, "ik", 1024), sb(sub, "iw", 64)
        wih, wil, wir = sb(sub, "wih", 64, FR), sb(sub, "wil", 64, FR), sb(sub, "wir", 64)
        t_iq, t_iw = [], []

        def index_proj():
            t_w = dma(SP, wir[:, :].rearrange("p (k c) -> p k c", k=8),
                      T["w_in"].rearrange("(k p) c -> p k c", p=128)[:, :, OFF_IW:OFF_IW + 8])
            th = copy_a(wih[:, :], wir[:, :], t_w)
            tl = tt(wil[:, :], wir[:, :], wih[:, :].bitcast(F32), ALU.subtract, th)
            for n, c in enumerate((OFF_IQ, OFF_IQ + 128, OFF_IK)):
                u = get("F", "w_in", c)
                for half in range(2):
                    j, bank, r = gemm_f(u, xh, xl, 512 * half, 512, t_x)
                    dst = iq[:, 1024 * n + 512 * half:1024 * n + 512 * half + 512] if n < 2 else ik[:, 512 * half:512 * half + 512]
                    e = copy_a(dst, bank[:, :], r)
                    G.give(j, e)
                    t_iq.append(e)
                    yield
                done(u[0], r)
            for tb in range(8):
                j, bank, fr = G.take()
                for k in range(8):
                    o = 1024 * k + 128 * tb
                    mm(bank[:, 0:8], xh[:, o:o + 128], wih[:, 8 * k:8 * k + 8], k == 0, False, th, tl, fr)
                    mm(bank[:, 0:8], xh[:, o:o + 128], wil[:, 8 * k:8 * k + 8], False, False)
                    r = mm(bank[:, 0:8], xl[:, o:o + 128], wih[:, 8 * k:8 * k + 8], False, k == 7, inc=k == 7)
                e = ts(iw[:, 8 * tb:8 * tb + 8], bank[:, 0:8], 1.0 / 16, None, ALU.mult, None, r)
                G.give(j, e)
                t_iw.append(e)
                yield

        merge((gmlp_norm(), 8), (index_proj(), 14))
        t_oa = []
        for g in range(4):
            j, bank, fr = L.take()
            mv = av.rearrange("p (n g c) -> p n g c", g=4, c=64)[:, :, g, :]
            r = mm(bank[:, :].rearrange("p (n c) -> p n c", n=8), wst[:, 128 * g:128 * g + 128], mv, True, True,
                   fr, last, e1, inc=True)
            uv = au.rearrange("p (n g c) -> p n g c", g=4, c=64)[:, :, g, :]
            e = stt(uv, bank[:, :].rearrange("p (n c) -> p n c", n=8), bsc[:, g:g + 1], uv, ALU.add, ALU.mult,
                    r, e2, [t_ge["u", q] for q in range(8)])
            L.give(j, e)
            t_oa.append(e)
        for tb in range(8):
            mixw[tb, "a"] = dma(SP, mix_d[128 * tb:128 * tb + 128, 0:256], au[:, 256 * tb:256 * tb + 256], t_oa, store=True)
        hq = [[hbuf[:, 1024 * (3 * i + x):1024 * (3 * i + x) + 1024] for x in range(3)] for i in range(2)]
        gdone = (t_oa, r, [mixw[tb, "a"] for tb in range(8)])
        hfree = [gdone, gdone]

        t_score = {}

        def scores():
            for i in range(2, 8):
                o, ln = cols[i]
                for c0 in range(0, ln, 512):
                    n = min(512, ln - c0)
                    prev = None
                    for h in range(8):
                        j, bank, fr = L.take()
                        pr = slice(32 * (h % 4), 32 * (h % 4) + 32)
                        q = iq[pr, 1024 * (h // 4) + 128 * i:1024 * (h // 4) + 128 * i + 128]
                        r = mm(bank[:, 0:n], q, ik[pr, c0:c0 + n], True, True, fr, t_iq, inc=True)
                        jv, vb, vf = V.take()
                        a = act(vb[:, 0:n], bank[:, 0:n], ACT.Relu, r, vf)
                        L.give(j, a)
                        dst = score[:, o + c0:o + c0 + n]
                        w8 = iw[:, 8 * i + h:8 * i + h + 1]
                        if h == 0:
                            prev = ts(dst, vb[:, 0:n], w8, None, ALU.mult, None, a, t_iw)
                        else:
                            prev = stt(dst, vb[:, 0:n], w8, dst, ALU.mult, ALU.add, a, prev)
                        V.give(jv, prev)
                        yield
                t_score[i] = DV.put(lambda e, o=o, ln=ln: e.memset(score[0:64, o + ln - 64:o + ln], -BIG), (prev,))

        def project(n, off, h, scale, xw):
            q, k, v = hq[n % 2]
            toks = []
            cond = n < 4
            for m, (dst, o) in enumerate(((q, off[0]), (k, off[1]))):
                u = get("F", "w_in", o + 128 * h)
                for half in range(2):
                    j, bank, r = gemm_f(u, xh, xl, 512 * half, 512, xw)
                    d = dst[:, 512 * half:512 * half + 512]
                    if m == 0 and not isinstance(scale, float):
                        e = ts(d, bank[:, :], scale, None, ALU.mult, None, r, hfree[n % 2])
                    else:
                        e = copy_a(d, bank[:, :], r, hfree[n % 2], scale=scale if m == 0 else 1.0)
                    G.give(j, e)
                    toks.append(e)
                    yield
                done(u[0], r)
                if cond:
                    yield from modulate(3 * n + m)
            u = get("F", "w_in", off[2] + 128 * h)
            for tb in range(8):
                j, bank, r = gemm_tf(u, xh, xl, tb, xw)
                e = copy_a(v[:, 128 * tb:128 * tb + 128], bank[:, 0:128], r, hfree[n % 2])
                G.give(j, e)
                toks.append(e)
                yield
            done(u[0], r)
            if cond:
                yield from modulate(3 * n + 2)
            ready[n] = toks
            last_proj[0] = r

        last_proj = [None]
        ready = {}
        B_OFF, C_OFF = (OFF_BQ, OFF_BK, OFF_BV), (OFF_CQ, OFF_CK, OFF_CV)
        projects = [project(h, B_OFF, h, 2.0 ** (2 * (h + 1) - 3), t_x) for h in range(4)]
        projects += [project(4 + h, C_OFF, h, con[:, C_Q + h:C_Q + h + 1], t_x) for h in range(2)]
        merge((scores(), 108), (projects[0], 24))
        snap = so_far()
        sub.close()

        sub = ExitStack()
        PT = Ring([sb(sub, f"pt{i}", 1024) for i in range(2)], snap)
        osb = sb(sub, "osb", 1024)
        tcum = sb(sub, "tcum", 1024)
        tj = sb(sub, "tj", 1024, BF)
        sg = sb(sub, "sg", 128)
        lamt = sb(sub, "lamt", 264)
        t_sg = dma(SP, sg[:, :], T["diff_subln_g"].partition_broadcast(128), snap)
        t_l = [dma(SP, lamt[:, 64 * n:64 * n + 64], T[nm].partition_broadcast(128), snap)
               for n, nm in enumerate(("lam_q1", "lam_k1", "lam_q2", "lam_k2"))]
        a = ttr(lamt[:, 0:64], lamt[:, 0:64], lamt[:, 64:128], 1.0, 0.0, ALU.mult, ALU.add, lamt[:, 256:257], t_l)
        b = ttr(lamt[:, 128:192], lamt[:, 128:192], lamt[:, 192:256], 1.0, 0.0, ALU.mult, ALU.add, lamt[:, 257:258], t_l)
        c = act(lamt[:, 258:260], lamt[:, 256:258], ACT.Exp, a, b)
        d = tt(lamt[:, 260:261], lamt[:, 259:260], lamt[:, 258:259], ALU.subtract, c)
        t_lam = ts(lamt[:, 261:262], lamt[:, 260:261], -LAM_INIT, None, ALU.add, None, d)
        nlam = lamt[:, 261:262]

        def softmax(i, q, k, bias, slope, w, wb):
            ln = 128 * (i + 1)
            jv, vb, vf = V.take()
            mx = small(4)
            prev = None
            for c0 in range(0, ln, 512):
                n = min(512, ln - c0)
                j, bank, fr = L.take()
                r = mm(bank[:, 0:n], q[:, 128 * i:128 * i + 128], k[:, c0:c0 + n], True, True, fr, w, inc=True)
                z = c0 // 512
                prev = ttr(vb[:, c0:c0 + n], bank[:, 0:n], bias[:, c0:c0 + n], 1.0, -3.0e38 if z == 0 else mx[:, 0:1],
                           ALU.add, ALU.max, mx[:, z:z + 1], r, vf, prev, wb)
                L.give(j, prev)
            m = mx[:, z:z + 1]
            nb = ts(mx[:, 2:3], m, -slope, None, ALU.mult, None, prev)
            e = act(vb[:, 0:ln], vb[:, 0:ln], ACT.Exp, nb, prev, bias=mx[:, 2:3], scale=slope, acc=mx[:, 3:4])
            rc = small(1)
            t = DV.put(lambda en: en.reciprocal(rc, mx[:, 3:4]), (e,))
            return jv, vb, e, rc, t

        def weigh(i, vb, v, vw, w, cols_v, obuf, scale, wo):
            jp, pb, pf = PT.take()
            toks = []
            for c0 in range(0, i + 1, 4):
                m = min(4, i + 1 - c0)
                j, bank, fr = X.take()
                for b in range(m):
                    t = tr(bank[:, 128 * b:128 * b + 128], vb[:, 128 * (c0 + b):128 * (c0 + b) + 128], idn, w, fr, inc=b == m - 1)
                e = copy_a(pb[:, 128 * c0:128 * (c0 + m)], bank[:, 0:128 * m], t, pf)
                X.give(j, e)
                toks.append(e)
            tlast = t
            j, bank, fr = X.take()
            nv = cols_v[1] - cols_v[0]
            for b in range(i + 1):
                r = mm(bank[:, 0:nv], pb[:, 128 * b:128 * b + 128], v[:, 128 * b + cols_v[0]:128 * b + cols_v[1]],
                       b == 0, b == i, toks, vw, fr, inc=b == i)
            PT.give(jp, r)
            if scale is None:
                e = copy_v(obuf, bank[:, 0:nv], r, wo)
            else:
                e = ts(obuf, bank[:, 0:nv], scale, None, ALU.mult, None, r, wo)
            X.give(j, e)
            return tlast, e, r

        ofree = [snap] * 8

        def attend_b():
            pend = None
            for h in range(4):
                q, k, v = hq[h % 2]
                w = ready[h]
                slope = 2.0 ** (-2 * (h + 1))
                nxt = projects[h + 1]
                for i in range(8):
                    bias = nd[:, 896 - 128 * i:1024]
                    ln = 128 * (i + 1)
                    a = softmax(i, q[0:64, :], k[0:64, :], bias, slope, w, t_nd)
                    if i:
                        next(nxt, None)
                    yield
                    b = softmax(i, q[64:128, :], k[64:128, :], bias, slope, w, t_nd)
                    c2 = small(1)
                    t2 = tt(c2, b[3], nlam, ALU.mult, b[4], t_lam)
                    t3 = ts(a[1][:, 0:ln], a[1][:, 0:ln], a[3], None, ALU.mult, None, a[2], a[4])
                    t4 = stt(a[1][:, 0:ln], b[1][:, 0:ln], c2, a[1][:, 0:ln], ALU.mult, ALU.add, t3, t2, b[2])
                    V.give(b[0], t4)
                    if i:
                        next(nxt, None)
                    yield
                    if pend:
                        finish_b(*pend)
                        next(nxt, None)
                        yield
                    pend = (h, i, a, v, w, t4)
                run(nxt)
            finish_b(*pend)

        oe = []

        def finish_b(h, i, a, v, w, t4):
            tlast, e, r = weigh(i, a[1], v, w, t4, (0, 128), osb[:, 128 * i:128 * i + 128], None, ofree[i])
            V.give(a[0], tlast)
            oe.append(e)
            if i < 7:
                return
            hfree[h % 2] = (r,)
            ss = small(24)
            jv, vb, vf = V.take()
            d = tt(vb[:, :], osb[:, :], osb[:, :], ALU.mult, oe, vf)
            d = DV.put(lambda en: en.tensor_reduce(ss[:, 0:8], vb[:, :].rearrange("p (n c) -> p n c", n=8), AX.X, ALU.add), (d,))
            V.give(jv, d)
            d = ts(ss[:, 0:8], ss[:, 0:8], 1.0 / 128, LN_EPS, ALU.mult, ALU.add, d)
            d = act(ss[:, 8:16], ss[:, 0:8], ACT.Sqrt, d)
            d = DV.put(lambda en: en.reciprocal(ss[:, 16:24], ss[:, 8:16]), (d,))
            d = ts(ss[:, 16:24], ss[:, 16:24], 1.0 - LAM_INIT, None, ALU.mult, None, d)
            for i in range(8):
                ob = osb[:, 128 * i:128 * i + 128]
                e = stt(ob, ob, ss[:, 16 + i:17 + i], sg[:, :], ALU.mult, ALU.mult, d, t_sg)
                mixw[i, h] = dma(SP, mix_d[128 * i:128 * i + 128, 256 + 128 * h:384 + 128 * h], ob, e, store=True)
                ofree[i] = mixw[i, h]
            oe.clear()

        t_sel = {}

        def topk():
            cu, ci = cand[:, 0:6].bitcast(U32), cand[:, 0:6].bitcast(I32)
            cnt = cand[:, 8:14]
            rj = cand[:, 16:22]
            tmp6 = cand[:, 24:30]
            junk = tj

            def count(thr, waits, op=ALU.is_ge):
                ts_ = []
                for n, i in enumerate(range(2, 8)):
                    o, ln = cols[i]
                    t1 = thr if isinstance(thr, float) else thr[:, n:n + 1]
                    ts_.append(ts(junk[:, 0:ln], score[:, o:o + ln], t1, 0.0, op, ALU.add, waits, t_score[i], snap,
                                  ts_[-1] if ts_ else None, acc=cnt[:, n:n + 1]))
                return ts_

            c = count(0.0, None)
            yield
            p = ts(ci, cnt, 256.0, -1.0, ALU.is_lt, ALU.mult, c)
            p = ts(cu, cu, 1 << 30, None, ALU.bitwise_xor, None, p)
            for b in range(30, -1, -1):
                c = count(cand[:, 0:6], (p,))
                yield
                r = ts(rj.bitcast(U32), cnt, 256.0, float(2 ** b), ALU.is_lt, ALU.mult, c)
                if b:
                    p = tt(cu, cu, rj.bitcast(U32), ALU.bitwise_xor, r)
                    p = ts(cu, cu, 1 << (b - 1), None, ALU.bitwise_xor, None, p)
                else:
                    p = tt(cu, cu, rj.bitcast(U32), ALU.bitwise_xor, r)
                yield
            c = count(cand[:, 0:6], (p,), ALU.is_gt)
            need = ts(tmp6, cnt, -1.0, 256.0, ALU.mult, ALU.add, c)
            cum, cf = tcum, snap
            prev = None
            for n, i in enumerate(range(2, 8)):
                o, ln = cols[i]
                sc = score[:, o:o + ln]
                thr = cand[:, n:n + 1]
                a = ts(junk[:, 0:ln], sc, thr, None, ALU.is_equal, None, p, need, prev)
                b = DV.put(lambda e, ln=ln: e.tensor_tensor_scan(cum[:, 0:ln], junk[:, 0:ln], junk[:, 0:ln], 0.0,
                                                                 ALU.add, ALU.bypass), (a, cf, prev))
                d = stt(junk[:, 0:ln], cum[:, 0:ln], tmp6[:, n:n + 1], junk[:, 0:ln], ALU.is_le, ALU.mult, b)
                f = stt(sc, sc, thr, junk[:, 0:ln], ALU.is_gt, ALU.add, d)
                g = ts(sc, sc, -1.0, BIG, ALU.add, ALU.mult, f)
                prev = tt(sc, sc, nd[:, 896 - 128 * i:1024], ALU.add, g, t_nd)
                t_sel[i] = prev
                yield

        t_mix = [None] * 8

        def attend_c():
            pend = []
            turns = []
            for pair in range(2):
                n = 4 + pair
                q, k, v = hq[n % 2]
                w = ready[n]
                for i in range(8):
                    bias = nd[:, 896 - 128 * i:1024] if i < 2 else score[:, cols[i][0]:cols[i][0] + cols[i][1]]
                    for hh in range(2):
                        slope = 2.0 ** (-2 * (2 * pair + hh + 1))
                        pr = slice(64 * hh, 64 * hh + 64)
                        a = softmax(i, q[pr, :], k[pr, :], bias, slope, w, t_sel.get(i, t_nd))
                        pend.append((pair, i, hh, a, v, w))
                        yield
                        if len(pend) > 1:
                            finish_c(turns, *pend.pop(0))
                            yield
                            if len(turns) > 1:
                                turn_mix(*turns.pop(0))
                                yield
            for p in pend:
                finish_c(turns, *p)
                yield
            for p in turns:
                turn_mix(*p)
                yield

        def finish_c(turns, pair, i, hh, a, v, w):
            tlast, e, r = weigh(i, a[1], v, w, a[2], (64 * hh, 64 * hh + 64),
                                osb[:, 128 * i + 64 * hh:128 * i + 64 * hh + 64], a[3], (ofree[i], a[4]))
            V.give(a[0], tlast)
            oe.append(e)
            if hh:
                mixw[i, "c", pair] = dma(SP, mix_d[128 * i:128 * i + 128, 768 + 128 * pair:896 + 128 * pair],
                                         osb[:, 128 * i:128 * i + 128], oe, store=True)
                ofree[i] = mixw[i, "c", pair]
                oe.clear()
                if pair:
                    j, buf, fr = V.take()
                    d = dma(SP, buf[:, :], mix_d[128 * i:128 * i + 128, :], fr, [x for key, x in mixw.items() if key[0] == i])
                    turns.append((i, j, buf, d))

        def turn_mix(i, j, buf, d):
            t_mix[i] = turn(buf, i, xh, xl, d, last_proj[0])
            V.give(j, t_mix[i], PE.now())

        merge((attend_b(), 96), (topk(), 70))
        c = attend_c()
        for k, _ in enumerate(c):
            if k % 2 == 0:
                next(projects[5], None)
            if k == 28:
                run(projects[5])
        snap = so_far()
        sub.close()
        ph.close()

        G = Ring(banks[0:5], snap)
        X = Ring(banks[5:8], snap)

        def bc(ctx, name, src, *w):
            t = sb(ctx, name, 1024)
            return t, dma(SP, t[:, :], src.partition_broadcast(128), *w)

        def mix_gemm(wname, tw, finish, after):
            for n in range(2):
                us = [get("T", wname, j, 512 * n) for j in range(4)]
                for tb in range(8):
                    j, bank, r = gemm_t(us, xh, xl, tb, tw[tb], last=tb == 7)
                    G.give(j, finish(tb, n, bank, r))
                    if n == 1:
                        after(tb, r)
            after(8, None)

        def ffn(wg, wu, up_off, wd, tw, acc, acc_tok, snap, fresh, between, after):
            sa, sc_ = ExitStack(), ExitStack()
            sil = [sb(sa, f"sil{i}" + wg, 512) for i in range(2)]
            SR = Ring(sil, snap)
            hh, hl = [sb(sa, "hh" + wg, 4096, FR)], [sb(sa, "hl" + wg, 4096, FR)]
            hh.append(sb(sc_, "hi" + wg, 2048, FR))
            hl.append(sb(sc_, "hm" + wg, 2048, FR))
            hfr = snap
            for a, kk in CHUNKS:
                if a == CHUNKS[-1][0]:
                    sc_.close()
                    between(sa, so_far())
                ht = []
                for f in range(a, a + kk):
                    ug = get("F", wg, 128 * f)
                    uu = get("F", wu, up_off + 128 * f)
                    for half in range(2):
                        w = tw[4 * half:4 * half + 4]
                        jg, bg, rg = gemm_f(ug, xh, xl, 512 * half, 512, w)
                        ju, bu, ru = gemm_f(uu, xh, xl, 512 * half, 512, w)
                        s, sbuf, sf = SR.take()
                        e = act(sbuf[:, :], bg[:, :], ACT.Silu, rg, sf)
                        G.give(jg, e)
                        m = tt(sbuf[:, :], sbuf[:, :], bu[:, :], ALU.mult, e, ru)
                        G.give(ju, m)
                        p = (f - a) // 4
                        o = 1024 * ((f - a) % 4) + 512 * half
                        c = copy_a(hh[p][:, o:o + 512], sbuf[:, :], m, hfr)
                        d = tt(hl[p][:, o:o + 512], sbuf[:, :], hh[p][:, o:o + 512].bitcast(F32), ALU.subtract, c, hfr)
                        SR.give(s, d)
                        ht.append((c, d))
                    done(ug[0], rg)
                    done(uu[0], ru)
                fdone = ru
                for n in range(2):
                    us = [get("T", wd, j, 512 * n) for j in range(a // 2, (a + kk) // 2)]
                    for tb in range(8):
                        j, bank, r = gemm_t(us, hh, hl, tb, ht, last=tb == 7)
                        dst = acc[:, 1024 * tb + 512 * n:1024 * tb + 512 * n + 512]
                        if fresh and a == 0:
                            e = copy_v(dst, bank[:, :], r, acc_tok[tb])
                        else:
                            e = tt(dst, bank[:, :], dst, ALU.add, r, acc_tok[tb])
                        acc_tok[tb] = (acc_tok[tb], e)
                        G.give(j, e)
                        if n == 1 and a == CHUNKS[-1][0]:
                            after(tb, fdone)
                hfr = (r,)
            after(8, None)
            return sa

        def dump(buf, toks):
            for tb in range(8):
                dma(SP, out[128 * tb:128 * tb + 128, :], buf[:, 1024 * tb:1024 * tb + 1024], toks, store=True)

        ph = ExitStack()
        res = sb(ph, "res", 8192)

        def block(tb):
            return res[:, 1024 * tb:1024 * tb + 1024]

        sub = ExitStack()
        g1, tg1 = bc(sub, "g1", T["ln1_g"], snap)
        b1, tb1 = bc(sub, "b1", T["ln1_b"], snap)
        t_r = [dma(SP, block(tb), xd[128 * tb:128 * tb + 128, :], snap) for tb in range(8)]

        def fin1(tb, n, bank, r):
            dst = block(tb)[:, 512 * n:512 * n + 512]
            e = stt(dst, dst, ALPHA, bank[:, :], ALU.mult, ALU.add, r, t_r[tb])
            t_r[tb] = (t_r[tb], e)
            return e

        ty = [None] * 8
        late = []

        def norm1(tb, r):
            if late:
                b, t, pe = late.pop()
                ty[b] = turn(block(b), b, xh, xl, t, pe)
                t_r[b] = ts(block(b), block(b), ALPHA, None, ALU.mult, None, PE.now(), t)
            if tb < 8:
                src = block(tb)
                mu, rs, t = mean_rstd(src, LN_EPS, t_r[tb])
                t = ts(src, src, mu, rs, ALU.subtract, ALU.mult, t)
                t = tt(src, src, g1[:, :], ALU.mult, t, tg1)
                t = tt(src, src, b1[:, :], ALU.add, t, tb1)
                late.append((tb, t, r))

        mix_gemm("w_out", t_mix, fin1, norm1)
        snap = so_far()
        sub.close()

        vec = {}

        def row(name, dst, n, *w):
            return dma(SP, dst, T["vec_d"][0, 1024 * n:1024 * n + 1024].partition_broadcast(128), mod_w, *w)

        def vectors2(ctx, snap):
            g2, t2 = bc(ctx, "g2", T["ln2_g"], snap)
            b2, t3 = bc(ctx, "b2", T["ln2_b"], snap)
            gp, t4 = bc(ctx, "gp", T["g_mix_pre_2"], snap)
            sh = sb(ctx, "sh", 1024)
            t5 = row("scale", sh[:, :], 1, snap)
            t6 = stt(gp[:, :], sh[:, :], 1.0, gp[:, :], ALU.add, ALU.mult, t4, t5)
            t7 = row("shift", sh[:, :], 0, t6)
            vec["2"] = (g2, b2, gp, sh, t2, t3, t6, t7)
            vec["junk"] = [sb(ctx, "sq2", 1024, BF), None]

        t_h = [None] * 8
        t_x2 = []

        def norm2(tb, r):
            g2, b2, gp, sh, t2, t3, t6, t7 = vec["2"]
            if late:
                b, t = late.pop()
                t_h[b] = turn(block(b), b, xh, xl, t, pe2[0])
            if tb < 8:
                pe2[0] = r
                src = block(tb)
                mu, rs, t = mean_rstd(src, LN_EPS, t_r[tb])
                t = ts(src, src, mu, rs, ALU.subtract, ALU.mult, t)
                t = tt(src, src, g2[:, :], ALU.mult, t, t2)
                t = tt(src, src, b2[:, :], ALU.add, t, t3)
                d = dma(SP, x2_d[128 * tb:128 * tb + 128, :], src, t, store=True)
                t_x2.append(d)
                rr, t, vec["junk"][1] = rms(src, EPS, vec["junk"][0][:, :], t, vec["junk"][1])
                t = stt(src, src, rr, gp[:, :], ALU.mult, ALU.mult, t, t6, d)
                t = tt(src, src, sh[:, :], ALU.add, t, t7)
                late.append((tb, t))

        pe2 = [None]
        late.clear()
        sa = ffn("w_gu", "w_gu", FF, "w_down", ty, res, t_r, snap, False, vectors2, norm2)
        snap = so_far()
        sa.close()
        turned = PE.now()

        sub = ExitStack()
        vt = sb(sub, "vt", 4096)
        sq = ExitStack()
        ut = sb(sq, "ut", 4096)
        bd = sb(sq, "bd", 1536)
        wp = sb(sq, "wp", 512)
        pl = [sb(sq, f"pl{i}", 1024) for i in range(2)]
        ps = sb(sq, "ps", 8)
        ps4 = sb(sq, "ps4", 128, p=4)
        t_bd = dma(SP, bd[:, :], T["bands"], snap)
        t_wp = dma(SP, wp[:, :].rearrange("p (g d) -> p g d", g=4), T["w_pool_2"].rearrange("g c d -> c g d"), snap)
        d = dma(SP, ps4[:, :], T["pool_scale_2"].rearrange("(g p) -> g p", p=128), snap)
        tv, tu = [], []
        for n, (dst, toks) in enumerate(((vt, tv), (ut, tu))):
            us = [get("T", "w_in_2", j, 1024 + 512 * n) for j in range(4)]
            for tb in range(8):
                j, bank, r = gemm_t(us, xh, xl, tb, t_h[tb], last=tb == 7)
                e = copy_a(dst[:, 512 * tb:512 * tb + 512], bank[:, :], r, snap)
                G.give(j, e)
                toks.append(e)
        j, bank, fr = X.take()
        t = tr(bank[:, 0:4], ps4[:, :], idn[0:4, 0:4], d, fr, inc=True)
        t_ps = copy_v(ps[:, 0:4], bank[:, 0:4], t, snap)
        X.give(j, t_ps)
        snap_v = snap
        plf = [snap, snap]
        t_pool = {}

        def pooling():
            for g in range(4):
                p_ = pl[g % 2]
                te = []
                for c in range(2):
                    j, bank, fr = X.take()
                    for b in range(4 * c, 4 * c + 4):
                        o = bank[:, 128 * (b % 4):128 * (b % 4) + 128]
                        ub = ut[:, 512 * b + 128 * g:512 * b + 128 * g + 128]
                        band = bd[:, 384 * g:384 * g + 384]
                        if b == 0:
                            r = mm(o, ub, band[:, 256:384], True, True, tu, t_bd, fr, inc=True)
                        else:
                            up = ut[:, 512 * (b - 1) + 128 * g:512 * (b - 1) + 128 * g + 128]
                            mm(o, ub, band[:, 0:128], True, False, tu, t_bd, fr)
                            r = mm(o, up, band[:, 128:256], False, True, inc=True)
                    e = copy_v(p_[:, 512 * c:512 * c + 512], bank[:, :], r, plf[g % 2])
                    X.give(j, e)
                    te.append(e)
                    yield
                for c in range(2):
                    j, bank, fr = X.take()
                    r = mm(bank[:, :], wp[:, 128 * g:128 * g + 128], p_[:, 512 * c:512 * c + 512], True, True,
                           te, t_wp, fr, inc=True)
                    o = 1024 * (4 + g) + 512 * c
                    e = ts(res[:, o:o + 512], bank[:, :], ps[:, g:g + 1], None, ALU.mult, None, r, t_ps, t_x2, turned)
                    X.give(j, e)
                    t_pool[g, c] = e
                plf[g % 2] = r
                yield

        run(pooling())
        snap = so_far()
        sq.close()
        sq = ExitStack()
        qk = [[sb(sq, f"s{x}{i}", 1024) for x in "qk"] for i in range(2)]
        lt = [sb(sq, f"lt{i}", 512) for i in range(3)]
        spb = [sb(sq, f"sp{i}", 512) for i in range(4)]
        wt = [sb(sq, f"wt{i}", 512) for i in range(2)]
        run_s = [sb(sq, f"rs{i}", 512) for i in range(2)]
        zb = sb(sq, "zb", 512, BF)
        t_zb = DV.put(lambda e: e.memset(zb[:, :], 0.0), (snap,))
        LT, SPR, WT = Ring(lt, snap), Ring(spb, snap), Ring(wt, snap)
        G, Z, O = Ring(banks[0:2], snap), Ring(banks[2:6], snap), Ring(banks[6:8], snap)
        AC.put(lambda e: e.preload_act_table_set("natural_log_exp_and_others"), (), inc=False)
        sfree = [snap, snap]
        sready = {}
        last_p = [None]

        def project2(h):
            toks = []
            for n, dst in enumerate(qk[h % 2]):
                u = get("F", "w_in_2", 512 * n + 128 * h)
                for half in range(2):
                    j, bank, r = gemm_f(u, xh, xl, 512 * half, 512, t_h)
                    e = copy_a(dst[:, 512 * half:512 * half + 512], bank[:, :], r, sfree[h % 2],
                               scale=0.125 if n == 0 else 1.0)
                    G.give(j, e)
                    toks.append(e)
                    yield
                done(u[0], r)
            last_p[0] = r
            sready[h] = toks

        def stick(h, hh, toks_out):
            q, k = qk[h % 2]
            pr = slice(64 * hh, 64 * hh + 64)
            w = sready[h]
            rs = run_s[hh]
            for c in range(2):
                jo, ob, fo = O.take()
                mm(ob[0:64, :], zb[:, 0:64], zb[:, :], True, False, t_zb, fo, skip=True)
                z0 = DV.put(lambda e: e.memset(rs[:, :], 0.0), (rfree[hh],))
                state = {"sum": z0}

                def first(b):
                    t0 = max(128 * b, 512 * c)
                    n = 512 * (c + 1) - t0
                    jz, z, fz = Z.take()
                    r = mm(z[:, 0:n], k[pr, 128 * b:128 * b + 128], q[pr, t0:t0 + n], True, False, fz, w, inc=True, skip=True)
                    jl, l, fl = LT.take()
                    a = act(l[:, 0:n], z[:, 0:n], ACT.Abs, r, fl)
                    a = act(l[:, 0:n], l[:, 0:n], ACT.Exp, a, scale=-1.0)
                    a = act(l[:, 0:n], l[:, 0:n], ACT.Ln, a, bias=1.0)
                    js, s_, fs = SPR.take()
                    d = stt(s_[:, 0:n], z[:, 0:n], 0.0, l[:, 0:n], ALU.max, ALU.add, a, fs)
                    LT.give(jl, d)
                    m = d
                    if 128 * b >= 512 * c:
                        m = PO.put(lambda e: e.affine_select(out=s_[:, 0:128], in_=s_[:, 0:128], compare_op=ALU.is_gt,
                                                             fill=0.0, base=0, pattern=[[1, 128]],
                                                             channel_multiplier=-1), (d,))
                    return b, t0, n, jz, z, js, s_, m, d

                def second(x):
                    b, t0, n, jz, z, js, s_, m, d = x
                    o0 = t0 - 512 * c
                    top_b = 4 * c + 3
                    r = mm(z[:, 0:n], negu, s_[:, 0:n], False, b == top_b, m, d, inc=True, skip=True)
                    if b != top_b:
                        r = mm(z[:, 0:n], neg1, rs[:, o0:512], False, True, state["sum"], inc=True, skip=True)
                    if b:
                        state["sum"] = tt(rs[:, o0:512], rs[:, o0:512], s_[:, 0:n], ALU.add, r, m, state["sum"], q=PO)
                        SPR.give(js, state["sum"])
                    else:
                        SPR.give(js, r)
                        rfree[hh] = r
                    jw, wb, fw = WT.take()
                    e = act(wb[:, 0:n], z[:, 0:n], ACT.Exp, r, fw)
                    Z.give(jz, e)
                    if 128 * b >= 512 * c:
                        e = PO.put(lambda en: en.affine_select(out=wb[:, 0:128], in_=wb[:, 0:128], compare_op=ALU.is_gt,
                                                               fill=0.0, base=0, pattern=[[1, 128]],
                                                               channel_multiplier=-1), (e,))
                    r = mm(ob[0:64, o0:512], vt[:, 512 * b + 128 * h + 64 * hh:512 * b + 128 * h + 64 * hh + 64],
                           wb[:, 0:n], False, b == 0, e, tv, inc=True, skip=True)
                    WT.give(jw, r)
                    return r

                x = first(4 * c + 3)
                yield
                for b in range(4 * c + 2, -1, -1):
                    y = first(b)
                    r = second(x)
                    x = y
                    yield
                r = second(x)
                e = copy_v(res[pr, 1024 * h + 512 * c:1024 * h + 512 * c + 512], ob[0:64, :], r, t_x2, turned)
                O.give(jo, e)
                toks_out.append(e)
                yield
            last_r[0] = r

        rfree = [snap, snap]
        last_r = [None]
        t_att = []
        halves = [None] * 8

        def split(k, *w):
            src = res[:, 1024 * k:1024 * k + 1024]
            a = copy_a(xh[:, 1024 * k:1024 * k + 1024], src, w, proj_done[0])
            b = tt(xl[:, 1024 * k:1024 * k + 1024], src, xh[:, 1024 * k:1024 * k + 1024].bitcast(F32), ALU.subtract, a, q=PO)
            halves[k] = (a, b)

        proj_done = [None]

        def splits():
            for g in range(4):
                split(4 + g, t_pool[g, 0], t_pool[g, 1])
                yield
            for h in range(3):
                split(h, t_att3)
                yield

        run(project2(0))
        for h in range(4):
            gens = [(stick(h, 0, t_att), 14), (stick(h, 1, t_att), 14)]
            if h < 3:
                gens.append((project2(h + 1), 5))
            else:
                proj_done[0] = last_p[0]
                t_att3 = list(t_att)
                gens.append((splits(), 7))
            merge(*gens)
            sfree[h % 2] = (last_r[0], PE.now())
        split(3, t_att)
        snap = so_far()
        sq.close()
        sub.close()
        sub = ExitStack()
        G = Ring(banks[0:5], snap)
        X = Ring(banks[5:8], snap)
        gm, sf, gs, gt = [sb(sub, n, 1024) for n in ("gm", "sf", "gs", "gt")]
        t1, t2, t3 = row("", gm[:, :], 2, snap), row("", sf[:, :], 3, snap), row("", gs[:, :], 4, snap)
        d = dma(SP, gt[:, :], T["g_mix_post_2"].partition_broadcast(128), snap)
        m1 = tt(gm[:, :], gm[:, :], gt[:, :], ALU.mult, t1, d)
        d = dma(SP, gt[:, :], T["g_ffn_pre_2"].partition_broadcast(128), m1)
        m3 = stt(gs[:, :], gs[:, :], 1.0, gt[:, :], ALU.add, ALU.mult, t3, d)
        xb = [sb(sub, f"xb{i}", 1024) for i in range(3)]
        junk = [sb(sub, "sq3", 1024, BF), snap]
        xbf = [snap] * 3
        t_m = [halves] * 8
        ty = [None] * 8
        t_x3 = []

        def fin2(tb, n, bank, r):
            e = copy_a(block(tb)[:, 512 * n:512 * n + 512], bank[:, :], r, t_m[tb])
            t_m[tb] = (t_m[tb], e)
            return e

        late.clear()

        def norm3(tb, r):
            if late:
                b, t, pe = late.pop()
                ty[b] = turn(xb[b % 3], b, xh, xl, t, pe)
                xbf[b % 3] = PE.now()
            if tb < 8:
                src, x_ = block(tb), xb[tb % 3]
                d = dma(SP, x_[:, :], x2_d[128 * tb:128 * tb + 128, :], xbf[tb % 3], t_x2)
                rr, t, junk[1] = rms(src, EPS, junk[0][:, :], t_m[tb], junk[1])
                t = stt(src, src, rr, gm[:, :], ALU.mult, ALU.mult, t, m1)
                t = tt(src, src, x_[:, :], ALU.add, t, d)
                t_x3.append(dma(SP, mix_d[128 * tb:128 * tb + 128, :], src, t, store=True))
                rr, t2_, junk[1] = rms(src, EPS, junk[0][:, :], t, junk[1])
                t = stt(x_[:, :], src, rr, gs[:, :], ALU.mult, ALU.mult, t2_, m3, t)
                t = tt(x_[:, :], x_[:, :], sf[:, :], ALU.add, t, t2)
                late.append((tb, t, r))
                t_rd[tb] = t

        t_rd = [None] * 8
        mix_gemm("w_out_2", [halves] * 8, fin2, norm3)
        snap = so_far()
        sub.close()
        t_acc = [(t_x3[tb], t_rd[tb]) for tb in range(8)]

        def vectors3(ctx, snap):
            gf, gq = sb(ctx, "gf", 1024), sb(ctx, "gq", 1024)
            xc = [gq, sb(ctx, "xc1", 1024), sb(ctx, "xc2", 1024)]
            t = row("", gf[:, :], 5, snap)
            t2 = dma(SP, gq[:, :], T["g_ffn_post_2"].partition_broadcast(128), snap)
            t3 = tt(gf[:, :], gf[:, :], gq[:, :], ALU.mult, t, t2)
            vec["3"] = (gf, xc, [t3, snap, snap], t3)
            vec["junk"] = [sb(ctx, "sq4", 1024, BF), snap]

        def norm4(tb, r):
            gf, xc, free, tg = vec["3"]
            if tb == 8:
                return
            src, x_ = block(tb), xc[tb % 3]
            d = dma(SP, x_[:, :], mix_d[128 * tb:128 * tb + 128, :], free[tb % 3], t_x3)
            rr, t, vec["junk"][1] = rms(src, EPS, vec["junk"][0][:, :], t_acc[tb], vec["junk"][1])
            t = stt(src, src, rr, gf[:, :], ALU.mult, ALU.mult, t, tg)
            t = tt(src, src, x_[:, :], ALU.add, t, d)
            free[tb % 3] = t
            dma(SP, out[128 * tb:128 * tb + 128, :], src, t, store=True)

        sa = ffn("w_gate_2", "w_up_2", 0, "w_down_2", ty, res, t_acc, snap, True, vectors3, norm4)
        sa.close()
        ph.close()
        SPw = [*drams]
        SP.items.append((flat(SPw, {}), None, None, 0))
        block = top.enter_context(nc.Block())

        @block.sync
        def _(e):
            SP.emit(e)

        @block.scalar
        def _(e):
            AC.emit(e)

        @block.vector
        def _(e):
            DV.emit(e)

        @block.gpsimd
        def _(e):
            PO.emit(e)

        @block.tensor
        def _(e):
            PE.emit(e)


_NAMES = ['x', 'w_in', 'gmlp_w_s', 'gmlp_b_s', 'gmlp_ln_g', 'gmlp_ln_b', 'lam_q1', 'lam_k1', 'lam_q2', 'lam_k2',
          'diff_subln_g', 'w_out', 'ln1_g', 'ln1_b', 'w_gu', 'w_down', 'ln2_g', 'ln2_b', 'c_2', 'w_cond_2',
          'b_cond_2', 'g_mix_pre_2', 'g_mix_post_2', 'w_in_2', 'w_pool_2', 'pool_scale_2', 'w_out_2',
          'g_ffn_pre_2', 'g_ffn_post_2', 'w_gate_2', 'w_up_2', 'w_down_2']


def kernel(**inputs):
    import concourse.bacc as _bacc
    from concourse.bass_utils import run_bass_kernel_spmd as _run

    nc = _bacc.Bacc("TRN2", target_bir_lowering=False, num_devices=1)
    arrays, T = {}, {}
    for name in _NAMES:
        a = np.ascontiguousarray(inputs[name])
        arrays["in_" + name] = a
        T[name] = nc.dram_tensor("in_" + name, a.shape, mybir.dt.from_np(a.dtype), kind="ExternalInput").ap()[0]
    con, dist, bands = shape_constants()
    for name, a in (("consts", con), ("dist", dist), ("bands", bands)):
        arrays["in_" + name] = a
        T[name] = nc.dram_tensor("in_" + name, a.shape, F32, kind="ExternalInput").ap()
    T["mix_d"] = nc.dram_tensor("mix_d", (1024, 1024), F32, kind="Internal").ap()
    T["vec_d"] = nc.dram_tensor("vec_d", (1, 6144), F32, kind="Internal").ap()
    T["x2_d"] = nc.dram_tensor("x2_d", (1024, 1024), F32, kind="Internal").ap()
    out = nc.dram_tensor("out_0", (1, 1024, 1024), F32, kind="ExternalOutput").ap()
    build(nc, T, out[0])
    r = _run(nc, [arrays], core_ids=[0])
    return r.results[0]["out_0"]
```

```python
from contextlib import ExitStack

import numpy as np

import concourse.bass as bass
from concourse import mybir

F32 = mybir.dt.float32
FR = mybir.dt.float32r
U32 = mybir.dt.uint32
I32 = mybir.dt.int32
BF = mybir.dt.bfloat16
ALU = mybir.AluOpType
ACT = mybir.ActivationFunctionType
AX = mybir.AxisListType

D = 1024
S = 1024
NB = 8
FF = 2816
BIG = 1.0e30
OFF_BQ, OFF_BK, OFF_BV = 512, 1024, 1536
OFF_CQ, OFF_CK, OFF_CV = 2048, 2304, 2560
OFF_IQ, OFF_IK, OFF_IW = 2816, 3072, 3104
ALPHA = 2.0 ** 0.25
LAM_INIT = 0.2
LN_EPS = 1e-5
EPS = 1e-6
NRAW = 3
NU = 5
CHUNKS = [(0, 6), (6, 6), (12, 6), (18, 4)]
WINDOWS = (2, 4, 8, 16)
C_ID, C_NU, C_N1, C_Q, C_END = 0, 128, 256, 384, 386


def shape_constants():
    p = np.arange(128)[:, None]
    r = np.arange(1024)[None, :] - 896
    neg = -np.abs(p - r).astype(np.float32)
    neg = np.where((r >= 64) & (p < 64), np.float32(-BIG), neg).astype(np.float32)
    q = np.arange(128)[None, :]
    c = np.zeros((128, C_END), np.float32)
    c[:, C_ID:C_ID + 128] = np.eye(128)
    c[:, C_NU:C_NU + 128] = -(p >= q).astype(np.float32)
    c[:, C_N1:C_N1 + 128] = -1.0
    for j in range(2):
        for h in range(2):
            c[64 * h:64 * h + 64, C_Q + j] = 2.0 ** (2 * (2 * j + h + 1) - 3)
    m = np.zeros((128, 4, 3, 128), np.float32)
    s_ = np.arange(128)[:, None]
    t_ = np.arange(128)[None, :]
    for g, w in enumerate(WINDOWS):
        eye = (s_ == t_).astype(np.float32)
        m[:, g, 0, :] = ((s_ <= t_) & (s_ > t_ - w)) / w - eye
        m[:, g, 1, :] = ((s_ - 128) > t_ - w) / w
        m[:, g, 2, :] = ((s_ <= t_) & (s_ > t_ - w)) / np.minimum(t_ + 1, w) - eye
    return c, neg, m.reshape(128, 1536)


class Queue:

    def __init__(self, sem):
        self.sem = sem
        self.n = 0
        self.items = []

    def put(self, fn, waits, inc=True):
        self.items.append((flat(waits, {}), fn, self.sem if inc else None, 1))
        if inc:
            self.n += 1
        return (self.sem, self.n)

    def now(self):
        return (self.sem, self.n)

    def emit(self, eng):
        seen = {}
        for need, fn, sem, k in self.items:
            for s, v in need.values():
                if seen.get(s.name, 0) < v:
                    eng.wait_ge(s, v)
                    seen[s.name] = v
            if fn is None:
                continue
            ins = fn(eng)
            if sem is not None:
                ins.then_inc(sem, k)


def flat(waits, need):
    if not waits:
        return need
    if isinstance(waits, tuple) and len(waits) == 2 and isinstance(waits[1], int):
        s, v = waits
        if v > need.get(s.name, (s, 0))[1]:
            need[s.name] = (s, v)
        return need
    for w in waits:
        flat(w, need)
    return need


def merge(*gens):
    left = [[g, n, 0] for g, n in gens]
    while left:
        left.sort(key=lambda x: x[2] / x[1])
        try:
            next(left[0][0])
            left[0][2] += 1
        except StopIteration:
            left.pop(0)


def merge_until(stop, gens):
    left = [[g, n, 0] for g, n in gens]
    while True:
        left.sort(key=lambda x: x[2] / x[1])
        g = left[0]
        try:
            next(g[0])
            g[2] += 1
        except StopIteration:
            left.pop(0)
            if g[0] is stop:
                return


def run(gen):
    for _ in gen:
        pass


def build(nc, T, out):
    top = ExitStack()
    with top:
        def sem(name):
            return top.enter_context(nc.semaphore(name))

        def sb(ctx, name, n, dt=F32, p=128):
            return ctx.enter_context(nc.sbuf_tensor(name, [p, n], dt))

        PE, DV, AC, PO, SP = [Queue(sem("s_" + n)) for n in ("pe", "dve", "act", "pool", "sp")]
        NDS = 32
        dsem = [sem(f"d{i}") for i in range(NDS)]
        dcount = [0] * NDS
        dnext = [0]
        drams = []

        def dma(q, o, i, *waits, store=False):
            o = o.bitcast(F32) if o.dtype == FR else o
            i = i.bitcast(F32) if i.dtype == FR else i
            k = dnext[0] % NDS
            dnext[0] += 1
            prev = (dsem[k], 16 * dcount[k]) if dcount[k] else None
            dcount[k] += 1
            q.items.append((flat([waits, prev], {}), lambda e: e.dma_start(o, i), dsem[k], 16))
            tok = (dsem[k], 16 * dcount[k])
            if store:
                drams.append(tok)
            return tok

        def so_far():
            return [q.now() for q in (PE, DV, AC, PO)] + [(dsem[k], 16 * dcount[k]) for k in range(NDS) if dcount[k]]

        def act(o, i, func, *w, bias=0.0, scale=1.0, acc=None):
            if acc is None:
                return AC.put(lambda e: e.activation(o, i, func, bias=bias, scale=scale), w)
            return AC.put(lambda e: e.activation(o, i, func, bias=bias, scale=scale, accum_out=acc), w)

        def copy_a(o, i, *w, scale=1.0):
            return act(o, i, ACT.Copy, *w, scale=scale)

        def copy_v(o, i, *w):
            return DV.put(lambda e: e.tensor_copy(o, i), w)

        def ts(o, i, s1, s2, op0, op1, *w, acc=None, q=None):
            q = q or DV
            if acc is not None:
                return q.put(lambda e: e.tensor_scalar(o, i, s1, s2, op0, op1, accum_out=acc), w)
            if op1 is None:
                return q.put(lambda e: e.tensor_scalar(o, i, s1, None, op0), w)
            return q.put(lambda e: e.tensor_scalar(o, i, s1, s2, op0, op1), w)

        def tt(o, a, b, op, *w, q=None):
            return (q or DV).put(lambda e: e.tensor_tensor(o, a, b, op), w)

        def stt(o, a, s, b, op0, op1, *w):
            return DV.put(lambda e: e.scalar_tensor_tensor(out=o, in0=a, scalar=s, in1=b, op0=op0, op1=op1), w)

        def ttr(o, a, b, scale, init, op0, op1, acc, *w):
            return DV.put(lambda e: e.tensor_tensor_reduce(out=o, in0=a, in1=b, scale=scale, scalar=init,
                                                           op0=op0, op1=op1, accum_out=acc), w)

        def mm(o, l, r, start, stop, *w, inc=False, skip=False):
            return PE.put(lambda e: e.matmul(o, l, r, start=start, stop=stop, skip_group_check=skip), w, inc)

        def tr(o, i, idn, *w, inc=False):
            return PE.put(lambda e: e.transpose(o, i, idn), w, inc)

        class Ring:

            def __init__(self, bufs, toks=None):
                self.bufs = bufs
                self.free = [(j, toks) for j in range(len(bufs))]

            def take(self):
                j, toks = self.free.pop(0)
                return j, self.bufs[j], toks

            def give(self, j, *toks):
                self.free.append((j, toks))

        banks = [top.enter_context(nc.psum_tensor(f"bank{i}", [128, 512], F32)) for i in range(8)]
        G = Ring(banks[0:3])
        L = Ring(banks[3:6])
        X = Ring(banks[6:8])

        con = sb(top, "con", C_END)
        t_con = dma(SP, con[:, :], T["consts"])
        idn = con[:, C_ID:C_ID + 128]
        negu = con[:, C_NU:C_NU + 128]
        neg1 = con[:, C_N1:C_N1 + 128]
        st = sb(top, "st", 512)
        cc = sb(top, "cc", 8)
        res = sb(top, "res", 8192)

        def block(tb):
            return res[:, 1024 * tb:1024 * tb + 1024]


        raw = [sb(top, f"raw{i}", 1024) for i in range(NRAW)]
        wh = [sb(top, f"wh{i}", 1024, FR) for i in range(NU)]
        wl = [sb(top, f"wl{i}", 1024, FR) for i in range(NU)]
        rsem = [sem(f"r{i}") for i in range(NRAW)]

        mod_at = [0]

        def mrows(n):
            for _ in range(n):
                m = mod_at[0]
                mod_at[0] += 1
                yield ("R", "w_cond_2", m % 4, 512 * (m // 4))

        def plan():
            for j in range(4):
                yield ("T", "w_in", j, 0)
            for c in (OFF_IQ, OFF_IQ + 128, OFF_IK):
                yield ("F", "w_in", c)
            for j in range(4):
                yield ("T", "w_in", j, OFF_BV)
            for j in range(2):
                yield ("H", "w_in", j, OFF_CV)
            for q, k, n in ((OFF_BQ, OFF_BK, 4), (OFF_CQ, OFF_CK, 2)):
                for h in range(n):
                    yield ("F", "w_in", q + 128 * h)
                    yield ("F", "w_in", k + 128 * h)
            for n in range(2):
                for j in range(4):
                    yield ("T", "w_out", j, 512 * n)
            for a, k in CHUNKS:
                for f in range(a, a + k):
                    yield ("F", "w_gu", 128 * f)
                    yield ("F", "w_gu", FF + 128 * f)
                    if a < 18:
                        yield from mrows(1)
                for n in range(2):
                    for j in range(a // 2, (a + k) // 2):
                        yield ("T", "w_down", j, 512 * n)
                    if a < 18:
                        yield from mrows(5)
            for n in range(2):
                for j in range(4):
                    yield ("T", "w_in_2", j, 1024 + 512 * n)
            for h in range(4):
                yield ("F", "w_in_2", 128 * h)
                yield ("F", "w_in_2", 512 + 128 * h)
            for n in range(2):
                for j in range(4):
                    yield ("T", "w_out_2", j, 512 * n)
            for a, k in CHUNKS:
                for f in range(a, a + k):
                    yield ("F", "w_gate_2", 128 * f)
                    yield ("F", "w_up_2", 128 * f)
                for n in range(2):
                    for j in range(a // 2, (a + k) // 2):
                        yield ("T", "w_down_2", j, 512 * n)

        keys = list(plan())
        raw_free = [None] * NRAW
        raw_tok = {}
        split_tok = {}
        raw_rel = set()
        rel = {}
        slot_of = {}
        at = {"dma": 0, "split": 0, "get": 0, "slots": 0}
        slot_prev = [None] * NU

        def pump():
            while True:
                moved = False
                m = at["dma"]
                if m < len(keys) and (m < NRAW or (m - NRAW) in raw_rel):
                    key = keys[m]
                    w = T[key[1]]
                    r = raw[m % NRAW]
                    if key[0] == "F":
                        dst = r[:, :].rearrange("p (k c) -> p k c", k=8)
                        wv = w.rearrange("(k p) c -> p k c", p=128)
                        if key[2] == OFF_IK and key[1] == "w_in":
                            pairs = [(dst[:, :, 32 * j:32 * j + 32], wv[:, :, key[2]:key[2] + 32]) for j in range(4)]
                        else:
                            pairs = [(dst, wv[:, :, key[2]:key[2] + 128])]
                    elif key[0] == "H":
                        dst = r[:, :].rearrange("p (k c) -> p k c", k=4)
                        wv = w[512 * key[2]:512 * key[2] + 512, key[3]:key[3] + 256]
                        pairs = [(dst, wv.rearrange("(k p) c -> p k c", p=128))]
                    else:
                        dst = r[:, :].rearrange("p (k c) -> p k c", k=2)
                        wv = w[256 * key[2]:256 * key[2] + 256, key[3]:key[3] + 512]
                        pairs = [(dst, wv.rearrange("(k p) c -> p k c", p=128))]
                    toks = []
                    for j, (o, i) in enumerate(pairs):
                        if len(pairs) == 1:
                            cnt = at.get(m % NRAW, 0) + 16
                            at[m % NRAW] = cnt
                            SP.items.append((flat([raw_free[m % NRAW]], {}), lambda e, o=o, i=i: e.dma_start(o, i),
                                             rsem[m % NRAW], 16))
                            toks.append((rsem[m % NRAW], cnt))
                        else:
                            toks.append(dma(SP, o, i, raw_free[m % NRAW]))
                    raw_tok[m] = toks
                    at["dma"] += 1
                    moved = True
                m = at["split"]
                if m < len(keys) and m < at["dma"] and m <= at["get"] + 9:
                    if keys[m][0] == "R":
                        at["split"] += 1
                        moved = True
                    else:
                        s = at["slots"] % NU
                        if slot_prev[s] is None or slot_prev[s] in rel:
                            prev = rel.get(slot_prev[s])
                            r = raw[m % NRAW]
                            th = copy_a(wh[s][:, :], r[:, :], raw_tok[m], prev)
                            tl = tt(wl[s][:, :], r[:, :], wh[s][:, :].bitcast(F32), ALU.subtract, th, raw_tok[m], prev, q=PO)
                            raw_free[m % NRAW] = (th, tl)
                            raw_rel.add(m)
                            split_tok[m] = (th, tl)
                            slot_of[m] = s
                            slot_prev[s] = m
                            at["slots"] += 1
                            at["split"] += 1
                            moved = True
                if not moved:
                    return

        def get(*key):
            m = at["get"]
            assert keys[m] == key, (keys[m], key)
            at["get"] += 1
            pump()
            if key[0] == "R":
                return m, raw[m % NRAW], None, raw_tok[m]
            assert m in split_tok, key
            s = slot_of[m]
            return m, wh[s], wl[s], split_tok[m]

        def done(m, *toks):
            if keys[m][0] == "R":
                raw_free[m % NRAW] = toks
                raw_rel.add(m)
            else:
                rel[m] = toks
            pump()

        def gemm_f(u, xh, xl, t0, n, w):
            m, h, l, tok = u
            j, bank, fr = G.take()
            for k in range(8):
                a, b = h[:, 128 * k:128 * k + 128], l[:, 128 * k:128 * k + 128]
                xa, xb = xh[:, 1024 * k + t0:1024 * k + t0 + n], xl[:, 1024 * k + t0:1024 * k + t0 + n]
                mm(bank[:, 0:n], a, xa, k == 0, False, tok, w, fr)
                mm(bank[:, 0:n], a, xb, False, False)
                r = mm(bank[:, 0:n], b, xa, False, k == 7, inc=k == 7)
            return j, bank, r

        def gemm_t(us, xh, xl, tb, w, last=False, wide=512):
            j, bank, fr = G.take()
            per = 1024 // wide
            nk = per * len(us)
            for k in range(nk):
                m, h, l, tok = us[k // per]
                c = wide * (k % per)
                o = 1024 * (k % 4 if isinstance(xh, list) else k) + 128 * tb
                ah, al = (xh[k // 4], xl[k // 4]) if isinstance(xh, list) else (xh, xl)
                xa, xb = ah[:, o:o + 128], al[:, o:o + 128]
                mm(bank[:, 0:wide], xa, h[:, c:c + wide], k == 0, False, tok, w, fr)
                mm(bank[:, 0:wide], xa, l[:, c:c + wide], False, False)
                free = k == nk - 1 or (last and k % per == per - 1)
                r = mm(bank[:, 0:wide], xb, h[:, c:c + wide], False, k == nk - 1, inc=free)
                if last and k % per == per - 1:
                    done(m, r)
            return j, bank, r

        def turn(src, tb, xh, xl, *w):
            last = None
            for half in range(2):
                j, bank, fr = X.take()
                for k in range(4):
                    c = 128 * (4 * half + k)
                    t = tr(bank[:, 128 * k:128 * k + 128], src[:, c:c + 128], idn, w, fr, t_con, inc=k == 3)
                v = bank[:, :].rearrange("p (k c) -> p k c", k=4)
                oh = xh[:, :].rearrange("p (k c) -> p k c", k=8)[:, 4 * half:4 * half + 4, 128 * tb:128 * tb + 128]
                ol = xl[:, :].rearrange("p (k c) -> p k c", k=8)[:, 4 * half:4 * half + 4, 128 * tb:128 * tb + 128]
                a = copy_a(oh, v, t)
                b = tt(ol, v, oh.bitcast(F32), ALU.subtract, a)
                X.give(j, b)
                last = b
            return last

        stn = [0]
        st_tok = {}

        def small(n):
            if stn[0] + n > 512:
                stn[0] = 0
            o = stn[0]
            stn[0] += n
            return st[:, o:o + n]

        bns = sb(top, "bns", 24)

        def mean_rstd(src, eps, *w):
            mv, r = small(2), small(2)
            a = DV.put(lambda e: e.bn_stats(bns[:, 0:6], src[:, 0:512]), w)
            b = DV.put(lambda e: e.bn_stats(bns[:, 6:12], src[:, 512:1024]), w)
            c = DV.put(lambda e: e.bn_aggr(mv, bns[:, 0:12]), (a, b))
            d = ts(r[:, 0:1], mv[:, 1:2], eps, None, ALU.add, None, c)
            f = act(r[:, 1:2], r[:, 0:1], ACT.Sqrt, d)
            g = DV.put(lambda e: e.reciprocal(r[:, 0:1], r[:, 1:2]), (f,))
            return mv[:, 0:1], r[:, 0:1], g

        def rms(src, eps, junk, *w):
            ss = small(1)
            a = act(junk, src, ACT.Square, w, acc=ss)
            return *rms_of(ss, eps, a), a

        def rms_of(ss, eps, a):
            r = small(2)
            b = ts(r[:, 0:1], ss, 1.0 / 1024, eps, ALU.mult, ALU.add, a)
            f = act(r[:, 1:2], r[:, 0:1], ACT.Sqrt, b)
            g = DV.put(lambda e: e.reciprocal(r[:, 0:1], r[:, 1:2]), (f,))
            return r[:, 0:1], g

        mix_d, x2_d = T["mix_d"], T["x2_d"]
        xd = T["x"]

        ph = ExitStack()
        score = sb(ph, "score", 4224)
        cols = {}
        o = 0
        for i in range(2, 8):
            cols[i] = (o, 128 * (i + 1))
            o += 128 * (i + 1)
        cand = sb(ph, "cand", 64)
        nd = sb(ph, "nd", 1024)
        nat = [sb(ph, f"nat{i}", 1024, FR) for i in range(2)]
        qst, kst = sb(ph, "qst", 3072, FR), sb(ph, "kst", 1024, FR)
        sx = ExitStack()
        xh, xl = sb(sx, "xh", 8192, FR), sb(sx, "xl", 8192, FR)
        V = Ring([block(tb) for tb in (6, 7, 0, 1, 2, 3)])
        mixw = {}

        t_x = [None] * 8
        for tb in range(8):
            j, buf, fr = V.take()
            d = dma(SP, buf, xd[128 * tb:128 * tb + 128, :], fr)
            t_x[tb] = turn(buf, tb, xh, xl, d)
            V.give(j, t_x[tb], PE.now())
            if tb == 3:
                pump()
        t_nd = dma(SP, nd[:, :], T["dist"])

        d2 = dma(SP, score[0:8, 0:128], T["c_2"].rearrange("(k p) -> k p", p=128))
        j, bank, fr = X.take()
        t = tr(bank[:, 0:8], score[0:8, 0:128], idn[0:8, 0:8], d2, fr, t_con, inc=True)
        t_cc = act(cc[:, :], bank[:, 0:8], ACT.Silu, t)
        X.give(j, t_cc)
        hbuf = res
        au, av = hbuf[:, 0:2048], hbuf[:, 2048:4096]
        wst, lng, tmp = hbuf[:, 4096:4608], hbuf[:, 4608:5120], hbuf[:, 5120:5632]
        bsc, gst = hbuf[:, 5632:5640], hbuf[:, 5640:5768]
        b4 = hbuf[0:4, 5768:5896]
        t_g = [dma(SP, lng[:, 0:256], T["gmlp_ln_g"].rearrange("a b -> (a b)").partition_broadcast(128)),
               dma(SP, lng[:, 256:512], T["gmlp_ln_b"].rearrange("a b -> (a b)").partition_broadcast(128))]
        t_ws = dma(SP, tmp.rearrange("p (g s) -> p g s", g=4), T["gmlp_w_s"].rearrange("g t s -> t g s"))
        t_b4 = dma(SP, b4, T["gmlp_b_s"])
        j, bank, fr = X.take()
        for g in range(4):
            t = tr(bank[:, 128 * g:128 * g + 128], tmp[:, 128 * g:128 * g + 128], idn, t_ws, fr, inc=g == 3)
        e1 = copy_v(wst, bank[:, :], t)
        X.give(j, e1)
        wv = wst[64:128, :].rearrange("p (g s) -> p g s", g=4)[:, :, 0:64]
        e1 = DV.put(lambda e: e.memset(wv, 0.0), (e1,))
        j, bank, fr = X.take()
        t = tr(bank[:, 0:4], b4, idn[0:4, 0:4], t_b4, fr, inc=True)
        e2 = copy_v(bsc[:, 0:4], bank[:, 0:4], t)
        X.give(j, e2)
        us = [get("T", "w_in", j, 0) for j in range(4)]
        t_ge = {}
        for tb in range(8):
            j, bank, r = gemm_t(us, xh, xl, tb, t_x[tb], last=tb == 7)
            a = act(au[:, 256 * tb:256 * tb + 256], bank[:, 0:256], ACT.Gelu_apprx_tanh, r)
            b = act(av[:, 256 * tb:256 * tb + 256], bank[:, 256:512], ACT.Gelu_apprx_tanh, r)
            G.give(j, a, b)
            t_ge["u", tb], t_ge["v", tb] = a, b
        last = []

        def gmlp_norm():
            prev = None
            for q in range(4):
                flat_v = av[:, 512 * q:512 * q + 512]
                vq = flat_v.rearrange("p (n c) -> p n c", c=64)
                s8 = gst[:, 8 * q:8 * q + 8]
                a = DV.put(lambda e, vq=vq, s8=s8: e.tensor_reduce(s8, vq, AX.X, ALU.add), (t_ge["v", 2 * q], t_ge["v", 2 * q + 1]))
                b = ts(s8, s8, 1.0 / 64, None, ALU.mult, None, a)
                c = tt(vq, vq, s8.unsqueeze(2).broadcast_to([128, 8, 64]), ALU.subtract, b)
                d = tt(tmp, flat_v, flat_v, ALU.mult, c, e1, prev)
                yield
                v8 = gst[:, 32 + 8 * q:40 + 8 * q]
                f = DV.put(lambda e, v8=v8: e.tensor_reduce(v8, tmp.rearrange("p (n c) -> p n c", c=64), AX.X, ALU.add), (d,))
                g = ts(v8, v8, 1.0 / 64, LN_EPS, ALU.mult, ALU.add, f)
                h = act(gst[:, 64 + 8 * q:72 + 8 * q], v8, ACT.Sqrt, g)
                r8 = gst[:, 96 + 8 * q:104 + 8 * q]
                k = DV.put(lambda e, q=q, r8=r8: e.reciprocal(r8, gst[:, 64 + 8 * q:72 + 8 * q]), (h,))
                m = tt(vq, vq, r8.unsqueeze(2).broadcast_to([128, 8, 64]), ALU.mult, k)
                v2 = flat_v.rearrange("p (n c) -> p n c", c=256)
                m = tt(v2, v2, lng[:, 0:256].unsqueeze(1).broadcast_to([128, 2, 256]), ALU.mult, m, t_g)
                m = tt(v2, v2, lng[:, 256:512].unsqueeze(1).broadcast_to([128, 2, 256]), ALU.add, m, t_g)
                prev = m
                last.append(m)
                yield

        sub = ExitStack()
        iw = sb(sub, "iw", 64)
        wih, wil, wir = sb(sub, "wih", 64, FR), sb(sub, "wil", 64, FR), sb(sub, "wir", 64)
        t_iw, t_kst, t_qst = [], [], []

        def stack_queries(toks, free):
            t_qst.clear()
            for h in range(4):
                for j in range(4):
                    t_qst.append(dma(SP, qst[32 * j:32 * j + 32, 768 * h:768 * h + 768],
                                     nat[j % 2][32 * h:32 * h + 32, 256:1024], toks, free))

        def index_proj():
            t_w = dma(SP, wir[:, :].rearrange("p (k c) -> p k c", k=8),
                      T["w_in"].rearrange("(k p) c -> p k c", p=128)[:, :, OFF_IW:OFF_IW + 8])
            th = copy_a(wih[:, :], wir[:, :], t_w)
            tl = tt(wil[:, :], wir[:, :], wih[:, :].bitcast(F32), ALU.subtract, th)
            for n, c in enumerate((OFF_IQ, OFF_IQ + 128, OFF_IK)):
                u = get("F", "w_in", c)
                toks = []
                for half in range(2):
                    hs = slice(512 * half, 512 * half + 512)
                    j, bank, r = gemm_f(u, xh, xl, 512 * half, 512, t_x)
                    if n < 2:
                        a = copy_a(nat[0][:, hs], bank[:, :], r, t_qst)
                        b = tt(nat[1][:, hs], bank[:, :], nat[0][:, hs].bitcast(F32), ALU.subtract, a, t_qst)
                        toks += [a, b]
                    else:
                        a = copy_a(kst[:, hs], bank[:, :], r)
                        b = tt(kst[64:128, hs], bank[64:128, :], kst[64:128, hs].bitcast(F32), ALU.subtract, a)
                        t_kst.extend([a, b])
                    G.give(j, b)
                    yield
                done(u[0], r)
                if n == 0:
                    stack_queries(toks, None)
                elif n == 1:
                    nat_t.extend(toks)
            for tb in range(8):
                j, bank, fr = G.take()
                for k in range(8):
                    o = 1024 * k + 128 * tb
                    mm(bank[:, 0:8], xh[:, o:o + 128], wih[:, 8 * k:8 * k + 8], k == 0, False, th, tl, fr)
                    mm(bank[:, 0:8], xh[:, o:o + 128], wil[:, 8 * k:8 * k + 8], False, False)
                    r = mm(bank[:, 0:8], xl[:, o:o + 128], wih[:, 8 * k:8 * k + 8], False, k == 7, inc=k == 7)
                e = ts(iw[:, 8 * tb:8 * tb + 8], bank[:, 0:8], 1.0 / 16, None, ALU.mult, None, r)
                G.give(j, e)
                t_iw.append(e)
                yield

        nat_t = []
        merge((gmlp_norm(), 8), (index_proj(), 14))
        t_oa = []
        for g in range(4):
            j, bank, fr = L.take()
            mv = av.rearrange("p (n g c) -> p n g c", g=4, c=64)[:, :, g, :]
            r = mm(bank[:, :].rearrange("p (n c) -> p n c", n=8), wst[:, 128 * g:128 * g + 128], mv, True, True,
                   fr, last, e1, inc=True)
            uv = au.rearrange("p (n g c) -> p n g c", g=4, c=64)[:, :, g, :]
            e = stt(uv, bank[:, :].rearrange("p (n c) -> p n c", n=8), bsc[:, g:g + 1], uv, ALU.add, ALU.mult,
                    r, e2, [t_ge["u", q] for q in range(8)])
            L.give(j, e)
            t_oa.append(e)
        for tb in range(8):
            mixw[tb, "a"] = dma(SP, mix_d[128 * tb:128 * tb + 128, 0:256], au[:, 256 * tb:256 * tb + 256], t_oa, store=True)
        gdone = [t_oa, r, [mixw[tb, "a"] for tb in range(8)]]
        V = Ring([res[:, 512 * i:512 * i + 512] for i in range(16)][8:] , gdone + [PE.now(), t_x])
        prh = [sb(sub, f"prh{i}", 512, FR) for i in range(2)]
        prl = [sb(sub, f"prl{i}", 512, FR) for i in range(2)]
        PR = Ring([0, 1])
        spill, spill_v = {}, {}

        stacks = [[nat[0], nat[1], qst[:, 0:1024], qst[:, 1024:2048], qst[:, 2048:3072], kst[:, :].bitcast(F32)], None]
        sfree = [None, None]
        ready = {}

        def load_head(n):
            qa, qb, ka, kb, kl, v = stacks[n % 2]
            d, fr = T["qk_d"], [sfree[n % 2], spill[n]]
            toks = []
            for dst, pieces in ((qa, ((0, 0), (1, 0))), (ka, ((2, 0), (2, 0))), (qb, ((1, 64), (0, 64))), (kb, ((2, 64), (2, 64)))):
                for at_, (w, r0) in enumerate(pieces):
                    toks.append(dma(SP, dst[64 * at_:64 * at_ + 64, :], d[4 * n + w, r0:r0 + 64, :], fr))
            toks.append(dma(SP, kl[:, :], d[4 * n + 3, :, :], fr))
            src = T["v_d"].rearrange("(b p) c -> p b c", p=128)[:, :, 128 * n:128 * n + 128]
            toks.append(dma(SP, v[:, :].rearrange("p (b c) -> p b c", b=8), src, fr,
                            [spill_v["b" if n < 4 else "c", tb] for tb in range(8)]))
            ready[n] = toks

        def project_all():
            us = [get("T", "w_in", j, OFF_BV) for j in range(4)]
            for tb in range(8):
                j, bank, r = gemm_t(us, xh, xl, tb, t_x, last=tb == 7)
                jv, vb, vf = V.take()
                e = copy_a(vb, bank[:, :], r, vf)
                G.give(j, e)
                spill_v["b", tb] = dma(SP, T["v_d"][128 * tb:128 * tb + 128, 0:512], vb, e, store=True)
                V.give(jv, spill_v["b", tb])
                yield
            us = [get("H", "w_in", j, OFF_CV) for j in range(2)]
            for tb in range(8):
                j, bank, r = gemm_t(us, xh, xl, tb, t_x, last=tb == 7, wide=256)
                jv, vb, vf = V.take()
                e = copy_a(vb[:, 0:256], bank[:, 0:256], r, vf)
                G.give(j, e)
                spill_v["c", tb] = dma(SP, T["v_d"][128 * tb:128 * tb + 128, 512:768], vb[:, 0:256], e, store=True)
                V.give(jv, spill_v["c", tb])
                yield
            for n in range(6):
                spill[n] = []
                for m in range(2):
                    off = (OFF_BQ, OFF_BK)[m] + 128 * n if n < 4 else (OFF_CQ, OFF_CK)[m] + 128 * (n - 4)
                    if m:
                        scale = 1.0
                    else:
                        scale = 2.0 ** (2 * (n + 1) - 3) if n < 4 else con[:, C_Q + n - 4:C_Q + n - 3]
                    u = get("F", "w_in", off)
                    for half in range(2):
                        hs = slice(512 * half, 512 * half + 512)
                        j, bank, r = gemm_f(u, xh, xl, 512 * half, 512, t_x)
                        jp, p, pf = PR.take()
                        a = copy_a(prh[p][:, :], bank[:, :], r, pf, scale=scale)
                        b = stt(prl[p][:, :], bank[:, :], scale, prh[p][:, :].bitcast(F32), ALU.mult, ALU.subtract, a, pf)
                        G.give(j, b)
                        d = [dma(SP, T["qk_d"][4 * n + 2 * m, :, hs], prh[p][:, :], a, store=True),
                             dma(SP, T["qk_d"][4 * n + 2 * m + 1, :, hs], prl[p][:, :], b, store=True)]
                        PR.give(jp, d)
                        spill[n] += d
                        if half:
                            done(u[0], r)
                        pdone[0] = so_far()
                        if n and len(t_score) == 6 and 0 not in ready:
                            sfree[0] = [PE.now(), list(t_score.values())]
                            load_head(0)
                        yield

        t_score = {}
        pdone = [None]

        def scores():
            for g in range(2):
                if g:
                    stack_queries(nat_t, [PE.now()])
                tq = list(t_qst)
                for i in range(2, 8):
                    o, ln = cols[i]
                    for c0 in range(0, ln, 512):
                        n = min(512, ln - c0)
                        prev = None
                        for h in range(4):
                            j, bank, fr = L.take()
                            q = qst[:, 768 * h + 128 * (i - 2):768 * h + 128 * (i - 1)]
                            r = mm(bank[:, 0:n], q, kst[:, c0:c0 + n], True, True, fr, tq, t_kst, inc=True)
                            jv, vb, vf = V.take()
                            a = act(vb[:, 0:n], bank[:, 0:n], ACT.Relu, r, vf)
                            L.give(j, a)
                            dst = score[:, o + c0:o + c0 + n]
                            w8 = iw[:, 8 * i + 4 * g + h:8 * i + 4 * g + h + 1]
                            if g == 0 and h == 0:
                                prev = ts(dst, vb[:, 0:n], w8, None, ALU.mult, None, a, t_iw)
                            else:
                                prev = stt(dst, vb[:, 0:n], w8, dst, ALU.mult, ALU.add, a, prev, part.get((i, c0)))
                            V.give(jv, prev)
                            yield
                        part[i, c0] = prev
                    if g:
                        t_score[i] = DV.put(lambda e, o=o, ln=ln: e.memset(score[0:64, o + ln - 64:o + ln], -BIG), (prev,))

        part = {}

        def index_and_select():
            yield from scores()
            yield from topk()

        tj = res[:, 0:512].bitcast(BF)
        tcum = [None, None]
        t_sel = {}

        def topk():
            cu, ci = cand[:, 0:6].bitcast(U32), cand[:, 0:6].bitcast(I32)
            cnt = cand[:, 8:14]
            rj = cand[:, 16:22]
            tmp6 = cand[:, 24:30]
            junk = tj

            def count(thr, waits, op=ALU.is_ge):
                ts_ = []
                for n, i in enumerate(range(2, 8)):
                    o, ln = cols[i]
                    t1 = thr if isinstance(thr, float) else thr[:, n:n + 1]
                    ts_.append(ts(junk[:, 0:ln], score[:, o:o + ln], t1, 0.0, op, ALU.add, waits, t_score[i], gdone,
                                  ts_[-1] if ts_ else None, acc=cnt[:, n:n + 1]))
                    if n % 2:
                        yield
                return ts_

            c = yield from count(0.0, None)
            p = ts(ci, cnt, 256.0, -1.0, ALU.is_lt, ALU.mult, c)
            p = ts(cu, cu, 1 << 30, None, ALU.bitwise_xor, None, p)
            for b in range(30, -1, -1):
                c = yield from count(cand[:, 0:6], (p,))
                r = ts(rj.bitcast(U32), cnt, 256.0, float(2 ** b), ALU.is_lt, ALU.mult, c)
                if b:
                    p = tt(cu, cu, rj.bitcast(U32), ALU.bitwise_xor, r)
                    p = ts(cu, cu, 1 << (b - 1), None, ALU.bitwise_xor, None, p)
                else:
                    p = tt(cu, cu, rj.bitcast(U32), ALU.bitwise_xor, r)
            c = yield from count(cand[:, 0:6], (p,), ALU.is_gt)
            need = ts(tmp6, cnt, -1.0, 256.0, ALU.mult, ALU.add, c)
            cum, cf = tcum[0], tcum[1]
            prev = None
            for n, i in enumerate(range(2, 8)):
                o, ln = cols[i]
                sc = score[:, o:o + ln]
                thr = cand[:, n:n + 1]
                a = ts(junk[:, 0:ln], sc, thr, None, ALU.is_equal, None, p, need, prev)
                b = DV.put(lambda e, ln=ln: e.tensor_tensor_scan(cum[:, 0:ln], junk[:, 0:ln], junk[:, 0:ln], 0.0,
                                                                 ALU.add, ALU.bypass), (a, cf, prev))
                d = stt(junk[:, 0:ln], cum[:, 0:ln], tmp6[:, n:n + 1], junk[:, 0:ln], ALU.is_le, ALU.mult, b)
                f = stt(sc, sc, thr, junk[:, 0:ln], ALU.is_gt, ALU.add, d)
                g = ts(sc, sc, -1.0, BIG, ALU.add, ALU.mult, f)
                prev = tt(sc, sc, nd[:, 896 - 128 * i:1024], ALU.add, g, t_nd)
                t_sel[i] = prev
                yield


        G.free += [(3 + j, toks) for j, toks in X.free]
        G.bufs = G.bufs + X.bufs
        ixs = index_and_select()
        pj = project_all()
        steps = [(ixs, 128), (pj, 40)]
        merge_until(pj, steps)
        snap = pdone[0]
        sub.close()
        sx.close()

        L = Ring([banks[i] for i in (0, 3, 4, 5)], snap)
        X = Ring([banks[i] for i in (1, 2, 6, 7)], snap)
        sub = ExitStack()
        V = Ring([sb(sub, f"vals{i}", 1024) for i in range(6)], snap)
        PT = Ring([sb(sub, f"pt{i}", 1024) for i in range(3)], snap)
        tcum[0], tcum[1] = sb(sub, "tcum", 1024), snap
        osb = sb(sub, "osb", 1024)
        stacks[1] = [sb(sub, x, 1024, FR) for x in ("qa", "qb", "ka", "kb", "kl")] + [sb(sub, "v1", 1024)]
        sfree[1] = snap
        if 0 not in ready:
            sfree[0] = snap
            load_head(0)
        sg = sb(sub, "sg", 128)
        lamt = sb(sub, "lamt", 264)
        t_sg = dma(SP, sg[:, :], T["diff_subln_g"].partition_broadcast(128), snap)
        t_l = [dma(SP, lamt[:, 64 * n:64 * n + 64], T[nm].partition_broadcast(128), snap)
               for n, nm in enumerate(("lam_q1", "lam_k1", "lam_q2", "lam_k2"))]
        a = ttr(lamt[:, 0:64], lamt[:, 0:64], lamt[:, 64:128], 1.0, 0.0, ALU.mult, ALU.add, lamt[:, 256:257], t_l)
        b = ttr(lamt[:, 128:192], lamt[:, 128:192], lamt[:, 192:256], 1.0, 0.0, ALU.mult, ALU.add, lamt[:, 257:258], t_l)
        c = act(lamt[:, 258:260], lamt[:, 256:258], ACT.Exp, a, b)
        d = tt(lamt[:, 260:261], lamt[:, 259:260], lamt[:, 258:259], ALU.subtract, c)
        t_lam = ts(lamt[:, 261:262], lamt[:, 260:261], -LAM_INIT, None, ALU.add, None, d)
        nlam = lamt[:, 261:262]

        def softmax(i, n, m, bias, slope, wb):
            ln = 128 * (i + 1)
            st_ = stacks[n % 2]
            q, k, kl, w = st_[m], st_[2 + m], st_[4], ready[n]
            pr = slice(64 * m, 64 * m + 64)
            jv, vb, vf = V.take()
            mx = small(4)
            prev = None
            for c0 in range(0, ln, 512):
                n = min(512, ln - c0)
                j, bank, fr = L.take()
                mm(bank[:, 0:n], q[:, 128 * i:128 * i + 128], k[:, c0:c0 + n], True, False, fr, w)
                r = mm(bank[:, 0:n], q[pr, 128 * i:128 * i + 128], kl[pr, c0:c0 + n], False, True, inc=True)
                z = c0 // 512
                prev = ttr(vb[:, c0:c0 + n], bank[:, 0:n], bias[:, c0:c0 + n], 1.0, -3.0e38 if z == 0 else mx[:, 0:1],
                           ALU.add, ALU.max, mx[:, z:z + 1], r, vf, prev, wb)
                L.give(j, prev)
            m = mx[:, z:z + 1]
            nb = ts(mx[:, 2:3], m, -slope, None, ALU.mult, None, prev)
            e = act(vb[:, 0:ln], vb[:, 0:ln], ACT.Exp, nb, prev, bias=mx[:, 2:3], scale=slope, acc=mx[:, 3:4])
            return jv, vb, e, mx[:, 3:4]

        def inverse(x):
            rc = small(1)
            return rc, DV.put(lambda en: en.reciprocal(rc, x[3]), (x[2],))

        def over(i, vb, w):
            jp, pb, pf = PT.take()
            toks = []
            for c0 in range(0, i + 1, 4):
                m = min(4, i + 1 - c0)
                j, bank, fr = X.take()
                for b in range(m):
                    t = tr(bank[:, 128 * b:128 * b + 128], vb[:, 128 * (c0 + b):128 * (c0 + b) + 128], idn, w, fr, inc=b == m - 1)
                e = copy_a(pb[:, 128 * c0:128 * (c0 + m)], bank[:, 0:128 * m], t, pf)
                X.give(j, e)
                toks.append(e)
            return jp, pb, toks, t

        def weigh(i, p, v, vw, cols_v, obuf, scale, wo):
            jp, pb, toks, _ = p
            j, bank, fr = X.take()
            nv = cols_v[1] - cols_v[0]
            for b in range(i + 1):
                r = mm(bank[:, 0:nv], pb[:, 128 * b:128 * b + 128], v[:, 128 * b + cols_v[0]:128 * b + cols_v[1]],
                       b == 0, b == i, toks, vw, fr, inc=b == i)
            PT.give(jp, r)
            e = copy_a(obuf, bank[:, 0:nv], r, wo, scale=scale)
            X.give(j, e)
            return e, r

        ofree = [snap] * 8

        def attend_b():
            fresh, whole, turned_ = [], [], []

            def turn_b():
                h, i, a, v, w, t4 = whole.pop(0)
                p = over(i, a[1], t4)
                V.give(a[0], p[3])
                turned_.append((h, i, a, v, w, p))

            def combine(h, i, a, b, w):
                ln = 128 * (i + 1)
                rb, tb_ = inverse(b)
                c2 = small(1)
                t2 = stt(c2, rb, nlam, a[3], ALU.mult, ALU.mult, tb_, a[2], t_lam)
                t4 = stt(a[1][:, 0:ln], b[1][:, 0:ln], c2, a[1][:, 0:ln], ALU.mult, ALU.add, t2, b[2], a[2])
                V.give(b[0], t4)
                whole.append((h, i, a, stacks[h % 2][5], w, t4))

            for h in range(4):
                slope = 2.0 ** (-2 * (h + 1))
                for i in range(8):
                    bias = nd[:, 896 - 128 * i:1024]
                    a = softmax(i, h, 0, bias, slope, t_nd)
                    yield
                    b = softmax(i, h, 1, bias, slope, t_nd)
                    fresh.append((h, i, a, b, ready[h]))
                    yield
                    if len(fresh) > 1:
                        combine(*fresh.pop(0))
                        yield
                    if turned_:
                        finish_b(*turned_.pop(0))
                        yield
                    if len(whole) > 1:
                        turn_b()
                        yield
            combine(*fresh.pop(0))
            while whole or turned_:
                if turned_:
                    finish_b(*turned_.pop(0))
                if whole:
                    turn_b()
                yield

        oe = []

        def finish_b(h, i, a, v, w, p):
            ra, ta = inverse(a)
            e, r = weigh(i, p, v, w, (0, 128), osb[:, 128 * i:128 * i + 128], ra, (ofree[i], ta))
            oe.append(e)
            if i < 7:
                return
            sfree[h % 2] = (r, PE.now())
            load_head(h + 2)
            ss = small(24)
            jv, vb, vf = V.take()
            d = tt(vb[:, :], osb[:, :], osb[:, :], ALU.mult, oe, vf)
            d = DV.put(lambda en: en.tensor_reduce(ss[:, 0:8], vb[:, :].rearrange("p (n c) -> p n c", n=8), AX.X, ALU.add), (d,))
            V.give(jv, d)
            d = ts(ss[:, 0:8], ss[:, 0:8], 1.0 / 128, LN_EPS, ALU.mult, ALU.add, d)
            d = act(ss[:, 8:16], ss[:, 0:8], ACT.Sqrt, d)
            d = DV.put(lambda en: en.reciprocal(ss[:, 16:24], ss[:, 8:16]), (d,))
            d = ts(ss[:, 16:24], ss[:, 16:24], 1.0 - LAM_INIT, None, ALU.mult, None, d)
            for i in range(8):
                ob = osb[:, 128 * i:128 * i + 128]
                e = stt(ob, ob, ss[:, 16 + i:17 + i], sg[:, :], ALU.mult, ALU.mult, d, t_sg)
                mixw[i, h] = dma(SP, mix_d[128 * i:128 * i + 128, 256 + 128 * h:384 + 128 * h], ob, e, store=True)
                ofree[i] = mixw[i, h]
            oe.clear()

        t_mix = [None] * 8

        def attend_c():
            pend, turned_ = [], []

            def turn_c():
                pair, i, hh, a, v, w = pend.pop(0)
                p = over(i, a[1], a[2])
                V.give(a[0], p[3])
                turned_.append((pair, i, hh, a, v, w, p))

            for pair in range(2):
                n = 4 + pair
                v = stacks[n % 2][5]
                for i in range(8):
                    bias = nd[:, 896 - 128 * i:1024] if i < 2 else score[:, cols[i][0]:cols[i][0] + cols[i][1]]
                    for hh in range(2):
                        slope = 2.0 ** (-2 * (2 * pair + hh + 1))
                        a = softmax(i, n, hh, bias, slope, t_sel.get(i, t_nd))
                        pend.append((pair, i, hh, a, v, ready[n]))
                        if turned_:
                            finish_c(*turned_.pop(0))
                        if len(pend) > 4:
                            turn_c()
            while pend or turned_:
                if turned_:
                    finish_c(*turned_.pop(0))
                if pend:
                    turn_c()

        def finish_c(pair, i, hh, a, v, w, p):
            ra, ta = inverse(a)
            e, r = weigh(i, p, v, w, (64 * hh, 64 * hh + 64),
                                osb[:, 128 * i + 64 * hh:128 * i + 64 * hh + 64], ra, (ofree[i], ta))
            oe.append(e)
            if hh:
                mixw[i, "c", pair] = dma(SP, mix_d[128 * i:128 * i + 128, 768 + 128 * pair:896 + 128 * pair],
                                         osb[:, 128 * i:128 * i + 128], oe, store=True)
                ofree[i] = mixw[i, "c", pair]
                oe.clear()

        load_head(1)
        merge((attend_b(), 125), (ixs, 52))
        attend_c()
        snap = so_far()
        sub.close()
        ph.close()

        G = Ring(banks[0:5], snap)
        X = Ring(banks[5:8], snap)

        def bc(ctx, name, src, *w):
            t = sb(ctx, name, 1024)
            return t, dma(SP, t[:, :], src.partition_broadcast(128), *w)

        def mix_gemm(wname, tw, finish, after):
            for n in range(2):
                us = [get("T", wname, j, 512 * n) for j in range(4)]
                for tb in range(8):
                    j, bank, r = gemm_t(us, xh, xl, tb, tw[tb], last=tb == 7)
                    G.give(j, finish(tb, n, bank, r))
                    if n == 1:
                        after(tb, r)

        mod_w = []

        def modulate(acc, snap):
            free = [snap, snap]
            stored = []

            def over(n, d):
                j, bank, fr = X.take()
                r = mm(bank[0:1, :], neg1[:, 0:1], acc[n % 2][:, :], True, True, d, fr, inc=True)
                return n, j, bank, r

            def keep(n, j, bank, r):
                e = ts(acc[n % 2][0:1, :], bank[0:1, :], -1.0, None, ALU.mult, None, r)
                X.give(j, e)
                free[n % 2] = dma(SP, T["vec_d"][0:1, 512 * n:512 * n + 512], acc[n % 2][0:1, :], e, store=True)
                stored.append(free[n % 2])

            whole, summed = None, None
            for n in range(12):
                for q in range(4):
                    u = get("R", "w_cond_2", q, 512 * n)
                    if summed:
                        keep(*summed)
                        summed = None
                    if whole:
                        summed = over(*whole)
                        whole = None
                    a = acc[n % 2]
                    for k in range(2):
                        w = u[1][:, 512 * k:512 * k + 512]
                        c = cc[:, 2 * q + k:2 * q + k + 1]
                        if q == 0 and k == 0:
                            d = ts(a[:, :], w, c, None, ALU.mult, None, u[3], t_cc, free[n % 2])
                        else:
                            d = stt(a[:, :], w, c, a[:, :], ALU.mult, ALU.add, u[3], d)
                    done(u[0], d)
                    if q == 3:
                        whole = (n, d)
                    if n < 11 or q < 3:
                        yield
            keep(*over(*whole))
            rows = T["vec_d"][0, :].rearrange("(p c) -> p c", p=128)
            t = dma(SP, acc[0][:, 0:48], rows, stored)
            b = dma(SP, acc[0][:, 64:112], T["b_cond_2"].rearrange("(p c) -> p c", p=128), stored)
            t = tt(acc[0][:, 0:48], acc[0][:, 0:48], acc[0][:, 64:112], ALU.add, t, b)
            mod_w.append(dma(SP, rows, acc[0][:, 0:48], t, store=True))
            yield

        def ffn(wg, wu, up_off, wd, tw, acc, acc_tok, snap, fresh, between, after, begun=None):
            sa, sc_ = ExitStack(), ExitStack()
            sil = [sb(sa, f"sil{i}" + wg, 512) for i in range(2)]
            SR = Ring(sil, snap)
            hh, hl = [sb(sa, "hh" + wg, 4096, FR)], [sb(sa, "hl" + wg, 4096, FR)]
            hh.append(sb(sc_, "hi" + wg, 2048, FR))
            hl.append(sb(sc_, "hm" + wg, 2048, FR))
            mod = iter(())
            if wg == "w_gu":
                mod = modulate([sb(sc_, f"macc{i}", 512) for i in range(2)], snap)
            hfr = snap
            for a, kk in CHUNKS:
                if a == CHUNKS[-1][0]:
                    sc_.close()
                    between(sa, so_far())
                ht = []
                for f in range(a, a + kk):
                    ug = get("F", wg, 128 * f)
                    uu = get("F", wu, up_off + 128 * f)
                    for half in range(2):
                        w = tw[4 * half:4 * half + 4]
                        jg, bg, rg = gemm_f(ug, xh, xl, 512 * half, 512, w)
                        ju, bu, ru = gemm_f(uu, xh, xl, 512 * half, 512, w)
                        if begun and f == half == 0:
                            begun(8, None)
                        s, sbuf, sf = SR.take()
                        e = act(sbuf[:, :], bg[:, :], ACT.Silu, rg, sf)
                        G.give(jg, e)
                        m = tt(sbuf[:, :], sbuf[:, :], bu[:, :], ALU.mult, e, ru)
                        G.give(ju, m)
                        p = (f - a) // 4
                        o = 1024 * ((f - a) % 4) + 512 * half
                        c = copy_a(hh[p][:, o:o + 512], sbuf[:, :], m, hfr)
                        d = tt(hl[p][:, o:o + 512], sbuf[:, :], hh[p][:, o:o + 512].bitcast(F32), ALU.subtract, c, hfr)
                        SR.give(s, d)
                        ht.append((c, d))
                    done(ug[0], rg)
                    done(uu[0], ru)
                    if a < CHUNKS[-1][0]:
                        next(mod, None)
                fdone = ru
                if a == CHUNKS[-1][0]:
                    us = [[get("T", wd, j, 512 * n) for j in range(a // 2, (a + kk) // 2)] for n in range(2)]
                    for tb in range(8):
                        for n in range(2):
                            j, bank, r = gemm_t(us[n], hh, hl, tb, ht, last=tb == 7)
                            dst = acc[:, 1024 * tb + 512 * n:1024 * tb + 512 * n + 512]
                            e = tt(dst, bank[:, :], dst, ALU.add, r, acc_tok[tb])
                            acc_tok[tb] = (acc_tok[tb], e)
                            G.give(j, e)
                        after(tb, fdone)
                    break
                for n in range(2):
                    us = [get("T", wd, j, 512 * n) for j in range(a // 2, (a + kk) // 2)]
                    for tb in range(8):
                        j, bank, r = gemm_t(us, hh, hl, tb, ht, last=tb == 7)
                        dst = acc[:, 1024 * tb + 512 * n:1024 * tb + 512 * n + 512]
                        if fresh and a == 0:
                            e = copy_v(dst, bank[:, :], r, acc_tok[tb])
                        else:
                            e = tt(dst, bank[:, :], dst, ALU.add, r, acc_tok[tb])
                        acc_tok[tb] = (acc_tok[tb], e)
                        G.give(j, e)
                        if tb < 5:
                            next(mod, None)
                hfr = (r,)
            after(8, None)
            return sa

        ph = ExitStack()
        xh, xl = sb(ph, "yh", 8192, FR), sb(ph, "yl", 8192, FR)
        sub = ExitStack()
        ms = Ring([sb(sub, f"ms{i}", 1024) for i in range(4)], snap)
        for tb in range(8):
            j, buf, fr = ms.take()
            d = dma(SP, buf[:, :], mix_d[128 * tb:128 * tb + 128, :], fr, [x for key, x in mixw.items() if key[0] == tb])
            t_mix[tb] = turn(buf, tb, xh, xl, d, snap)
            ms.give(j, t_mix[tb], PE.now())
        g1, tg1 = bc(sub, "g1", T["ln1_g"], snap)
        b1, tb1 = bc(sub, "b1", T["ln1_b"], snap)
        t_r = [dma(SP, block(tb), xd[128 * tb:128 * tb + 128, :], snap) for tb in range(8)]

        def fin1(tb, n, bank, r):
            dst = block(tb)[:, 512 * n:512 * n + 512]
            e = stt(dst, dst, ALPHA, bank[:, :], ALU.mult, ALU.add, r, t_r[tb])
            t_r[tb] = (t_r[tb], e)
            return e

        ty = [None] * 8
        late = []

        def norm1(tb, r):
            if late:
                b, t, pe = late.pop()
                ty[b] = turn(block(b), b, xh, xl, t, pe)
                t_r[b] = copy_a(block(b), block(b), PE.now(), t, scale=ALPHA)
            if tb < 8:
                src = block(tb)
                mu, rs, t = mean_rstd(src, LN_EPS, t_r[tb])
                t = ts(src, src, mu, rs, ALU.subtract, ALU.mult, t)
                t = tt(src, src, g1[:, :], ALU.mult, t, tg1)
                t = tt(src, src, b1[:, :], ALU.add, t, tb1)
                late.append((tb, t, r))

        mix_gemm("w_out", t_mix, fin1, norm1)
        snap = so_far()
        sub.close()

        vec = {}

        def row(name, dst, n, *w):
            return dma(SP, dst, T["vec_d"][0, 1024 * n:1024 * n + 1024].partition_broadcast(128), mod_w, *w)

        def vectors2(ctx, snap):
            g2, t2 = bc(ctx, "g2", T["ln2_g"], snap)
            b2, t3 = bc(ctx, "b2", T["ln2_b"], snap)
            gp, t4 = bc(ctx, "gp", T["g_mix_pre_2"], snap)
            sh = sb(ctx, "sh", 1024)
            t5 = row("scale", sh[:, :], 1, snap)
            t6 = stt(gp[:, :], sh[:, :], 1.0, gp[:, :], ALU.add, ALU.mult, t4, t5)
            t7 = row("shift", sh[:, :], 0, t6)
            vec["2"] = (g2, b2, gp, sh, t2, t3, t6, t7)
            vec["junk"] = [sb(ctx, "sq2", 1024, BF), None]

        t_h = [None] * 8
        t_x2 = []

        def norm2(tb, r):
            g2, b2, gp, sh, t2, t3, t6, t7 = vec["2"]

            def turned_around():
                b, t, pe = late.pop(0)
                t_h[b] = turn(block(b), b, xh, xl, t, pe)

            def modulated():
                b, pe, ss, a, d = squared.pop(0)
                rr, t = rms_of(ss, EPS, a)
                t = stt(block(b), block(b), rr, gp[:, :], ALU.mult, ALU.mult, t, t6, d)
                late.append((b, tt(block(b), block(b), sh[:, :], ALU.add, t, t7, q=PO), pe))

            if len(late) > 1:
                turned_around()
            squared = []
            if half_way:
                b, pe, t, d = half_way.pop(0)
                ss = small(1)
                a = act(vec["junk"][0][:, :], block(b), ACT.Square, t, vec["junk"][1], acc=ss)
                vec["junk"][1] = a
                squared.append((b, pe, ss, a, d))
            if tb < 8:
                src = block(tb)
                mu, rs, t = mean_rstd(src, LN_EPS, t_r[tb])
                t = ts(src, src, mu, rs, ALU.subtract, ALU.mult, t)
                t = tt(src, src, g2[:, :], ALU.mult, t, t2)
                if squared:
                    modulated()
                t = tt(src, src, b2[:, :], ALU.add, t, t3, q=PO)
                d = dma(SP, x2_d[128 * tb:128 * tb + 128, :], src, t, store=True)
                t_x2.append(d)
                half_way.append((tb, r, t, d))
                return
            modulated()
            while late:
                turned_around()

        half_way = []
        sa = ffn("w_gu", "w_gu", FF, "w_down", ty, res, t_r, snap, False, vectors2, norm2, norm1)
        snap = so_far()
        sa.close()
        turned = PE.now()

        sub = ExitStack()
        vt = sb(sub, "vt", 4096)
        sq = ExitStack()
        ut = sb(sq, "ut", 4096)
        bd = sb(sq, "bd", 1536)
        wp = sb(sq, "wp", 512)
        pl = [sb(sq, f"pl{i}", 1024) for i in range(2)]
        ps = sb(sq, "ps", 8)
        ps4 = sb(sq, "ps4", 128, p=4)
        t_bd = dma(SP, bd[:, :], T["bands"], snap)
        t_wp = dma(SP, wp[:, :].rearrange("p (g d) -> p g d", g=4), T["w_pool_2"].rearrange("g c d -> c g d"), snap)
        d = dma(SP, ps4[:, :], T["pool_scale_2"].rearrange("(g p) -> g p", p=128), snap)
        tv, tu = [], []
        for n, (dst, toks) in enumerate(((vt, tv), (ut, tu))):
            us = [get("T", "w_in_2", j, 1024 + 512 * n) for j in range(4)]
            for tb in range(8):
                j, bank, r = gemm_t(us, xh, xl, tb, t_h[tb], last=tb == 7)
                e = copy_a(dst[:, 512 * tb:512 * tb + 512], bank[:, :], r, snap)
                G.give(j, e)
                toks.append(e)
        j, bank, fr = X.take()
        t = tr(bank[:, 0:4], ps4[:, :], idn[0:4, 0:4], d, fr, inc=True)
        t_ps = copy_v(ps[:, 0:4], bank[:, 0:4], t, snap)
        X.give(j, t_ps)
        snap_v = snap
        plf = [snap, snap]
        t_pool = {}

        def pooling():
            for g in range(4):
                p_ = pl[g % 2]
                te = []
                for c in range(2):
                    j, bank, fr = X.take()
                    for b in range(4 * c, 4 * c + 4):
                        o = bank[:, 128 * (b % 4):128 * (b % 4) + 128]
                        ub = ut[:, 512 * b + 128 * g:512 * b + 128 * g + 128]
                        band = bd[:, 384 * g:384 * g + 384]
                        if b == 0:
                            r = mm(o, ub, band[:, 256:384], True, True, tu, t_bd, fr, inc=True)
                        else:
                            up = ut[:, 512 * (b - 1) + 128 * g:512 * (b - 1) + 128 * g + 128]
                            mm(o, ub, band[:, 0:128], True, False, tu, t_bd, fr)
                            r = mm(o, up, band[:, 128:256], False, True, inc=True)
                    e = copy_v(p_[:, 512 * c:512 * c + 512], bank[:, :], r, plf[g % 2])
                    X.give(j, e)
                    te.append(e)
                    yield
                for c in range(2):
                    j, bank, fr = X.take()
                    r = mm(bank[:, :], wp[:, 128 * g:128 * g + 128], p_[:, 512 * c:512 * c + 512], True, True,
                           te, t_wp, fr, inc=True)
                    o = 1024 * (4 + g) + 512 * c
                    e = ts(res[:, o:o + 512], bank[:, :], ps[:, g:g + 1], None, ALU.mult, None, r, t_ps, t_x2, turned)
                    X.give(j, e)
                    t_pool[g, c] = e
                plf[g % 2] = r
                yield

        run(pooling())
        snap = so_far()
        sq.close()
        sq = ExitStack()
        qk = [[sb(sq, f"s{x}{i}", 1024) for x in "qk"] for i in range(2)]
        lt = [sb(sq, f"lt{i}", 512) for i in range(2)]
        spb = [sb(sq, f"sp{i}", 512) for i in range(4)]
        wt = [sb(sq, f"wt{i}", 512) for i in range(3)]
        run_s = [sb(sq, f"rs{i}", 512) for i in range(2)]
        zb = sb(sq, "zb", 512, BF)
        t_zb = DV.put(lambda e: e.memset(zb[:, :], 0.0), (snap,))
        LT, SPR, WT = Ring(lt, snap), Ring(spb, snap), Ring(wt, snap)
        G, Z, O = Ring(banks[0:2], snap), Ring(banks[2:6], snap), Ring(banks[6:8], snap)
        AC.put(lambda e: e.preload_act_table_set("natural_log_exp_and_others"), (), inc=False)
        sfree = [snap, snap]
        sready = {}
        last_p = [None]

        def project2(h):
            toks = []
            for n, dst in enumerate(qk[h % 2]):
                u = get("F", "w_in_2", 512 * n + 128 * h)
                for half in range(2):
                    j, bank, r = gemm_f(u, xh, xl, 512 * half, 512, t_h)
                    e = copy_a(dst[:, 512 * half:512 * half + 512], bank[:, :], r, sfree[h % 2],
                               scale=0.125 if n == 0 else 1.0)
                    G.give(j, e)
                    toks.append(e)
                    yield
                done(u[0], r)
            last_p[0] = r
            sready[h] = toks

        def stick(h, hh, toks_out):
            q, k = qk[h % 2]
            pr = slice(64 * hh, 64 * hh + 64)
            w = sready[h]
            rs = run_s[hh]
            for c in range(2):
                jo, ob, fo = O.take()
                mm(ob[0:64, :], zb[:, 0:64], zb[:, :], True, False, t_zb, fo, skip=True)
                z0 = DV.put(lambda e: e.memset(rs[:, :], 0.0), (rfree[hh],))
                state = {"sum": z0}

                def first(b):
                    t0 = max(128 * b, 512 * c)
                    n = 512 * (c + 1) - t0
                    jz, z, fz = Z.take()
                    r = mm(z[:, 0:n], k[pr, 128 * b:128 * b + 128], q[pr, t0:t0 + n], True, False, fz, w, inc=True, skip=True)
                    jl, l, fl = LT.take()
                    a = act(l[:, 0:n], z[:, 0:n], ACT.Abs, r, fl)
                    a = act(l[:, 0:n], l[:, 0:n], ACT.Exp, a, scale=-1.0)
                    a = act(l[:, 0:n], l[:, 0:n], ACT.Ln, a, bias=1.0)
                    js, s_, fs = SPR.take()
                    d = stt(s_[:, 0:n], z[:, 0:n], 0.0, l[:, 0:n], ALU.max, ALU.add, a, fs)
                    LT.give(jl, d)
                    m = d
                    if 128 * b >= 512 * c:
                        m = PO.put(lambda e: e.affine_select(out=s_[:, 0:128], in_=s_[:, 0:128], compare_op=ALU.is_gt,
                                                             fill=0.0, base=0, pattern=[[1, 128]],
                                                             channel_multiplier=-1), (d,))
                    return b, t0, n, jz, z, js, s_, m, d

                def second(x):
                    b, t0, n, jz, z, js, s_, m, d = x
                    o0 = t0 - 512 * c
                    top_b = 4 * c + 3
                    r = mm(z[:, 0:n], negu, s_[:, 0:n], False, b == top_b, m, d, inc=True, skip=True)
                    if b != top_b:
                        r = mm(z[:, 0:n], neg1, rs[:, o0:512], False, True, state["sum"], inc=True, skip=True)
                    if b:
                        state["sum"] = tt(rs[:, o0:512], rs[:, o0:512], s_[:, 0:n], ALU.add, r, m, state["sum"], q=PO)
                        SPR.give(js, state["sum"])
                    else:
                        SPR.give(js, r)
                        rfree[hh] = r
                    jw, wb, fw = WT.take()
                    e = act(wb[:, 0:n], z[:, 0:n], ACT.Exp, r, fw)
                    Z.give(jz, e)
                    if 128 * b >= 512 * c:
                        e = PO.put(lambda en: en.affine_select(out=wb[:, 0:128], in_=wb[:, 0:128], compare_op=ALU.is_gt,
                                                               fill=0.0, base=0, pattern=[[1, 128]],
                                                               channel_multiplier=-1), (e,))
                    return b, o0, n, jw, wb, e

                def third(x):
                    b, o0, n, jw, wb, e = x
                    r = mm(ob[0:64, o0:512], vt[:, 512 * b + 128 * h + 64 * hh:512 * b + 128 * h + 64 * hh + 64],
                           wb[:, 0:n], False, b == 0, e, tv, inc=True, skip=True)
                    WT.give(jw, r)
                    return r

                x = first(4 * c + 3)
                yield
                late_w = None
                for b in range(4 * c + 2, -1, -1):
                    y = first(b)
                    if late_w:
                        third(late_w)
                    z = second(x)
                    x, late_w = y, z
                    yield
                third(late_w)
                z = second(x)
                yield
                r = third(z)
                e = copy_v(res[pr, 1024 * h + 512 * c:1024 * h + 512 * c + 512], ob[0:64, :], r, t_x2, turned)
                O.give(jo, e)
                toks_out.append(e)
                yield
            last_r[0] = r

        rfree = [snap, snap]
        last_r = [None]
        t_att = []
        halves = [None] * 8

        def split(k, *w):
            src = res[:, 1024 * k:1024 * k + 1024]
            a = copy_a(xh[:, 1024 * k:1024 * k + 1024], src, w, proj_done[0])
            b = tt(xl[:, 1024 * k:1024 * k + 1024], src, xh[:, 1024 * k:1024 * k + 1024].bitcast(F32), ALU.subtract, a, q=PO)
            halves[k] = (a, b)

        proj_done = [None]

        def splits():
            for g in range(4):
                split(4 + g, t_pool[g, 0], t_pool[g, 1])
                yield
            for h in range(3):
                split(h, t_att3)
                yield

        run(project2(0))
        for h in range(4):
            gens = [(stick(h, 0, t_att), 16), (stick(h, 1, t_att), 16)]
            if h < 3:
                gens.append((project2(h + 1), 5))
            else:
                proj_done[0] = last_p[0]
                t_att3 = list(t_att)
                gens.append((splits(), 7))
            merge(*gens)
            sfree[h % 2] = (last_r[0], PE.now())
        split(3, t_att)
        snap = so_far()
        sq.close()
        sub.close()
        sub = ExitStack()
        G = Ring(banks[0:5], snap)
        X = Ring(banks[5:8], snap)
        gm, sf, gs, gt = [sb(sub, n, 1024) for n in ("gm", "sf", "gs", "gt")]
        t1, t2, t3 = row("", gm[:, :], 2, snap), row("", sf[:, :], 3, snap), row("", gs[:, :], 4, snap)
        d = dma(SP, gt[:, :], T["g_mix_post_2"].partition_broadcast(128), snap)
        m1 = tt(gm[:, :], gm[:, :], gt[:, :], ALU.mult, t1, d)
        d = dma(SP, gt[:, :], T["g_ffn_pre_2"].partition_broadcast(128), m1)
        m3 = stt(gs[:, :], gs[:, :], 1.0, gt[:, :], ALU.add, ALU.mult, t3, d)
        xb = [sb(sub, f"xb{i}", 1024) for i in range(3)]
        junk = [sb(sub, "sq3", 1024, BF), snap]
        xbf = [snap] * 3
        t_m = [halves] * 8
        ty = [None] * 8
        t_x3 = []

        def fin2(tb, n, bank, r):
            e = copy_a(block(tb)[:, 512 * n:512 * n + 512], bank[:, :], r, t_m[tb])
            t_m[tb] = (t_m[tb], e)
            return e

        late.clear()

        def norm3(tb, r):
            if late:
                b, t, pe = late.pop()
                ty[b] = turn(xb[b % 3], b, xh, xl, t, pe)
                xbf[b % 3] = PE.now()
            if tb < 8:
                src, x_ = block(tb), xb[tb % 3]
                d = dma(SP, x_[:, :], x2_d[128 * tb:128 * tb + 128, :], xbf[tb % 3], t_x2)
                rr, t, junk[1] = rms(src, EPS, junk[0][:, :], t_m[tb], junk[1])
                t = stt(src, src, rr, gm[:, :], ALU.mult, ALU.mult, t, m1)
                t = tt(src, src, x_[:, :], ALU.add, t, d)
                t_x3.append(dma(SP, mix_d[128 * tb:128 * tb + 128, :], src, t, store=True))
                rr, t2_, junk[1] = rms(src, EPS, junk[0][:, :], t, junk[1])
                t = stt(x_[:, :], src, rr, gs[:, :], ALU.mult, ALU.mult, t2_, m3, t)
                t = tt(x_[:, :], x_[:, :], sf[:, :], ALU.add, t, t2)
                late.append((tb, t, r))
                t_rd[tb] = t

        t_rd = [None] * 8
        mix_gemm("w_out_2", [halves] * 8, fin2, norm3)
        norm3(8, None)
        snap = so_far()
        sub.close()
        t_acc = [(t_x3[tb], t_rd[tb]) for tb in range(8)]

        def vectors3(ctx, snap):
            gf, gq = sb(ctx, "gf", 1024), sb(ctx, "gq", 1024)
            xc = [gq, sb(ctx, "xc1", 1024), sb(ctx, "xc2", 1024)]
            t = row("", gf[:, :], 5, snap)
            t2 = dma(SP, gq[:, :], T["g_ffn_post_2"].partition_broadcast(128), snap)
            t3 = tt(gf[:, :], gf[:, :], gq[:, :], ALU.mult, t, t2)
            vec["3"] = (gf, xc, [t3, snap, snap], t3)
            vec["junk"] = [sb(ctx, "sq4", 1024, BF), snap]

        def norm4(tb, r):
            gf, xc, free, tg = vec["3"]
            if tb == 8:
                return
            src, x_ = block(tb), xc[tb % 3]
            d = dma(SP, x_[:, :], mix_d[128 * tb:128 * tb + 128, :], free[tb % 3], t_x3)
            rr, t, vec["junk"][1] = rms(src, EPS, vec["junk"][0][:, :], t_acc[tb], vec["junk"][1])
            t = stt(src, src, rr, gf[:, :], ALU.mult, ALU.mult, t, tg)
            t = tt(src, src, x_[:, :], ALU.add, t, d)
            free[tb % 3] = t
            dma(SP, out[128 * tb:128 * tb + 128, :], src, t, store=True)

        sa = ffn("w_gate_2", "w_up_2", 0, "w_down_2", ty, res, t_acc, snap, True, vectors3, norm4)
        sa.close()
        ph.close()
        SPw = [*drams]
        SP.items.append((flat(SPw, {}), None, None, 0))
        block = top.enter_context(nc.Block())

        @block.sync
        def _(e):
            SP.emit(e)

        @block.scalar
        def _(e):
            AC.emit(e)

        @block.vector
        def _(e):
            DV.emit(e)

        @block.gpsimd
        def _(e):
            PO.emit(e)

        @block.tensor
        def _(e):
            PE.emit(e)


_NAMES = ['x', 'w_in', 'gmlp_w_s', 'gmlp_b_s', 'gmlp_ln_g', 'gmlp_ln_b', 'lam_q1', 'lam_k1', 'lam_q2', 'lam_k2',
          'diff_subln_g', 'w_out', 'ln1_g', 'ln1_b', 'w_gu', 'w_down', 'ln2_g', 'ln2_b', 'c_2', 'w_cond_2',
          'b_cond_2', 'g_mix_pre_2', 'g_mix_post_2', 'w_in_2', 'w_pool_2', 'pool_scale_2', 'w_out_2',
          'g_ffn_pre_2', 'g_ffn_post_2', 'w_gate_2', 'w_up_2', 'w_down_2']


def kernel(**inputs):
    import concourse.bacc as _bacc
    from concourse.bass_utils import run_bass_kernel_spmd as _run

    nc = _bacc.Bacc("TRN2", target_bir_lowering=False, num_devices=1)
    arrays, T = {}, {}
    for name in _NAMES:
        a = np.ascontiguousarray(inputs[name])
        arrays["in_" + name] = a
        T[name] = nc.dram_tensor("in_" + name, a.shape, mybir.dt.from_np(a.dtype), kind="ExternalInput").ap()[0]
    con, dist, bands = shape_constants()
    for name, a in (("consts", con), ("dist", dist), ("bands", bands)):
        arrays["in_" + name] = a
        T[name] = nc.dram_tensor("in_" + name, a.shape, F32, kind="ExternalInput").ap()
    T["mix_d"] = nc.dram_tensor("mix_d", (1024, 1024), F32, kind="Internal").ap()
    T["vec_d"] = nc.dram_tensor("vec_d", (1, 6144), F32, kind="Internal").ap()
    T["qk_d"] = nc.dram_tensor("qk_d", (24, 128, 1024), F32, kind="Internal").ap()
    T["v_d"] = nc.dram_tensor("v_d", (1024, 768), F32, kind="Internal").ap()
    T["x2_d"] = nc.dram_tensor("x2_d", (1024, 1024), F32, kind="Internal").ap()
    out = nc.dram_tensor("out_0", (1, 1024, 1024), F32, kind="ExternalOutput").ap()
    build(nc, T, out[0])
    r = _run(nc, [arrays], core_ids=[0])
    return r.results[0]["out_0"]
```
